# Optimizing a Trainium2 kernel written in Bass

```python
import math
import jax
import jax.numpy as jnp
from jax import lax
import numpy as np
import jax, jax.numpy as jnp

D_MODEL = 1024
BATCH = 1
SEQ = 1024
DEPTH = 1

A_WIDTH = 256
A_GROUPS = 4
A_GDIM = A_WIDTH // A_GROUPS
CHUNK = 128
B_WIDTH = 256
POOL_WINDOWS = (2, 4, 8, 16)
B_GROUPS = len(POOL_WINDOWS)
B_GDIM = B_WIDTH // B_GROUPS
C_HEADS = 4
C_HEAD_DIM = 64
C_VDIM = 2 * C_HEAD_DIM
C_QK_WIDTH = C_HEADS * 2 * C_HEAD_DIM
C_V_WIDTH = C_HEADS * C_VDIM
Q_BLOCK = 128
N_BUCKETS = 32
MAX_EXACT = 16
MAX_DISTANCE = 128
IN_COLS = 2 * A_WIDTH + B_WIDTH + 2 * C_QK_WIDTH + C_V_WIDTH
N_BRANCH = 3
D_FF = 2816
CONV_WIDTH = 3
EPS = 1e-6


def rmsnorm(x, g, eps=EPS):
    xf = x.astype(jnp.float32)
    y = xf * lax.rsqrt(jnp.mean(xf * xf, axis=-1, keepdims=True) + eps)
    return (y * g.astype(jnp.float32)).astype(x.dtype)

def layernorm(x, g, b, eps=1e-5):
    xf = x.astype(jnp.float32)
    mu = jnp.mean(xf, axis=-1, keepdims=True)
    var = jnp.mean(jnp.square(xf - mu), axis=-1, keepdims=True)
    y = (xf - mu) * lax.rsqrt(var + eps)
    return (y * g.astype(jnp.float32) + b.astype(jnp.float32)).astype(x.dtype)

def gmlp_mixer(zuv, ln_g, ln_b, w_s, b_s):
    B, S, _ = zuv.shape
    z = jax.nn.gelu(zuv, approximate=False)
    u, v = z[..., :A_WIDTH], z[..., A_WIDTH:]
    v = layernorm(v, ln_g, ln_b)
    vc = v.reshape(B, S // CHUNK, CHUNK, A_GROUPS, A_GDIM)
    mask = jnp.tril(jnp.ones((CHUNK, CHUNK), dtype=bool))
    ws = jnp.where(mask[None], w_s, jnp.zeros_like(w_s))
    mixed = jnp.einsum('gts,bcsgd->bctgd', ws, vc) + b_s.T[None, None, :, :, None]
    return u * mixed.reshape(B, S, A_WIDTH)

def pool_mixer(xb, pool_w, pool_scale):
    B, S, _ = xb.shape
    xf = xb.astype(jnp.float32)
    cs = jnp.cumsum(xf, axis=1)
    t = jnp.arange(S)
    outs = []
    for gi, w in enumerate(POOL_WINDOWS):
        sl = slice(gi * B_GDIM, (gi + 1) * B_GDIM)
        c = cs[..., sl]
        lag = jnp.pad(c, ((0, 0), (w, 0), (0, 0)))[:, :S]
        cnt = jnp.minimum(t + 1, w).astype(jnp.float32)[None, :, None]
        outs.append((c - lag) / cnt - xf[..., sl])
    p = jnp.stack(outs, axis=2).astype(xb.dtype)
    y = jnp.einsum('bsgc,gcd->bsgd', p, pool_w).reshape(B, S, B_WIDTH)
    return y * pool_scale

def t5_causal_bucket(rel):
    n = jnp.maximum(rel, 0)
    nf = jnp.maximum(n, 1).astype(jnp.float32)
    large = MAX_EXACT + (jnp.log(nf / MAX_EXACT) / math.log(MAX_DISTANCE / MAX_EXACT)
                         * (N_BUCKETS - MAX_EXACT)).astype(jnp.int32)
    large = jnp.minimum(large, N_BUCKETS - 1)
    return jnp.where(n < MAX_EXACT, n, large)

def diff_attention(q, k, v, lam, rel_bias):
    B, S, H, _, dh = q.shape
    nb = S // Q_BLOCK
    scale = dh ** -0.5
    qb = q.reshape(B, nb, Q_BLOCK, H, 2, dh).transpose(1, 0, 2, 3, 4, 5)
    kpos = jnp.arange(S)

    def block(args):
        qi, i = args
        qpos = i * Q_BLOCK + jnp.arange(Q_BLOCK)
        rel = qpos[:, None] - kpos[None, :]
        bias = rel_bias[t5_causal_bucket(rel)].astype(jnp.float32)
        s = jnp.einsum('bqhcd,bkhcd->bhcqk', qi, k).astype(jnp.float32) * scale
        s = s + bias.transpose(2, 0, 1)[None, :, None]
        s = jnp.where((rel >= 0)[None, None, None], s, -1e30)
        p = jax.nn.softmax(s, axis=-1)
        a = p[:, :, 0] - lam * p[:, :, 1]
        return jnp.einsum('bhqk,bkhd->bqhd', a.astype(v.dtype), v)

    out = lax.map(block, (qb, jnp.arange(nb)))
    return out.transpose(1, 0, 2, 3, 4).reshape(B, S, H, v.shape[-1])

def diff_attn_mixer(zq, zk, zv, lam_vecs, subln_g, rel_bias, layer_idx):
    B, S, _ = zq.shape
    q = zq.reshape(B, S, C_HEADS, 2, C_HEAD_DIM)
    k = zk.reshape(B, S, C_HEADS, 2, C_HEAD_DIM)
    v = zv.reshape(B, S, C_HEADS, C_VDIM)
    lam_init = 0.8 - 0.6 * math.exp(-0.3 * layer_idx)
    lv = lam_vecs.astype(jnp.float32)
    lam = jnp.exp(jnp.sum(lv[0] * lv[1])) - jnp.exp(jnp.sum(lv[2] * lv[3])) + lam_init
    o = diff_attention(q, k, v, lam, rel_bias)
    o = rmsnorm(o, subln_g, eps=1e-5) * (1.0 - lam_init)
    return o.reshape(B, S, C_V_WIDTH)

def conv_ffn(h, w_up, conv_w, conv_b, w_down):
    gu = h @ w_up
    gate, up = gu[..., :D_FF], gu[..., D_FF:]
    gate = lax.conv_general_dilated(
        gate, conv_w[:, None, :], window_strides=(1,), padding=[(CONV_WIDTH - 1, 0)],
        dimension_numbers=('NWC', 'WIO', 'NWC'), feature_group_count=D_FF) + conv_b
    return (jax.nn.gelu(gate, approximate=False) * up) @ w_down

def first_inputs(seed: int = 0) -> dict:
    key = jax.random.key(seed)
    ks = jax.random.split(key, 24)
    L, D = DEPTH, D_MODEL

    def nrm(k, shape, scale):
        return jax.random.normal(k, shape, jnp.float32) * scale

    def gain(k, shape):
        return 1.0 + nrm(k, shape, 0.05)

    return {
        'x': nrm(ks[0], (BATCH, SEQ, D), 1.0),
        'attn_norm_g': gain(ks[1], (L, D)),
        'w_in': nrm(ks[2], (L, D, IN_COLS), D ** -0.5),
        'w_gate': nrm(ks[3], (L, D, N_BRANCH * D), D ** -0.5),
        'b_gate': nrm(ks[4], (L, N_BRANCH * D), 0.01),
        'sgu_ln_g': gain(ks[5], (L, A_WIDTH)),
        'sgu_ln_b': nrm(ks[6], (L, A_WIDTH), 0.01),
        'sgu_w': nrm(ks[7], (L, A_GROUPS, CHUNK, CHUNK), CHUNK ** -0.5),
        'sgu_b': gain(ks[8], (L, A_GROUPS, CHUNK)),
        'proj_a': nrm(ks[9], (L, A_WIDTH, D), A_WIDTH ** -0.5),
        'pool_w': nrm(ks[10], (L, B_GROUPS, B_GDIM, B_GDIM), B_GDIM ** -0.5),
        'pool_scale': gain(ks[11], (L, B_WIDTH)),
        'proj_b': nrm(ks[12], (L, B_WIDTH, D), B_WIDTH ** -0.5),
        'diff_lam': nrm(ks[13], (L, 4, C_HEAD_DIM), 0.1),
        'diff_subln_g': gain(ks[14], (L, C_VDIM)),
        'proj_c': nrm(ks[15], (L, C_V_WIDTH, D), C_V_WIDTH ** -0.5),
        'w_out': nrm(ks[16], (L, D, D), D ** -0.5),
        'ffn_norm_g': gain(ks[17], (L, D)),
        'w_up': nrm(ks[18], (L, D, 2 * D_FF), D ** -0.5),
        'conv_w': nrm(ks[19], (L, CONV_WIDTH, D_FF), CONV_WIDTH ** -0.5),
        'conv_b': nrm(ks[20], (L, D_FF), 0.01),
        'w_down': nrm(ks[21], (L, D_FF, D), D_FF ** -0.5),
        'rel_bias': nrm(ks[22], (N_BUCKETS, C_HEADS), 0.5),
        'final_norm_g': gain(ks[23], (D,)),
    }

def first_block(x, attn_norm_g, w_in, w_gate, b_gate, sgu_ln_g, sgu_ln_b, sgu_w, sgu_b,
              proj_a, pool_w, pool_scale, proj_b, diff_lam, diff_subln_g, proj_c, w_out,
              ffn_norm_g, w_up, conv_w, conv_b, w_down, rel_bias, final_norm_g):
    o_a = 2 * A_WIDTH
    o_b = o_a + B_WIDTH
    o_q = o_b + C_QK_WIDTH
    o_k = o_q + C_QK_WIDTH
    for l in range(DEPTH):
        h = rmsnorm(x, attn_norm_g[l])
        z = h @ w_in[l]
        gates = jax.nn.sigmoid(h @ w_gate[l] + b_gate[l])
        y_a = gmlp_mixer(z[..., :o_a], sgu_ln_g[l], sgu_ln_b[l], sgu_w[l], sgu_b[l])
        y_b = pool_mixer(z[..., o_a:o_b], pool_w[l], pool_scale[l])
        y_c = diff_attn_mixer(z[..., o_b:o_q], z[..., o_q:o_k], z[..., o_k:],
                              diff_lam[l], diff_subln_g[l], rel_bias, l)
        g_a = gates[..., :D_MODEL]
        g_b = gates[..., D_MODEL:2 * D_MODEL]
        g_c = gates[..., 2 * D_MODEL:]
        merged = g_a * (y_a @ proj_a[l]) + g_b * (y_b @ proj_b[l]) + g_c * (y_c @ proj_c[l])
        x = x + merged @ w_out[l]
        x = x + conv_ffn(rmsnorm(x, ffn_norm_g[l]), w_up[l], conv_w[l], conv_b[l], w_down[l])
    return rmsnorm(x, final_norm_g)


DEPTH_2 = 2

GRID_W = 64
CTX_LEN = 256
N_MIXERS = 2
NORM_EPS = 1e-6

MLA_HEADS = 8
QK_NOPE = 128
QK_ROPE = 64
V_DIM = 128
Q_LORA = 256
KV_LORA = 128
MLA_WIDTH = MLA_HEADS * V_DIM
MLA_IN_WIDTH = Q_LORA + KV_LORA + QK_ROPE + MLA_WIDTH
ROPE_AXIS_DIM = QK_ROPE // 2
ROPE_THETA = 10000.0

FOURIER_WIDTH = D_MODEL
FOURIER_GROUPS = 8
FOURIER_GROUP_DIM = FOURIER_WIDTH // FOURIER_GROUPS

N_MLA_LAYERS = (DEPTH_2 + 1) // 2
N_FOURIER_LAYERS = DEPTH_2 // 2
ADA_STD = 0.5 * D_MODEL ** -0.5


def rms_norm(x, g):
    xf = x.astype(jnp.float32)
    y = xf * lax.rsqrt(jnp.mean(xf * xf, axis=-1, keepdims=True) + NORM_EPS)
    return (y * g.astype(jnp.float32)).astype(x.dtype)

def axial_rope_tables(row, col):
    inv_freq = 1.0 / (ROPE_THETA ** (jnp.arange(0, ROPE_AXIS_DIM, 2, dtype=jnp.float32) / ROPE_AXIS_DIM))
    ang_r = row.astype(jnp.float32)[:, None] * inv_freq[None, :]
    ang_c = col.astype(jnp.float32)[:, None] * inv_freq[None, :]
    return jnp.cos(ang_r), jnp.sin(ang_r), jnp.cos(ang_c), jnp.sin(ang_c)

def _rotate(t, cos, sin):
    t1, t2 = jnp.split(t, 2, axis=-1)
    return jnp.concatenate([t1 * cos - t2 * sin, t2 * cos + t1 * sin], axis=-1)

def apply_axial_rope(t, tables):
    cos_r, sin_r, cos_c, sin_c = [a.astype(t.dtype)[None, :, None, :] for a in tables]
    t_r, t_c = jnp.split(t, 2, axis=-1)
    return jnp.concatenate([_rotate(t_r, cos_r, sin_r), _rotate(t_c, cos_c, sin_c)], axis=-1)

def mla_query(c_q, g_qa, w_qup):
    b, t, _ = c_q.shape
    q = (rms_norm(c_q, g_qa) @ w_qup).reshape(b, t, MLA_HEADS, QK_NOPE + QK_ROPE)
    return q[..., :QK_NOPE], q[..., QK_NOPE:]

def mla_keyvalue(c_kv, g_kva, w_kvup):
    b, t, _ = c_kv.shape
    kv = (rms_norm(c_kv, g_kva) @ w_kvup).reshape(b, t, MLA_HEADS, QK_NOPE + V_DIM)
    return kv[..., :QK_NOPE], kv[..., QK_NOPE:]

def assemble_keys(k_nope, k_pe):
    return jnp.concatenate([k_nope, jnp.broadcast_to(k_pe, k_nope.shape[:-1] + (QK_ROPE,))], axis=-1)

def dense_attention(q, k, v):
    scale = 1.0 / math.sqrt(QK_NOPE + QK_ROPE)
    s = jnp.einsum('bqhd,bkhd->bhqk', q, k).astype(jnp.float32) * scale
    p = jax.nn.softmax(s, axis=-1).astype(v.dtype)
    return jnp.einsum('bhqk,bkhd->bqhd', p, v)

def latent_attention(q, k_lat, v_lat, k_ctx, v_ctx):
    b, t, h, dk = q.shape
    k_all = jnp.concatenate([k_ctx, k_lat], axis=1)
    v_all = jnp.concatenate([v_ctx, v_lat], axis=1)
    nb = t // Q_BLOCK
    qb = q.reshape(b, nb, Q_BLOCK, h, dk).transpose(1, 0, 2, 3, 4)
    o = lax.map(lambda qblk: dense_attention(qblk, k_all, v_all), qb)
    return o.transpose(1, 0, 2, 3, 4).reshape(b, t, h * V_DIM)

def fourier_mix(u, w_in, w_out):
    proj = u @ w_in
    z, gate = proj[..., :FOURIER_WIDTH], proj[..., FOURIER_WIDTH:]
    b, t, _ = z.shape
    zg = z.reshape(b, t, FOURIER_GROUPS, FOURIER_GROUP_DIM).astype(jnp.float32)
    y = jnp.fft.fftn(zg, axes=(1, 3), norm="ortho").real.astype(u.dtype).reshape(b, t, FOURIER_WIDTH)
    return (y * jax.nn.silu(gate)) @ w_out

def ada_params(cond_act, w, b):
    mod = cond_act @ w + b
    return jnp.split(mod, 3, axis=-1)

def second_inputs(seed: int = 0) -> dict:
    key = jax.random.key(seed)
    ks = jax.random.split(key, 16)
    n = jax.random.normal
    f32 = jnp.float32
    return {
        "x": n(ks[0], (BATCH, SEQ, D_MODEL), f32),
        "c": n(ks[1], (BATCH, D_MODEL), f32),
        "ctx": n(ks[2], (BATCH, CTX_LEN, D_MODEL), f32),
        "c_ctx": n(ks[3], (D_MODEL,), f32),
        "norm_g": 1.0 + 0.02 * n(ks[4], (DEPTH_2, D_MODEL), f32),
        "w_ada": ADA_STD * n(ks[5], (DEPTH_2, D_MODEL, 3 * D_MODEL), f32),
        "b_ada": 0.02 * n(ks[6], (DEPTH_2, 3 * D_MODEL), f32),
        "mla_w_in": D_MODEL ** -0.5 * n(ks[7], (N_MLA_LAYERS, D_MODEL, MLA_IN_WIDTH), f32),
        "mla_g_qa": 1.0 + 0.02 * n(ks[8], (N_MLA_LAYERS, Q_LORA), f32),
        "mla_w_qup": Q_LORA ** -0.5 * n(ks[9], (N_MLA_LAYERS, Q_LORA, MLA_HEADS * (QK_NOPE + QK_ROPE)), f32),
        "mla_g_kva": 1.0 + 0.02 * n(ks[10], (N_MLA_LAYERS, KV_LORA), f32),
        "mla_w_kvup": KV_LORA ** -0.5 * n(ks[11], (N_MLA_LAYERS, KV_LORA, MLA_HEADS * (QK_NOPE + V_DIM)), f32),
        "mla_w_out": MLA_WIDTH ** -0.5 * n(ks[12], (N_MLA_LAYERS, MLA_WIDTH, D_MODEL), f32),
        "fno_w_in": D_MODEL ** -0.5 * n(ks[13], (N_FOURIER_LAYERS, D_MODEL, 2 * FOURIER_WIDTH), f32),
        "fno_w_out": FOURIER_WIDTH ** -0.5 * n(ks[14], (N_FOURIER_LAYERS, FOURIER_WIDTH, D_MODEL), f32),
        "final_g": 1.0 + 0.02 * n(ks[15], (D_MODEL,), f32),
    }

def second_block(x, c, ctx, c_ctx, norm_g, w_ada, b_ada, mla_w_in, mla_g_qa, mla_w_qup, mla_g_kva,
              mla_w_kvup, mla_w_out, fno_w_in, fno_w_out, final_g):
    n_tok = x.shape[1]
    rows = n_tok // GRID_W
    row = jnp.repeat(jnp.arange(rows, dtype=jnp.int32), GRID_W)
    col = jnp.tile(jnp.arange(GRID_W, dtype=jnp.int32), rows)
    rope = axial_rope_tables(row, col)

    act_lat = jax.nn.silu(c)
    act_ctx = jax.nn.silu(c_ctx)
    h_lat, h_ctx = x, ctx
    kv_lo, kv_hi = Q_LORA, Q_LORA + KV_LORA
    pe_hi = kv_hi + QK_ROPE

    for i in range(DEPTH_2):
        mixer = i % N_MIXERS
        idx = i // N_MIXERS
        ctx_later = any(j % N_MIXERS == 0 for j in range(i + 1, DEPTH_2))

        sh_l, sc_l, gt_l = ada_params(act_lat, w_ada[i], b_ada[i])
        u_lat = rms_norm(h_lat, norm_g[i]) * (1.0 + sc_l[:, None, :]) + sh_l[:, None, :]
        sh_c, sc_c, gt_c = ada_params(act_ctx, w_ada[i], b_ada[i])

        if mixer == 0:
            w_in = mla_w_in[idx]
            u_ctx = rms_norm(h_ctx, norm_g[i]) * (1.0 + sc_c) + sh_c
            p_lat = u_lat @ w_in
            qn_l, qp_l = mla_query(p_lat[..., :kv_lo], mla_g_qa[idx], mla_w_qup[idx])
            kn_l, v_l = mla_keyvalue(p_lat[..., kv_lo:kv_hi], mla_g_kva[idx], mla_w_kvup[idx])
            kp_l = apply_axial_rope(p_lat[..., None, kv_hi:pe_hi], rope)
            q_l = jnp.concatenate([qn_l, apply_axial_rope(qp_l, rope)], axis=-1)
            k_l = assemble_keys(kn_l, kp_l)
            if ctx_later:
                p_ctx = u_ctx @ w_in
            else:
                p_ctx = u_ctx @ w_in[:, kv_lo:pe_hi]
                p_ctx = jnp.concatenate([jnp.zeros(p_ctx.shape[:-1] + (kv_lo,), p_ctx.dtype), p_ctx], axis=-1) if False else p_ctx
            off = 0 if not ctx_later else kv_lo
            kn_c, v_c = mla_keyvalue(p_ctx[..., off:off + KV_LORA], mla_g_kva[idx], mla_w_kvup[idx])
            k_c = assemble_keys(kn_c, p_ctx[..., None, off + KV_LORA:off + KV_LORA + QK_ROPE])

            o_lat = latent_attention(q_l, k_l, v_l, k_c, v_c)
            y_lat = (o_lat * jax.nn.silu(p_lat[..., pe_hi:])) @ mla_w_out[idx]
            if ctx_later:
                qn_c, qp_c = mla_query(p_ctx[..., :kv_lo], mla_g_qa[idx], mla_w_qup[idx])
                q_c = jnp.concatenate([qn_c, qp_c], axis=-1)
                b_, t_c = h_ctx.shape[0], h_ctx.shape[1]
                o_ctx = dense_attention(q_c, k_c, v_c).reshape(b_, t_c, MLA_WIDTH)
                y_ctx = (o_ctx * jax.nn.silu(p_ctx[..., pe_hi:])) @ mla_w_out[idx]
                h_ctx = h_ctx + gt_c * y_ctx
            h_lat = h_lat + gt_l[:, None, :] * y_lat
        else:
            y_lat = fourier_mix(u_lat, fno_w_in[idx], fno_w_out[idx])
            if ctx_later:
                u_ctx = rms_norm(h_ctx, norm_g[i]) * (1.0 + sc_c) + sh_c
                h_ctx = h_ctx + gt_c * fourier_mix(u_ctx, fno_w_in[idx], fno_w_out[idx])
            h_lat = h_lat + gt_l[:, None, :] * y_lat

    return rms_norm(h_lat, final_g)


def setup_inputs(seed=0):
    out = dict(first_inputs(seed))
    for name, value in second_inputs(seed + 1).items():
        if name != "x":
            out[name + "_2"] = value
    return out


def reference(
    x, attn_norm_g, w_in, w_gate, b_gate, sgu_ln_g, sgu_ln_b, sgu_w, sgu_b, proj_a, pool_w,
    pool_scale, proj_b, diff_lam, diff_subln_g, proj_c, w_out, ffn_norm_g, w_up, conv_w, conv_b,
    w_down, rel_bias, final_norm_g, c_2, ctx_2, c_ctx_2, norm_g_2, w_ada_2, b_ada_2, mla_w_in_2,
    mla_g_qa_2, mla_w_qup_2, mla_g_kva_2, mla_w_kvup_2, mla_w_out_2, fno_w_in_2, fno_w_out_2,
    final_g_2,
):
    x = first_block(
        x, attn_norm_g, w_in, w_gate, b_gate, sgu_ln_g, sgu_ln_b, sgu_w, sgu_b, proj_a, pool_w,
        pool_scale, proj_b, diff_lam, diff_subln_g, proj_c, w_out, ffn_norm_g, w_up, conv_w,
        conv_b, w_down, rel_bias, final_norm_g,
    )
    return second_block(
        x, c_2, ctx_2, c_ctx_2, norm_g_2, w_ada_2, b_ada_2, mla_w_in_2, mla_g_qa_2, mla_w_qup_2,
        mla_g_kva_2, mla_w_kvup_2, mla_w_out_2, fno_w_in_2, fno_w_out_2, final_g_2,
    )


_drawn_inputs = setup_inputs


def setup_inputs(seed=0):
    import zlib

    import numpy as np

    out = dict(_drawn_inputs(seed))
    spreads = {}
    factors = {'b_gate': 8.0,
     'sgu_ln_g': 4.937,
     'sgu_ln_b': 8.0,
     'sgu_b': 3.85,
     'pool_scale': 2.749,
     'diff_lam': 8.0,
     'diff_subln_g': 2.936,
     'conv_b': 8.0,
     'ctx_2': 8.0,
     'c_ctx_2': 4.671,
     'norm_g_2': 8.0,
     'b_ada_2': 4.631,
     'mla_g_qa_2': 8.0,
     'mla_w_qup_2': 3.158,
     'mla_g_kva_2': 8.0,
     'final_g_2': 2.861}
    for name, (base, spread) in spreads.items():
        noise = np.random.default_rng([zlib.crc32(name.encode()), seed]).standard_normal(out[name].shape)
        drawn = base * np.exp(spread * noise) if base else spread * noise
        out[name] = jnp.asarray(drawn.astype(out[name].dtype))
    for name, factor in factors.items():
        out[name] = (out[name] * factor).astype(out[name].dtype)
    return out
```

```python
import math

import numpy as np

import concourse.bass as bass
from concourse import mybir

F32 = mybir.dt.float32
F32R = mybir.dt.float32r
ALU = mybir.AluOpType
ACT = mybir.ActivationFunctionType
AX = mybir.AxisListType.X

P = 128
T = 1024
D = 1024
KC = D // P
UW = KC * P
CTX = 256
TK = CTX + T
HEADS_C = 4
HEADS = 8
QT_N = T // P
FFC = 22
FF_PASSES = [8, 8, 6]
FG = 8
HALF = T // 2
GROW = T + P
LAM_INIT = 0.8 - 0.6 * math.exp(0.0)
MLA_SCALE = 1.0 / math.sqrt(192.0)

VEC_PARTS = [("attn_g", 8), ("b_gate", 24), ("pool_scale", 2), ("subln", 1), ("ffn_g", 8), ("conv0", 22),
             ("conv1", 22), ("conv2", 22), ("conv_b", 22), ("final_g", 8), ("norm_g0", 8), ("norm_g1", 8),
             ("b_both", 16), ("b_lat", 32), ("g_qa", 2), ("g_kva", 1), ("final_g2", 8), ("alt", 1),
             ("pool_inv", 2)]
VEC = {}
_at = 0
for _name, _n in VEC_PARTS:
    VEC[_name] = _at
    _at += _n
NVEC = _at

NORM = {2: 1, 3: 1, "norm": 1}
PHASES = [
    ("bias", {0: 4, 1: 4}),
    ("norm1", {**NORM, "split": 8, "square": 8}),
    ("ux", {0: 2, 1: 2, "unit": 4}),
    ("va", {2: 1, 3: 1, "unit": 2}),
    ("gmlp", {2: 1, 3: 1, "split": 2}),
    ("pool", {2: 1, 3: 1, "split": 2}),
    ("diff", {0: 10 * 4, 1: 9 * 4, 2: 9 * 4, 3: 9 * 4, "unit": 12, "split": 4, "norm": 4}),
    ("merge", {0: 16, 1: 16, 2: 8, 3: 8, "unit": 32}),
    ("msplit", {"split": 8}),
    ("out1", {0: 4, 1: 4, "unit": 8, "xnew": 8, "square": 8}),
    ("norm2", {**NORM, "split": 8}),
    ("up0", {0: 8, 1: 8, "unit": 16, "split": 8}),
    ("down0", {2: 4, 3: 4, "unit": 8, "xnew": 8}),
    ("up1", {0: 8, 1: 8, "unit": 16, "split": 8}),
    ("down1", {2: 4, 3: 4, "unit": 8, "xnew": 8}),
    ("up2", {0: 6, 1: 6, "unit": 12, "split": 6}),
    ("down2", {2: 4, 3: 4, "unit": 8, "xnew": 8, "square": 8}),
    ("fnorm", {**NORM, "xnew": 8}),
    ("norm3", {**NORM, "split": 8, "square": 8}),
    ("normc", {**NORM, "split": 8, "square": 8}),
    ("kvpe", {0: 2, 1: 2, 2: 1, 3: 1, "unit": 2}),
    ("cq", {0: 1, 1: 1, "unit": 2}),
    ("cqnorm", {**NORM, "split": 2, "square": 2}),
    ("ckvnorm", {**NORM, "split": 1}),
    ("ckvcnorm", {**NORM, "split": 1}),
    ("mgate", {0: 4, 1: 4, "unit": 8}),
    ("heads", {0: 16, 1: 16, 2: 8, 3: 8, "unit": 8}),
    ("osplit", {"split": 8}),
    ("out2", {0: 4, 1: 4, "unit": 8, "xnew": 8, "square": 8}),
    ("norm4", {**NORM, "split": 8}),
    ("four", {0: 8, 1: 8, 2: 16, 3: 16, "unit": 16}),
    ("ysplit", {"split": 8}),
    ("out3", {0: 4, 1: 4, "unit": 8, "xnew": 8, "square": 8}),
    ("final", {**NORM}),
]


def before(phase, what):
    total = 0
    for name, adds in PHASES:
        if name == phase:
            return total
        total += adds.get(what, 0)
    raise KeyError(phase)


NUNITS = sum(adds.get("unit", 0) for _, adds in PHASES)


class Chain:

    def __init__(self, eng, sem):
        self.eng, self.sem, self.n, self.off = eng, sem, 0, None

    def __call__(self, ins):
        ins.then_inc(self.sem, 1)
        self.n += 1
        self.eng.wait_ge(self.sem, self.n if self.off is None else self.off + self.n)

    def enter(self, i, per):
        self.off, self.per, self.start = i * per, per, self.n

    def leave(self, count):
        assert self.n - self.start == self.per, (self.n - self.start, self.per)
        self.n = self.start + self.per * count
        self.off = None


def build(nc, t_in, out):
    H_AT = 16512
    F_AT = H_AT + 65536
    X_AT = F_AT + 65536
    W_AT = X_AT + 32768
    T_AT = W_AT + 8192 + 16384
    TS = 1040
    C_AT = T_AT + 4 * TS * 4

    def at(name, cols, where, dt=F32, parts=P):
        return nc.alloc_sbuf_tensor_at(name, [parts, cols], dt, offset=where)

    H = at("H", 2 * KC * T, H_AT, F32R)
    w_raw = at("w_raw", 2 * UW, W_AT)
    w_hl = at("w_hl", 2 * 2 * UW, W_AT + 8192, F32R)
    SC = at("SC", 4 * TS, T_AT)
    ACC, SQ, TMP0, TMP1 = (SC[:, s * TS:s * TS + T] for s in range(4))
    TMP = [TMP0, TMP1]
    DIAG = SQ
    X = at("X", KC * T, X_AT)

    place = [C_AT]

    def small(name, cols, dt=F32):
        t = at(name, cols, place[0], dt)
        place[0] += (cols * 4 + 31) // 32 * 32
        return t

    ident = small("ident", P)
    ones = small("ones", P)
    dup = small("dup", P)
    vec = small("vec", NVEC)
    lngb = small("lngb", 512)
    cols = small("cols", 64)
    modb = small("modb", 32)
    modl = small("modl", 32)
    fac0 = small("fac0", 8)
    facc = small("facc", 8)
    fac1 = small("fac1", 8)
    adac = small("adac", 16)
    bn = small("bn", 6)
    lv = small("lv", 256)
    lvp = small("lvp", 64)
    stat = small("stat", 8)
    assert place[0] <= nc.sbuf_usable_end, place[0]

    def v1(name, j=0):
        return vec[:, VEC[name] + j:VEC[name] + j + 1]

    YA = at("YA", 2 * 2 * T, F_AT, F32R)
    YB = at("YB", 2 * 2 * T, F_AT + 16384, F32R)
    OCS = at("OCS", 2 * 4 * T, F_AT + 32768, F32R)
    onehot = at("onehot", GROW, F_AT)
    rb = at("rb", HEADS_C, F_AT + 4608)
    rbx = at("rbx", HEADS_C * P, F_AT + 4640)
    grow = at("grow", GROW, F_AT + 8192)
    U = at("U", 2 * T, F_AT + 32768)
    VA = at("VA", QT_N * 256, F_AT + 40960)
    PADX = T + 16
    XB = at("XB", 2 * PADX, F_AT + 49152)
    WST = at("WST", 4 * P, F_AT + 57472)
    SGB = at("SGB", 2 * P, F_AT + 59520)
    BD = at("BD", 2 * P, F_AT + 60544)
    EDGE = at("EDGE", 32, F_AT + 61568)
    TRI = at("TRI", P, F_AT + 61728)
    PA = SC[:, 0:2 * PADX]
    PB = at("PB", 2 * PADX, X_AT)
    S0 = at("S0", T, X_AT)
    S1 = at("S1", T, X_AT + 4096)
    AA = at("AA", T, X_AT + 8192)
    AT = at("AT", T, X_AT + 12288)
    QT = at("QT", T, X_AT + 16384)
    KT = at("KT", T, X_AT + 20480)
    VC = at("VC", T, X_AT + 24576)
    BR = at("BR", T, X_AT + 28672)
    OC = TMP1
    M = at("M", KC * T, X_AT)
    XIN = at("XIN", KC * T, F_AT)
    FF = at("FF", 2 * KC * T, F_AT, F32R)
    CL = at("CL", D, H_AT)
    CC = at("CC", D, H_AT + 4096)
    AJ = at("AJ", D, H_AT + 8192)
    AW = at("AW", 12 * D, H_AT + 12288)
    UC = at("UC", 2 * KC * CTX, F_AT, F32R)
    CST = at("CST", TK, F_AT + 16384)
    CKR = at("CKR", TK, F_AT + 21504)
    TPE = at("TPE", TK, F_AT + 26624)
    CXR = at("CXR", KC * CTX, F_AT + 32768)
    CQR = at("CQR", 2 * T, F_AT + 49152)
    G = at("G", KC * T, F_AT)
    CQ = at("CQ", 2 * 2 * T, F_AT + 32768, F32R)
    CKV = at("CKV", 2 * TK, F_AT + 49152, F32R)
    KPE = at("KPE", TK, F_AT + 59392)
    QN = at("QN", T, H_AT)
    QP = at("QP", T, H_AT + 4096)
    KN = at("KN", TK, H_AT + 8192)
    VN = at("VN", TK, H_AT + 13312)
    E = at("E", 2 * TK, H_AT + 18432)
    PT = at("PT", TK, H_AT + 28672)
    CSQ = at("CSQ", T, H_AT + 33792)
    Y = at("Y", KC * T, F_AT)
    CTAB = at("CTAB", 4 * HALF, F_AT + 32768)
    STAB = at("STAB", 4 * HALF, F_AT + 40960)
    CSD = at("CSD", 2 * P, F_AT + 49152)
    M12 = at("M12", 2 * HALF, F_AT + 50176)
    ZEO = at("ZEO", 2 * HALF, F_AT + 54272)
    ZR = at("ZR", T, F_AT + 58368)
    MR = at("MR", P, F_AT + 62464)
    ALT = at("ALT", HALF, F_AT + 62976)

    PS = nc.alloc_psum_tensor("PS", [P, 4096], F32)
    scratch = nc.dram_tensor("bias_scratch", (HEADS_C, P * GROW), F32).ap()
    shifted = bass.AP(scratch.tensor, P - 1, [[P * GROW, HEADS_C], [GROW - 1, P], [1, T]])

    def pair(p, n=T, start=0):
        return PS[:, p * 1024 + start:p * 1024 + start + n]

    sem = nc.alloc_semaphore
    w_in = [sem("w_in0"), sem("w_in1")]
    w_hi = sem("w_hi")
    w_split = sem("w_split")
    w_seen, sc_seen = sem("w_seen"), sem("sc_seen")
    w_used = sem("w_used")
    done = [sem(f"done{p}") for p in range(4)]
    free = [sem(f"free{p}") for p in range(4)]
    hi = sem("hi")
    lo = sem("lo")
    xt = sem("xt")
    sq_added = sem("sq_added")
    acc_ready = sem("acc_ready")
    ms_ready = sem("ms_ready")
    sd_ready = sem("sd_ready")
    diag_ready = sem("diag_ready")
    x_new = sem("x_new")
    sq_ready = sem("sq_ready")
    s_dve, s_act, s_pe = sem("s_dve"), sem("s_act"), sem("s_pe")
    c_early, c_gm, c_x = sem("c_early"), sem("c_gm"), sem("c_x")
    x_in = [sem(f"x_in{c}") for c in range(KC)]
    memset_done = sem("memset_done")
    g_row = sem("g_row")
    g_out = sem("g_out")
    br_in = sem("br_in")
    rbx_ready = sem("rbx_ready")
    u_ready, xb_ready, va_ready = sem("u_ready"), sem("xb_ready"), sem("va_ready")
    va_ms, va_sd = sem("va_ms"), sem("va_sd")
    va_norm, wst_ready, p_ready = sem("va_norm"), sem("wst_ready"), sem("p_ready")
    qkv_ready = sem("qkv_ready")
    neg_ready, exp_ready, aa_ready, at_ready, oc_ready = (
        sem(n) for n in ("neg_ready", "exp_ready", "aa_ready", "at_ready", "oc_ready"))
    lam_sum, lam_exp = sem("lam_sum"), sem("lam_exp")
    sg_ready, m_ready = sem("sg_ready"), sem("m_ready")
    gp_ready, cv_ready, gl_ready = sem("gp_ready"), sem("cv_ready"), sem("gl_ready")
    ada_in = [sem("ada_in0"), sem("ada_in1")]
    ada_used = sem("ada_used")
    c_rows, c_silu = sem("c_rows"), sem("c_silu")
    ctx_in, cs_in, csq_in, ft_in = sem("ctx_in"), sem("cs_in"), sem("csq_in"), sem("ft_in")
    csq_free = sem("csq_free")
    ckr_ready, tpe_ready, kpe_ready, cqr_ready = (
        sem(n) for n in ("ckr_ready", "tpe_ready", "kpe_ready", "cqr_ready"))
    hd_act, hd_dve = sem("hd_act"), sem("hd_dve")
    sc_done, sc_free, mx_ready, ex_ready, e_ready = (
        sem(n) for n in ("sc_done", "sc_free", "mx_ready", "ex_ready", "e_ready"))
    tpa_done, tpb_done, pta, ptb = (sem(n) for n in ("tpa_done", "tpb_done", "pta", "ptb"))
    pv_done, pv_free = sem("pv_done"), sem("pv_free")
    zr_ready, ze_ready, m_evac, mr_ready, qs_ready, sgf_ready, y_ready = (
        sem(n) for n in ("zr_ready", "ze_ready", "m_evac", "mr_ready", "qs_ready", "sgf_ready", "y_ready"))
    gate_ready = sem("gate_ready")
    o_ready, o_out = sem("o_ready"), sem("o_out")

    block_cm = nc.Block()
    block = block_cm.__enter__()

    @block.sync
    def _(sp):
        sp.dma_start(onehot[0:33, :], t_in["onehot"]).then_inc(c_early, 16)
        sp.dma_start(rb[0:32, :], t_in["rel_bias"]).then_inc(c_early, 16)
        sp.dma_start(ident[:, :], t_in["ident"]).then_inc(c_early, 16)
        sp.dma_start(vec[:, :], t_in["vec"]).then_inc(c_early, 16)
        for c in range(KC):
            sp.dma_start(X[:, c * T:(c + 1) * T], t_in["x"][c]).then_inc(x_in[c], 16)
        sp.dma_start(lngb[:, 0:256], t_in["ln_g"].partition_broadcast(P)).then_inc(c_gm, 16)
        sp.dma_start(lngb[:, 256:512], t_in["ln_b"].partition_broadcast(P)).then_inc(c_gm, 16)
        sp.dma_start(WST[:, :], t_in["wst"]).then_inc(c_gm, 16)
        sp.dma_start(TRI[:, :], t_in["tri"]).then_inc(c_gm, 16)
        for g in range(4):
            half = slice(64 * (g % 2), 64 * (g % 2) + 64)
            sp.dma_start(SGB[half, (g // 2) * P:(g // 2 + 1) * P],
                         t_in["sgu_b"][g].partition_broadcast(64)).then_inc(c_gm, 16)
        sp.wait_ge(memset_done, 1)
        for g in range(4):
            half = slice(64 * (g % 2), 64 * (g % 2) + 64)
            sp.dma_start(BD[half, (g // 2) * P + 64 * (g % 2):(g // 2) * P + 64 * (g % 2) + 64],
                         t_in["pool_w"][g]).then_inc(c_gm, 16)
        sp.dma_start(EDGE[:, :], t_in["edge"]).then_inc(c_gm, 16)
        sp.dma_start(lv[:, :], t_in["lam"].partition_broadcast(P)).then_inc(c_gm, 16)
        sp.dma_start(dup[:, :], t_in["dup"]).then_inc(c_gm, 16)
        for u in range(2):
            sp.dma_start(w_raw[:, u * UW:(u + 1) * UW], t_in["units"][u]).then_inc(w_in[u], 16)
        with sp.Fori(1, NUNITS // 2) as i:
            for s in range(2):
                sp.wait_ge(w_split, 2 * i + (s - 1))
                sp.dma_start(w_raw[:, s * UW:(s + 1) * UW],
                             t_in["units"][bass.ds(2 * i + s, 1)].rearrange("o p n -> p (o n)")
                             ).then_inc(w_in[s], 16)

    @block.gpsimd
    def _(pool):
        def split_unit(s, number):
            pool.wait_ge(w_in[s], 16 * (number // 2 + 1) if isinstance(number, int) else number)
            hi_part = w_hl[:, s * 2 * UW:s * 2 * UW + UW]
            raw = w_raw[:, s * UW:(s + 1) * UW]
            return hi_part, w_hl[:, s * 2 * UW + UW:(s + 1) * 2 * UW], raw

        for s in range(2):
            hi_part, lo_part, raw = split_unit(s, s)
            pool.tensor_copy(hi_part, raw).then_inc(w_hi, 1)
            pool.wait_ge(w_hi, s + 1)
            pool.tensor_tensor(lo_part, raw, hi_part.bitcast(F32), ALU.subtract).then_inc(w_split, 1)
        with pool.Fori(1, NUNITS // 2) as i:
            for s in range(2):
                pool.wait_ge(w_used, 2 * i + (s - 1))
                hi_part, lo_part, raw = split_unit(s, 16 * i + 16)
                pool.sem_inc(w_seen, 1)
                pool.tensor_copy(hi_part, raw).then_inc(w_hi, 1)
                pool.wait_ge(w_hi, 2 * i + (s + 1))
                pool.tensor_tensor(lo_part, raw, hi_part.bitcast(F32), ALU.subtract).then_inc(w_split, 1)

    @block.tensor
    def _(pe):
        def w(s, part, k):
            return w_hl[:, (2 * s + part) * UW + k * P:(2 * s + part) * UW + (k + 1) * P]

        PASSES = ((0, 0), (0, 1), (1, 0))

        def feature_major(s, src, src_cols, src_chunk, ks, out_at, n=T, w0=0):
            for k in range(ks):
                for wp, xp in PASSES:
                    for a in range(0, n, 512):
                        m = min(512, n - a)
                        o = xp * src_cols + src_chunk * k + a
                        mm = pe.matmul(PS[:, out_at + a:out_at + a + m], w(s, wp, w0 + k), src[:, o:o + m],
                                       start=(k == 0 and wp == 0 and xp == 0), stop=(k == ks - 1 and wp == 1))
            return mm

        def token_major(s, src, src_cols, src_chunk, ks, out_at, tiles, w0=0, first=0):
            for i in range(tiles):
                for k in range(ks):
                    for n, (xp, wp) in enumerate(PASSES):
                        o = xp * src_cols + src_chunk * k + (first + i) * P
                        mm = pe.matmul(PS[:, out_at + i * P:out_at + (i + 1) * P], src[:, o:o + P],
                                       w(s, wp, w0 + k), start=(k == 0 and n == 0), stop=(k == ks - 1 and n == 2))
            return mm

        def take(p, number):
            pe.wait_ge(free[p], number + 1)

        def norm(idx, p2, p3, n=T):
            pe.wait_ge(acc_ready, idx + 1)
            take(2, p2)
            for j in range(n // P):
                mm = pe.matmul(PS[:, 2048 + j:2049 + j], ACC[:, j * P:(j + 1) * P], ones[:, 0:1],
                               start=True, stop=True)
            mm.then_inc(done[2], 1)
            pe.wait_ge(diag_ready, idx + 1)
            take(3, p3)
            for a in range(0, n, 512):
                m = min(512, n - a)
                mm = pe.matmul(PS[:, 3072 + a:3072 + a + m], ones[:, :], DIAG[:, a:a + m], start=True, stop=True)
            mm.then_inc(done[3], 1)

        def phase_norm(phase, n=T):
            norm(before(phase, "norm"), before(phase, 2), before(phase, 3), n)

        def b(phase, p):
            return before(phase, p)

        pe.wait_ge(rbx_ready, 1)
        for h in range(HEADS_C):
            take(0, h)
            take(1, h)
            for a in range(0, GROW, 512):
                m = min(512, GROW - a)
                mm = pe.matmul(PS[:, a:a + m], rbx[0:33, h * P:(h + 1) * P], onehot[0:33, a:a + m],
                               start=True, stop=True)
                if a == 512:
                    mm.then_inc(done[0], 1)
            mm.then_inc(done[1], 1)

        phase_norm("norm1")

        unit = 0
        for j in range(4):
            take(j % 2, b("ux", j % 2) + j // 2)
            pe.wait_ge(w_split, unit + 1)
            if j == 0:
                pe.wait_ge(lo, 8)
            feature_major(unit % 2, H, KC * T, T, KC, (j % 2) * 1024).then_inc(w_used, 1)
            pe.wait_ge(w_used, unit + 1)
            pe.sem_inc(done[j % 2], 1)
            unit += 1
        for j in range(2):
            take(2 + j, b("va", 2 + j))
            pe.wait_ge(w_split, unit + 1)
            token_major(unit % 2, H, KC * T, T, KC, 2048 + j * 1024, QT_N).then_inc(w_used, 1)
            pe.wait_ge(w_used, unit + 1)
            pe.sem_inc(done[2 + j], 1)
            unit += 1
        pe.wait_ge(wst_ready, 1)
        pe.wait_ge(va_norm, QT_N)
        for j in range(2):
            take(2 + j, b("gmlp", 2 + j))
            for i in range(QT_N):
                for g in range(2):
                    mm = pe.matmul(PS[64 * g:64 * g + 64, 2048 + j * 1024 + i * P:2048 + j * 1024 + (i + 1) * P],
                                   VA[:, i * 256 + (2 * j + g) * 64:i * 256 + (2 * j + g) * 64 + 64],
                                   WST[:, (2 * j + g) * P:(2 * j + g + 1) * P], start=True, stop=True)
            mm.then_inc(done[2 + j], 1)
        pe.wait_ge(c_gm, 16 * 15)
        for j in range(2):
            pe.wait_ge(p_ready, j + 1)
            take(2 + j, b("pool", 2 + j))
            for a in (0, 512):
                mm = pe.matmul(PS[:, 2048 + j * 1024 + a:2048 + j * 1024 + a + 512], BD[:, j * P:(j + 1) * P],
                               XB[:, j * PADX + 16 + a:j * PADX + 16 + a + 512], start=True, stop=True)
            mm.then_inc(done[2 + j], 1)

        with pe.Fori(0, HEADS_C // 2) as i:
            for hh in range(2):
                u0 = before("diff", "unit") + 3 * hh
                n0, n1, n2, n3 = (b("diff", p) + k * hh for p, k in ((0, 10), (1, 9), (2, 9), (3, 9)))

                def val(x, per):
                    return i * (2 * per) + x

                for n, p in enumerate((0, 1, 0)):
                    take(p, val((n0, n1, n0 + 1)[n], (10, 9, 10)[n]))
                    pe.wait_ge(w_split, val(u0 + n + 1, 3))
                    s = (u0 + n) % 2
                    if n < 2:
                        mm = feature_major(s, H, KC * T, T, KC, p * 1024)
                    else:
                        mm = token_major(s, H, KC * T, T, KC, p * 1024, QT_N)
                    mm.then_inc(w_used, 1)
                    pe.wait_ge(w_used, val(u0 + n + 1, 3))
                    pe.sem_inc(done[p], 1)
                pe.wait_ge(qkv_ready, val(3 * hh + 2, 3))

                def scores(t):
                    n = (t + 1) * P
                    for c in range(2):
                        take(2 + c, val((n2, n3)[c] + t, 9))
                        for a in range(0, n, 512):
                            m = min(512, n - a)
                            mm = pe.matmul(PS[:, (2 + c) * 1024 + a:(2 + c) * 1024 + a + m],
                                           QT[64 * c:64 * c + 64, t * P:(t + 1) * P],
                                           KT[64 * c:64 * c + 64, a:a + m], start=True, stop=True)
                        mm.then_inc(done[2 + c], 1)

                scores(0)
                for t in range(QT_N):
                    if t + 1 < QT_N:
                        scores(t + 1)
                    pe.wait_ge(aa_ready, val(8 * hh + t + 1, 8))
                    take(0, val(n0 + 2 + t, 10))
                    for kb in range(t + 1):
                        mm = pe.transpose(PS[:, kb * P:(kb + 1) * P], AA[:, kb * P:(kb + 1) * P], ident[:, :])
                    mm.then_inc(done[0], 1)
                    if t == 0:
                        pe.wait_ge(qkv_ready, val(3 * hh + 3, 3))
                    pe.wait_ge(at_ready, val(8 * hh + t + 1, 8))
                    take(1, val(n1 + 1 + t, 9))
                    for kb in range(t + 1):
                        mm = pe.matmul(PS[:, 1024:1024 + P], VC[:, kb * P:(kb + 1) * P], AT[:, kb * P:(kb + 1) * P],
                                       start=(kb == 0), stop=(kb == t))
                    mm.then_inc(done[1], 1)
                norm(val(before("diff", "norm") + hh, 1), val(n2 + 8, 9), val(n3 + 8, 9))

        pe.wait_ge(lo, before("merge", "split"))
        with pe.Fori(0, KC) as i:
            u0 = before("merge", "unit")
            for j in range(3):
                take(j, i * (2 if j < 2 else 1) + b("merge", j))
                pe.wait_ge(w_split, i * 4 + u0 + j + 1)
                feature_major((u0 + j) % 2, H, KC * T, T, KC, j * 1024).then_inc(w_used, 1)
                pe.wait_ge(w_used, i * 4 + u0 + j + 1)
                pe.sem_inc(done[j], 1)
            pe.wait_ge(w_split, i * 4 + u0 + 4)
            s = (u0 + 3) % 2
            take(3, i + b("merge", 3))
            feature_major(s, YA, 2 * T, T, 2, 3072, w0=0).then_inc(done[3], 1)
            take(0, i * 2 + b("merge", 0) + 1)
            feature_major(s, YB, 2 * T, T, 2, 0, w0=2).then_inc(done[0], 1)
            take(1, i * 2 + b("merge", 1) + 1)
            feature_major(s, OCS, 4 * T, T, 4, 1024, w0=4).then_inc(w_used, 1)
            pe.wait_ge(w_used, i * 4 + u0 + 4)
            pe.sem_inc(done[1], 1)

        def project(phase, p0, src, ks, split_base):
            u0 = before(phase, "unit")
            pe.wait_ge(lo, split_base)
            with pe.Fori(0, KC // 2) as i:
                for s in range(2):
                    take(p0 + s, i + b(phase, p0 + s))
                    pe.wait_ge(w_split, i * 2 + u0 + s + 1)
                    feature_major((u0 + s) % 2, src, KC * T, T, ks, (p0 + s) * 1024).then_inc(w_used, 1)
                    pe.wait_ge(w_used, i * 2 + u0 + s + 1)
                    pe.sem_inc(done[p0 + s], 1)

        project("out1", 0, H, KC, before("out1", "split"))
        phase_norm("norm2")
        for n, chunks in enumerate(FF_PASSES):
            up, down = f"up{n}", f"down{n}"
            pe.wait_ge(lo, before(up, "split"))
            with pe.Fori(0, chunks) as i:
                u0 = before(up, "unit")
                for s in range(2):
                    take(s, i + b(up, s))
                    pe.wait_ge(w_split, i * 2 + u0 + s + 1)
                    feature_major((u0 + s) % 2, H, KC * T, T, KC, s * 1024).then_inc(w_used, 1)
                    pe.wait_ge(w_used, i * 2 + u0 + s + 1)
                    pe.sem_inc(done[s], 1)
            project(down, 2, FF, chunks, before(down, "split"))
        phase_norm("fnorm")
        phase_norm("norm3")
        phase_norm("normc", CTX)

        pe.wait_ge(lo, before("kvpe", "split"))
        for j in range(2):
            u = before("kvpe", "unit") + j
            take(0, b("kvpe", 0) + j)
            pe.wait_ge(w_split, u + 1)
            feature_major(u % 2, H, KC * T, T, KC, 0).then_inc(done[0], 1)
            take(1, b("kvpe", 1) + j)
            feature_major(u % 2, UC, KC * CTX, CTX, KC, 1024, n=CTX).then_inc(w_used, 1)
            pe.wait_ge(w_used, u + 1)
            pe.sem_inc(done[1], 1)
        for j in range(2):
            u = before("cq", "unit") + j
            take(j, b("cq", j))
            pe.wait_ge(w_split, u + 1)
            feature_major(u % 2, H, KC * T, T, KC, j * 1024).then_inc(w_used, 1)
            pe.wait_ge(w_used, u + 1)
            pe.sem_inc(done[j], 1)
        pe.wait_ge(tpe_ready, 2)
        take(2, b("kvpe", 2))
        for a in (0, 512):
            mm = pe.matmul(PS[:, 2048 + a:2560 + a], dup[:, :], TPE[:, CTX + a:CTX + a + 512], start=True, stop=True)
        mm.then_inc(done[2], 1)
        take(3, b("kvpe", 3))
        pe.matmul(PS[:, 3072:3072 + CTX], dup[:, :], TPE[:, 0:CTX], start=True, stop=True).then_inc(done[3], 1)
        phase_norm("cqnorm")
        phase_norm("ckvnorm")
        phase_norm("ckvcnorm", CTX)
        project("mgate", 0, H, KC, before("norm3", "split") + 8)

        pe.wait_ge(lo, before("mgate", "split"))
        pe.wait_ge(kpe_ready, 2)
        with pe.Fori(0, HEADS // 2) as i:
            for hh in range(2):
                u = before("heads", "unit") + hh
                s = u % 2
                t0 = 8 * hh
                pe.wait_ge(sc_free, i * 16 + t0 + 1)
                pe.wait_ge(pv_free, i * 16 + t0 + 1)
                pe.wait_ge(pta, i * 32 + 2 * t0 + 1)
                pe.wait_ge(ptb, i * 16 + t0 + 1)
                pe.wait_ge(w_split, i * 2 + u + 1)
                take(0, i * 4 + b("heads", 0) + 2 * hh)
                feature_major(s, CQ, 2 * T, T, 2, 0, w0=0).then_inc(done[0], 1)
                take(1, i * 4 + b("heads", 1) + 2 * hh)
                feature_major(s, CQ, 2 * T, T, 2, 1024, w0=2).then_inc(done[1], 1)
                take(2, i * 2 + b("heads", 2) + hh)
                feature_major(s, CKV, TK, TK, 1, 2048, n=T, w0=4).then_inc(done[2], 1)
                take(3, i * 2 + b("heads", 3) + hh)
                for n, (wp, xp) in enumerate(PASSES):
                    mm = pe.matmul(PS[:, 3072:3072 + CTX], w(s, wp, 4), CKV[:, xp * TK + T:xp * TK + TK],
                                   start=(n == 0), stop=(n == 2))
                mm.then_inc(done[3], 1)
                take(0, i * 4 + b("heads", 0) + 2 * hh + 1)
                token_major(s, CKV, TK, TK, 1, 0, 8, w0=5).then_inc(done[0], 1)
                take(1, i * 4 + b("heads", 1) + 2 * hh + 1)
                token_major(s, CKV, TK, TK, 1, 1024, 2, w0=5, first=8).then_inc(w_used, 1)
                pe.wait_ge(w_used, i * 2 + u + 1)
                pe.sem_inc(done[1], 1)
                pe.wait_ge(hd_act, i * 6 + 3 * hh + 3)
                pe.wait_ge(hd_dve, i * 6 + 3 * hh + 3)

                def mla_scores(t):
                    base = 1536 * (t % 2)
                    if t:
                        pe.wait_ge(sc_free, i * 16 + t0 + t)
                    for a in range(0, TK, 512):
                        m = min(512, TK - a)
                        pe.matmul(PS[:, base + a:base + a + m], QN[:, t * P:(t + 1) * P], KN[:, a:a + m],
                                  start=True, stop=False)
                        mm = pe.matmul(PS[:, base + a:base + a + m], QP[:, t * P:(t + 1) * P], KPE[:, a:a + m],
                                       start=False, stop=True)
                    mm.then_inc(sc_done, 1)

                mla_scores(0)
                for t in range(QT_N):
                    tg = t0 + t
                    if t + 1 < QT_N:
                        mla_scores(t + 1)
                    pe.wait_ge(e_ready, i * 16 + tg + 1)
                    for n, (blocks, bank) in enumerate((((0, 4), 3072), ((4, 8), 3584), ((8, 10), 3072))):
                        if bank == 3072:
                            pe.wait_ge(pta, i * 32 + 2 * tg + (n // 2) + 1)
                        else:
                            pe.wait_ge(ptb, i * 16 + tg + 1)
                            pe.wait_ge(pv_free, i * 16 + tg + 1)
                        for kb in range(*blocks):
                            mm = pe.transpose(PS[:, bank + (kb - blocks[0]) * P:bank + (kb - blocks[0] + 1) * P],
                                              E[:, (t % 2) * TK + kb * P:(t % 2) * TK + (kb + 1) * P], ident[:, :])
                        mm.then_inc(tpb_done if bank == 3584 else tpa_done, 1)
                    pe.wait_ge(ptb, i * 16 + tg + 2)
                    pe.wait_ge(pta, i * 32 + 2 * tg + 3)
                    for kb in range(10):
                        mm = pe.matmul(PS[:, 3584:3584 + P], VN[:, kb * P:(kb + 1) * P], PT[:, kb * P:(kb + 1) * P],
                                       start=(kb == 0), stop=(kb == 9))
                    mm.then_inc(pv_done, 1)

        pe.wait_ge(sc_free, 65)
        pe.wait_ge(pv_free, 65)
        pe.wait_ge(pta, 129)
        pe.wait_ge(ptb, 65)
        project("out2", 0, H, KC, before("out2", "split"))
        phase_norm("norm4")

        pe.wait_ge(lo, before("four", "split"))
        pe.wait_ge(ft_in, 16 * 4)
        with pe.Fori(0, FG) as i:
            u0 = before("four", "unit")
            for s in range(2):
                take(s, i + b("four", s))
                pe.wait_ge(w_split, i * 2 + u0 + s + 1)
                feature_major((u0 + s) % 2, H, KC * T, T, KC, s * 1024).then_inc(w_used, 1)
                pe.wait_ge(w_used, i * 2 + u0 + s + 1)
                pe.sem_inc(done[s], 1)
            pe.wait_ge(ze_ready, i * 2 + 2)
            take(2, i * 2 + b("four", 2))
            for q in range(2):
                for k in range(4):
                    mm = pe.matmul(PS[:, 2048 + q * 512 + k * P:2048 + q * 512 + (k + 1) * P],
                                   ZEO[:, q * HALF + k * P:q * HALF + (k + 1) * P], CSD[:, q * P:(q + 1) * P],
                                   start=True, stop=True)
            mm.then_inc(done[2], 1)
            take(3, i * 2 + b("four", 3))
            pe.matmul(PS[0:1, 3072:3072 + P], ZR[:, HALF:HALF + 1], CSD[:, 0:P], start=True, stop=True
                      ).then_inc(done[3], 1)
            pe.wait_ge(m_evac, i * 2 + 2)
            pe.wait_ge(mr_ready, i + 1)
            take(3, i * 2 + b("four", 3) + 1)
            for k in range(4):
                pe.matmul(PS[:, 3072:3584], M12[:, k * P:(k + 1) * P], CTAB[:, k * HALF:(k + 1) * HALF],
                          start=(k == 0), stop=False)
            pe.matmul(PS[:, 3072:3584], MR[0:1, :], ALT[0:1, :], start=False, stop=True)
            for k in range(4):
                mm = pe.matmul(PS[:, 3584:4096], M12[:, HALF + k * P:HALF + (k + 1) * P],
                               STAB[:, k * HALF:(k + 1) * HALF], start=(k == 0), stop=(k == 3))
            mm.then_inc(done[3], 1)
            take(2, i * 2 + b("four", 2) + 1)
            for k in range(4):
                pe.matmul(PS[:, 2048:2049], M12[:, k * P:(k + 1) * P], v1("alt"), start=(k == 0), stop=False)
            pe.matmul(PS[:, 2048:2049], MR[0:1, :], ones[0:1, 0:1], start=False, stop=True).then_inc(done[2], 1)
        project("out3", 0, H, KC, before("out3", "split"))
        phase_norm("final")

    @block.scalar
    def _(act):
        chain = Chain(act, s_act)

        def norm(idx, eps_cols):
            act.wait_ge(ms_ready, idx + 1)
            act.activation(stat[:, 0:eps_cols], stat[:, 0:eps_cols], ACT.Sqrt).then_inc(sd_ready, 1)

        def phase_norm(phase, n=T):
            norm(before(phase, "norm"), n // P)

        for h in range(HEADS_C):
            act.wait_ge(g_row, h + 1)
            act.dma_start(scratch[h].rearrange("(p n) -> p n", p=P), grow[:, :]).then_inc(g_out, 16)
        for c in range(KC):
            act.wait_ge(x_in[c], 16)
            if c >= 1:
                act.wait_ge(sq_added, c)
            act.activation(SQ, X[:, c * T:(c + 1) * T], ACT.Square).then_inc(sq_ready, 1)
        phase_norm("norm1")
        xts = [0]

        def hi_blocks(dst, cols_, size, count, base):
            for c in range(count):
                xts[0] += 1
                act.wait_ge(xt, xts[0])
                act.activation(dst[:, c * size:(c + 1) * size], TMP[c % 2][:, 0:size], ACT.Copy).then_inc(hi, 1)

        hi_blocks(H, KC * T, T, KC, 0)
        act.wait_ge(lam_sum, 1)
        act.activation(cols[:, 2:4], cols[:, 0:2], ACT.Exp).then_inc(lam_exp, 1)
        for j in range(4):
            p = j % 2
            act.wait_ge(done[p], before("ux", p) + j // 2 + 1)
            if j < 2:
                chain(act.activation(U[:, j * T:(j + 1) * T], pair(p), ACT.Gelu))
            else:
                chain(act.activation(XB[:, (j - 2) * PADX + 16:(j - 2) * PADX + 16 + T], pair(p), ACT.Copy))
            act.sem_inc(free[p], 1)
            act.sem_inc(u_ready if j < 2 else xb_ready, 1)
        for j in range(2):
            act.wait_ge(done[2 + j], before("va", 2 + j) + 1)
            dst = VA[:, :].rearrange("p (i c) -> p i c", i=QT_N)[:, :, j * P:(j + 1) * P]
            chain(act.activation(dst, pair(2 + j).rearrange("p (i c) -> p i c", i=QT_N), ACT.Gelu))
            act.sem_inc(free[2 + j], 1)
            act.sem_inc(va_ready, 1)
        act.wait_ge(va_ms, 1)
        act.activation(stat[:, 0:QT_N], stat[:, 0:QT_N], ACT.Sqrt).then_inc(va_sd, 1)
        act.wait_ge(g_out, 16 * HEADS_C)
        for j in range(2):
            xts[0] += 1
            act.wait_ge(xt, xts[0])
            act.activation(YA[:, j * T:(j + 1) * T], TMP[j], ACT.Copy).then_inc(hi, 1)
        for j in range(2):
            act.wait_ge(done[2 + j], before("pool", 2 + j) + 1)
            act.activation(YB[:, j * T:(j + 1) * T], pair(2 + j), ACT.Copy, scale=v1("pool_scale", j)).then_inc(hi, 1)

        act.wait_ge(lo, 12)
        with act.Fori(0, HEADS_C // 2) as i:
            for hh in range(2):
                n0, n1 = before("diff", 0) + 10 * hh, before("diff", 1) + 9 * hh
                if hh == 1:
                    act.wait_ge(neg_ready, i * 16 + 8 * hh)
                else:
                    act.wait_ge(lo, i * 2 + 12)
                act.dma_start(BR[:, :], shifted[bass.ds(i * 2 + hh, 1)].rearrange("o p n -> p (o n)")
                              ).then_inc(br_in, 16)
                act.wait_ge(done[0], i * 20 + n0 + 1)
                chain_q = act.activation(QT[:, :], pair(0), ACT.Copy, scale=0.125)
                chain_q.then_inc(qkv_ready, 1)
                act.wait_ge(qkv_ready, i * 6 + 3 * hh + 1)
                act.sem_inc(free[0], 1)
                act.wait_ge(done[1], i * 18 + n1 + 1)
                act.activation(KT[:, :], pair(1), ACT.Copy).then_inc(qkv_ready, 1)
                act.wait_ge(qkv_ready, i * 6 + 3 * hh + 2)
                act.sem_inc(free[1], 1)
                act.wait_ge(done[0], i * 20 + n0 + 2)
                act.activation(VC[:, :], pair(0), ACT.Copy).then_inc(qkv_ready, 1)
                act.wait_ge(qkv_ready, i * 6 + 3 * hh + 3)
                act.sem_inc(free[0], 1)

                def exps(t):
                    n = (t + 1) * P
                    act.wait_ge(neg_ready, i * 16 + 8 * hh + t + 1)
                    for c, S in enumerate((S0, S1)):
                        act.activation(S[:, 0:n], S[:, 0:n], ACT.Exp, bias=cols[:, 8 + c:9 + c],
                                       accum_out=cols[:, 10 + c:11 + c]).then_inc(exp_ready, 1)

                exps(0)
                for t in range(QT_N):
                    n = (t + 1) * P
                    act.wait_ge(done[0], i * 20 + n0 + 3 + t)
                    act.activation(AT[:, 0:n], PS[:, 0:n], ACT.Copy).then_inc(at_ready, 1)
                    act.wait_ge(at_ready, i * 16 + 8 * hh + t + 1)
                    act.sem_inc(free[0], 1)
                    if t + 1 < QT_N:
                        exps(t + 1)
                act.wait_ge(oc_ready, i * 16 + 8 * hh + 8)
                act.activation(ACC, OC, ACT.Square).then_inc(acc_ready, 1)
                norm(i * 2 + before("diff", "norm") + hh, QT_N)
                act.wait_ge(xt, i * 2 + xts[0] + hh + 1)
                act.activation(OCS[:, bass.ds(i * (2 * T) + hh * T, T)], TMP0, ACT.Copy).then_inc(hi, 1)
        xts[0] += 4

        with act.Fori(0, KC) as i:
            for j in range(3):
                act.wait_ge(done[j], i * (2 if j < 2 else 1) + before("merge", j) + 1)
                act.wait_ge(m_ready, i * 3 + j + 1)
                act.activation(SC[:, j * TS:j * TS + T], pair(j), ACT.Sigmoid,
                               bias=vec[:, bass.ds(i + (VEC["b_gate"] + 8 * j), 1)]).then_inc(sg_ready, 1)
                act.wait_ge(sg_ready, i * 3 + j + 1)
                act.sem_inc(free[j], 1)
        act.wait_ge(done[1], before("out1", 1))
        for c in range(KC):
            act.dma_start(XIN[:, c * T:(c + 1) * T], t_in["x"][c]).then_inc(c_x, 16)

        def block_hi(src, base_split):
            with act.Fori(0, KC) as i:
                act.activation(H[:, bass.ds(i * T, T)], src[:, bass.ds(i * T, T)], ACT.Copy).then_inc(hi, 1)

        act.wait_ge(m_ready, 3 * KC + 3)
        block_hi(M, 0)

        def residual(phase, extra=None):
            def turn(i, more):
                for s in range(2):
                    act.wait_ge(x_new, i * 2 + before(phase, "xnew") + s + 1)
                    act.activation(SQ, X[:, bass.ds(i * (2 * T) + s * T, T)], ACT.Square).then_inc(sq_ready, 1)
                    if more:
                        more(i, s)

            with act.Fori(0, KC // 2 - 1) as i:
                turn(i, extra)
            turn(KC // 2 - 1, None)

        residual("out1")
        phase_norm("norm2")
        hi_blocks(H, KC * T, T, KC, 0)

        f0 = 0
        for n, chunks in enumerate(FF_PASSES):
            up = f"up{n}"
            with act.Fori(0, chunks) as i:
                act.wait_ge(done[0], i + before(up, 0) + 1)
                act.wait_ge(cv_ready, i + f0 + 1)
                act.activation(SC[:, 2:2 + T], pair(0), ACT.Copy).then_inc(gp_ready, 1)
                act.wait_ge(gp_ready, i + f0 + 1)
                act.sem_inc(free[0], 1)
                act.wait_ge(cv_ready, i + f0 + 2)
                act.activation(SC[:, 2 * TS:2 * TS + T], SC[:, TS:TS + T], ACT.Gelu,
                               bias=vec[:, bass.ds(i + (VEC["conv_b"] + f0), 1)]).then_inc(gl_ready, 1)
                act.wait_ge(xt, i + xts[0] + 1)
                act.activation(FF[:, bass.ds(i * T, T)], SC[:, 3 * TS:3 * TS + T], ACT.Copy).then_inc(hi, 1)
            xts[0] += chunks
            f0 += chunks
            if n == len(FF_PASSES) - 1:
                act.wait_ge(done[1], before("down2", 1))
                act.dma_start(CL[:, :], t_in["c"].partition_broadcast(P)).then_inc(c_rows, 16)
                act.dma_start(CC[:, :], t_in["c_ctx"].partition_broadcast(P)).then_inc(c_rows, 16)
                for g in range(2):
                    act.dma_start(AW[:, g * 6 * D:(g + 1) * 6 * D], t_in["ada"][g]).then_inc(ada_in[g], 16)
                act.wait_ge(c_rows, 32)
                act.activation(CL[:, :], CL[:, :], ACT.Silu).then_inc(c_silu, 1)
                act.activation(CC[:, :], CC[:, :], ACT.Silu).then_inc(c_silu, 1)

                def next_ada(i, s):
                    act.wait_ge(ada_used, i * 2 + s + 1)
                    act.dma_start(AW[:, s * 6 * D:(s + 1) * 6 * D],
                                  t_in["ada"][bass.ds(i * 2 + s + 2, 1)].rearrange("o p n -> p (o n)")
                                  ).then_inc(ada_in[s], 16)

                residual("down2", extra=next_ada)
        phase_norm("fnorm")
        for c in range(KC):
            act.wait_ge(x_new, before("fnorm", "xnew") + c + 1)
            if c >= 1:
                act.wait_ge(sq_added, before("norm3", "square") + c)
            act.activation(SQ, X[:, c * T:(c + 1) * T], ACT.Square).then_inc(sq_ready, 1)
        phase_norm("norm3")
        hi_blocks(H, KC * T, T, KC, 0)
        act.dma_start(CXR[:, :], t_in["ctx"]).then_inc(ctx_in, 16)
        act.dma_start(CST[:, :], t_in["cs"]).then_inc(cs_in, 16)
        act.wait_ge(ctx_in, 16)
        for c in range(KC):
            if c >= 1:
                act.wait_ge(sq_added, before("normc", "square") + c)
            act.activation(SQ[:, 0:CTX], CXR[:, c * CTX:(c + 1) * CTX], ACT.Square).then_inc(sq_ready, 1)
        phase_norm("normc", CTX)
        hi_blocks(UC, KC * CTX, CTX, KC, 0)
        act.wait_ge(done[0], before("kvpe", 0) + 1)
        chain(act.activation(CKR[:, 0:T], pair(0), ACT.Copy))
        act.sem_inc(free[0], 1)
        act.wait_ge(done[1], before("kvpe", 1) + 1)
        chain(act.activation(CKR[:, T:TK], pair(1, CTX), ACT.Copy))
        act.sem_inc(free[1], 1)
        act.sem_inc(ckr_ready, 1)
        for j in range(2):
            act.wait_ge(done[j], before("cq", j) + 1)
            chain(act.activation(CQR[:, j * T:(j + 1) * T], pair(j), ACT.Copy))
            act.sem_inc(free[j], 1)
        act.wait_ge(done[2], before("kvpe", 2) + 1)
        chain(act.activation(KPE[:, 0:T], pair(2), ACT.Copy))
        act.sem_inc(free[2], 1)
        act.wait_ge(done[3], before("kvpe", 3) + 1)
        chain(act.activation(KPE[:, T:TK], pair(3, CTX), ACT.Copy))
        act.sem_inc(free[3], 1)
        act.sem_inc(kpe_ready, 2)
        for c in range(2):
            if c:
                act.wait_ge(sq_added, before("cqnorm", "square") + 1)
            act.activation(SQ, CQR[:, c * T:(c + 1) * T], ACT.Square).then_inc(sq_ready, 1)
        phase_norm("cqnorm")
        hi_blocks(CQ, 2 * T, T, 2, 0)
        for phase, a, n in (("ckvnorm", 0, T), ("ckvcnorm", T, CTX)):
            act.wait_ge(lo, before(phase, "split"))
            act.activation(ACC[:, 0:n], CKR[:, a:a + n], ACT.Square).then_inc(acc_ready, 1)
            phase_norm(phase, n)
            xts[0] += 1
            act.wait_ge(xt, xts[0])
            act.activation(CKV[:, a:a + n], TMP0[:, 0:n], ACT.Copy).then_inc(hi, 1)
        act.wait_ge(lo, before("mgate", "split"))
        with act.Fori(0, KC // 2) as i:
            for s in range(2):
                act.wait_ge(done[s], i + before("mgate", s) + 1)
                act.activation(G[:, bass.ds(i * (2 * T) + s * T, T)], pair(s), ACT.Silu).then_inc(gate_ready, 1)
                act.wait_ge(gate_ready, i * 2 + s + 1)
                act.sem_inc(free[s], 1)
        act.dma_start(CSQ[:, :], t_in["cs"][:, CTX:TK]).then_inc(csq_in, 16)

        with act.Fori(0, HEADS // 2) as i:
            for hh in range(2):
                t0 = 8 * hh
                for n, (dst, p, m, at_) in enumerate(((QN, 0, T, 0), (KN, 2, T, 0), (KN, 3, CTX, T))):
                    per = 2 if p == 0 else 1
                    act.wait_ge(done[p], i * (2 * per) + before("heads", p) + per * hh + 1)
                    act.activation(dst[:, at_:at_ + m], pair(p, m), ACT.Copy).then_inc(hd_act, 1)
                    act.wait_ge(hd_act, i * 6 + 3 * hh + n + 1)
                    act.sem_inc(free[p], 1)

                def mla_exp(t):
                    tg = t0 + t
                    act.wait_ge(mx_ready, i * 16 + tg + 1)
                    if tg >= 2:
                        act.wait_ge(tpa_done, i * 32 + 2 * tg - 2)
                    base = 1536 * (t % 2)
                    act.activation(E[:, (t % 2) * TK:(t % 2) * TK + TK], PS[:, base:base + TK], ACT.Exp,
                                   bias=cols[:, 16 + t % 2:17 + t % 2], scale=MLA_SCALE,
                                   accum_out=cols[:, 18 + t % 2:19 + t % 2]).then_inc(ex_ready, 1)
                    act.wait_ge(ex_ready, i * 16 + tg + 1)
                    act.sem_inc(sc_free, 1)

                mla_exp(0)
                for t in range(QT_N):
                    tg = t0 + t
                    if t + 1 < QT_N:
                        mla_exp(t + 1)
                    for n, (a, m) in enumerate(((0, 512), (1024, 256))):
                        act.wait_ge(tpa_done, i * 32 + 2 * tg + n + 1)
                        act.activation(PT[:, a:a + m], PS[:, 3072:3072 + m], ACT.Copy).then_inc(pta, 1)
        act.wait_ge(pv_free, 65)
        block_hi(G, 0)

        act.dma_start(CTAB[:, :], t_in["ctab"]).then_inc(ft_in, 16)
        act.dma_start(STAB[:, :], t_in["stab"]).then_inc(ft_in, 16)
        act.dma_start(CSD[:, :], t_in["csd"]).then_inc(ft_in, 16)
        act.dma_start(ALT[0:1, :], t_in["altrow"]).then_inc(ft_in, 16)
        residual("out2")
        phase_norm("norm4")
        hi_blocks(H, KC * T, T, KC, 0)
        with act.Fori(0, FG) as i:
            act.wait_ge(done[0], i + before("four", 0) + 1)
            act.activation(ZR[:, :], pair(0), ACT.Copy).then_inc(zr_ready, 1)
            act.wait_ge(zr_ready, i + 1)
            act.sem_inc(free[0], 1)
            act.wait_ge(done[1], i + before("four", 1) + 1)
            act.wait_ge(y_ready, i * 2 + 1)
            act.activation(TMP1, pair(1), ACT.Silu).then_inc(sgf_ready, 1)
            act.wait_ge(sgf_ready, i + 1)
            act.sem_inc(free[1], 1)
            act.wait_ge(done[2], i * 2 + before("four", 2) + 1)
            act.activation(M12[:, 0:HALF], PS[:, 2048:2560], ACT.Copy).then_inc(m_evac, 1)
            act.wait_ge(done[3], i * 2 + before("four", 3) + 1)
            act.activation(MR[0:1, :], PS[0:1, 3072:3072 + P], ACT.Copy).then_inc(mr_ready, 1)
            act.wait_ge(mr_ready, i + 1)
            act.sem_inc(free[3], 1)
            act.wait_ge(done[3], i * 2 + before("four", 3) + 2)
            act.activation(TMP0[:, 0:HALF], PS[:, 3584:4096], ACT.Copy).then_inc(qs_ready, 1)
        act.wait_ge(y_ready, 2 * FG + 1)
        block_hi(Y, 0)
        residual("out3")
        phase_norm("final")
        for c in range(KC):
            act.wait_ge(o_ready, c + 1)
            act.dma_start(out[c], X[:, c * T:(c + 1) * T]).then_inc(o_out, 16)
        act.wait_ge(o_out, 16 * KC)

    @block.vector
    def _(v):
        chain = Chain(v, s_dve)
        for p in range(4):
            v.sem_inc(free[p], 1)
        for s in (sc_free, pv_free, pta, ptb):
            v.sem_inc(s, 1)
        v.sem_inc(m_ready, 3)
        v.sem_inc(cv_ready, 1)
        v.sem_inc(y_ready, 1)
        xts = [0]
        his = [0]
        sqs = [0]

        chain(v.memset(ones[:, :], 1.0))
        v.memset(BD[:, :], 0.0).then_inc(memset_done, 1)
        chain(v.memset(XB[:, :], 0.0))
        v.wait_ge(c_early, 64)
        chain(v.memset(rbx[32:33, :], 1.0))
        chain(v.tensor_copy(rbx[0:32, :].rearrange("p (h n) -> p h n", h=HEADS_C),
                            rb[0:32, :].unsqueeze(2).to_broadcast([32, HEADS_C, P])))
        v.sem_inc(rbx_ready, 1)
        for h in range(HEADS_C):
            v.wait_ge(done[0], h + 1)
            v.wait_ge(done[1], h + 1)
            if h:
                v.wait_ge(g_out, 16 * h)
            chain(v.tensor_copy(grow[:, :], PS[:, 0:GROW]))
            v.sem_inc(free[0], 1)
            v.sem_inc(free[1], 1)
            v.sem_inc(g_row, 1)

        def add_squares(count, n=T, first=True):
            for c in range(count):
                sqs[0] += 1
                v.wait_ge(sq_ready, sqs[0])
                if c == 0:
                    ins = v.tensor_copy(ACC[:, 0:n], SQ[:, 0:n])
                else:
                    ins = v.tensor_tensor(ACC[:, 0:n], ACC[:, 0:n], SQ[:, 0:n], ALU.add)
                ins.then_inc(sq_added, 1)
                acs[0] += 1
                v.wait_ge(sq_added, acs[0])
            v.sem_inc(acc_ready, 1)

        acs = [0]

        def norm_scale(idx, p2, p3, n, width, eps):
            k = n // P
            v.wait_ge(done[2], p2 + 1)
            v.tensor_scalar(stat[:, 0:k], PS[:, 2048:2048 + k], 1.0 / width, eps, ALU.mult, ALU.add
                            ).then_inc(ms_ready, 1)
            v.wait_ge(ms_ready, idx + 1)
            v.sem_inc(free[2], 1)
            v.wait_ge(sd_ready, idx + 1)
            chain(v.reciprocal(stat[:, 0:k], stat[:, 0:k]))
            v.tensor_tensor(DIAG[:, 0:n].rearrange("p (j c) -> p j c", j=k),
                            ident[:, :].unsqueeze(1).to_broadcast([P, k, P]),
                            stat[:, 0:k].unsqueeze(2).to_broadcast([P, k, P]), ALU.mult).then_inc(diag_ready, 1)
            v.wait_ge(done[3], p3 + 1)

        def phase_scale(phase, width, eps, n=T):
            norm_scale(before(phase, "norm"), before(phase, 2), before(phase, 3), n, width, eps)

        def apply_split(dst, dst_cols, src, count, n, gain, shift=None, last_free=3):
            def make(c):
                t = TMP[c % 2][:, 0:n]
                ins = v.scalar_tensor_tensor(out=t, in0=src[:, c * n:(c + 1) * n], scalar=gain(c),
                                             in1=PS[:, 3072:3072 + n], op0=ALU.mult, op1=ALU.mult)
                if shift is not None:
                    chain(ins)
                    ins = v.tensor_scalar(t, t, shift(c), None, ALU.add)
                ins.then_inc(xt, 1)

            def low(c):
                his[0] += 1
                v.wait_ge(xt, xts[0] + c + 1)
                v.wait_ge(hi, his[0])
                h = dst[:, c * n:(c + 1) * n]
                v.tensor_tensor(dst[:, dst_cols + c * n:dst_cols + (c + 1) * n], TMP[c % 2][:, 0:n],
                                h.bitcast(F32), ALU.subtract).then_inc(lo, 1)
                v.wait_ge(lo, his[0])

            make(0)
            for c in range(count):
                if c + 1 < count:
                    make(c + 1)
                low(c)
            v.sem_inc(free[3], 1)
            xts[0] += count

        add_squares(KC)
        for c in range(KC):
            v.wait_ge(x_in[c], 16)
        phase_scale("norm1", D, 1e-6)
        apply_split(H, KC * T, X, KC, T, lambda c: v1("attn_g", c))

        v.wait_ge(c_gm, 16 * 15)
        for q in range(2):
            chain(v.tensor_tensor(lvp[:, :], lv[:, 128 * q:128 * q + 64], lv[:, 128 * q + 64:128 * q + 128], ALU.mult))
            chain(v.tensor_reduce(cols[:, q:q + 1], lvp[:, :], AX, ALU.add))
        v.sem_inc(lam_sum, 1)
        v.wait_ge(lam_exp, 1)
        chain(v.tensor_tensor(cols[:, 4:5], cols[:, 2:3], cols[:, 3:4], ALU.subtract))
        chain(v.tensor_scalar(cols[:, 5:6], cols[:, 4:5], LAM_INIT, None, ALU.add))
        chain(v.tensor_scalar(cols[:, 6:7], v1("subln"), 1.0 - LAM_INIT, None, ALU.mult))
        v.tensor_tensor(WST[:, :].rearrange("p (g t) -> p g t", g=4), WST[:, :].rearrange("p (g t) -> p g t", g=4),
                        TRI[:, :].unsqueeze(1).to_broadcast([P, 4, P]), ALU.mult).then_inc(wst_ready, 1)

        v.wait_ge(va_ready, 2)
        for i in range(QT_N):
            chain(v.bn_stats(bn[:, 0:6], VA[:, i * 256:(i + 1) * 256]))
            chain(v.bn_aggr(cols[:, 32 + 2 * i:34 + 2 * i], bn[:, 0:6]))
        chain(v.tensor_scalar(stat[:, 0:QT_N], cols[:, 32:48].rearrange("p (i c) -> p i c", c=2)[:, :, 1], 1e-5, None,
                              ALU.add))
        v.sem_inc(va_ms, 1)
        v.wait_ge(va_sd, 1)
        chain(v.reciprocal(stat[:, 0:QT_N], stat[:, 0:QT_N]))
        for i in range(QT_N):
            row = VA[:, i * 256:(i + 1) * 256]
            chain(v.tensor_scalar(row, row, cols[:, 32 + 2 * i:33 + 2 * i], stat[:, i:i + 1], ALU.subtract, ALU.mult))
            chain(v.tensor_tensor(row, row, lngb[:, 0:256], ALU.mult))
            v.tensor_tensor(row, row, lngb[:, 256:512], ALU.add).then_inc(va_norm, 1)
        v.wait_ge(u_ready, 2)
        for j in range(2):
            v.wait_ge(done[2 + j], before("gmlp", 2 + j) + 1)
            chain(v.tensor_tensor(TMP[j].rearrange("p (i t) -> p i t", i=QT_N),
                                  pair(2 + j).rearrange("p (i t) -> p i t", i=QT_N),
                                  SGB[:, j * P:(j + 1) * P].unsqueeze(1).to_broadcast([P, QT_N, P]), ALU.add))
            v.sem_inc(free[2 + j], 1)
            v.tensor_tensor(TMP[j], TMP[j], U[:, j * T:(j + 1) * T], ALU.mult).then_inc(xt, 1)
            xts[0] += 1
            v.wait_ge(xt, xts[0])
            his[0] += 1
            v.wait_ge(hi, his[0])
            v.tensor_tensor(YA[:, 2 * T + j * T:2 * T + (j + 1) * T], TMP[j],
                            YA[:, j * T:(j + 1) * T].bitcast(F32), ALU.subtract).then_inc(lo, 1)
            v.wait_ge(lo, his[0])

        v.wait_ge(xb_ready, 2)
        chain(v.memset(PA[:, 0:2 * PADX], 0.0))
        chain(v.memset(PB[:, :], 0.0))

        def double(dst, src, step, parts, j):
            a = j * PADX + 16
            chain(v.tensor_tensor(dst[parts, a:a + T], src[parts, a:a + T], src[parts, a - step:a - step + T], ALU.add))

        every = slice(0, P)
        for j in range(2):
            double(PA, XB, 1, every, j)
            double(PB, PA, 2, every, j)
        double(PA, PB, 4, every, 1)
        double(PB, PA, 8, slice(64, P), 1)
        sums = {0: PA, 1: PB, 2: PA, 3: PB}
        for g in range(4):
            j, parts = g // 2, slice(64 * (g % 2), 64 * (g % 2) + 64)
            a = j * PADX + 16
            s = sums[g]
            chain(v.tensor_tensor(s[parts, a:a + 16], s[parts, a:a + 16], EDGE[parts, j * 16:(j + 1) * 16], ALU.mult))
            x = XB[parts, a:a + T]
            chain(v.scalar_tensor_tensor(out=x[:, 16:T], in0=s[parts, a + 16:a + T],
                                         scalar=vec[parts, VEC["pool_inv"] + j:VEC["pool_inv"] + j + 1],
                                         in1=x[:, 16:T], op0=ALU.mult, op1=ALU.subtract))
            chain(v.tensor_tensor(x[:, 0:16], s[parts, a:a + 16], x[:, 0:16], ALU.subtract))
            if g % 2:
                v.sem_inc(p_ready, 1)
        for j in range(2):
            v.wait_ge(done[2 + j], before("pool", 2 + j) + 1)
            his[0] += 1
            v.wait_ge(hi, his[0])
            v.scalar_tensor_tensor(out=YB[:, 2 * T + j * T:2 * T + (j + 1) * T], in0=pair(2 + j),
                                   scalar=v1("pool_scale", j), in1=YB[:, j * T:(j + 1) * T].bitcast(F32),
                                   op0=ALU.mult, op1=ALU.subtract).then_inc(lo, 1)
            v.wait_ge(lo, his[0])
            v.sem_inc(free[2 + j], 1)

        with v.Fori(0, HEADS_C // 2) as i:
            chain.enter(i, 2 * (8 * 7 + 1))
            for hh in range(2):
                n0, n1, n2, n3 = (before("diff", p) + k * hh for p, k in ((0, 10), (1, 9), (2, 9), (3, 9)))
                v.wait_ge(br_in, i * 32 + 16 * hh + 16)

                def biased(t):
                    n = (t + 1) * P
                    for c, S in enumerate((S0, S1)):
                        v.wait_ge(done[2 + c], i * 18 + (n2, n3)[c] + t + 1)
                        v.sem_inc(sc_seen, 1)
                        chain(v.tensor_tensor_reduce(out=S[:, 0:n], in0=PS[:, (2 + c) * 1024:(2 + c) * 1024 + n],
                                                     in1=BR[:, T - n:T], scale=1.0, scalar=-3.0e38, op0=ALU.add,
                                                     op1=ALU.max, accum_out=cols[:, 12 + c:13 + c]))
                        v.sem_inc(free[2 + c], 1)
                    v.tensor_scalar(cols[:, 8:10], cols[:, 12:14], -1.0, None, ALU.mult).then_inc(neg_ready, 1)

                biased(0)
                for t in range(QT_N):
                    n = (t + 1) * P
                    v.wait_ge(exp_ready, i * 32 + 16 * hh + 2 * t + 2)
                    chain(v.reciprocal(cols[:, 14:16], cols[:, 10:12]))
                    chain(v.tensor_tensor(cols[:, 20:21], cols[:, 15:16], cols[:, 5:6], ALU.mult))
                    chain(v.tensor_scalar(S1[:, 0:n], S1[:, 0:n], cols[:, 20:21], None, ALU.mult))
                    if t:
                        v.wait_ge(done[0], i * 20 + n0 + 2 + t)
                    chain(v.scalar_tensor_tensor(out=AA[:, 0:n], in0=S0[:, 0:n], scalar=cols[:, 14:15],
                                                 in1=S1[:, 0:n], op0=ALU.mult, op1=ALU.subtract))
                    v.sem_inc(aa_ready, 1)
                    if t + 1 < QT_N:
                        biased(t + 1)
                    v.wait_ge(done[1], i * 18 + n1 + 2 + t)
                    chain(v.tensor_copy(OC[:, t * P:(t + 1) * P], PS[:, 1024:1024 + P]))
                    v.sem_inc(free[1], 1)
                    v.sem_inc(oc_ready, 1)
                norm_scale(i * 2 + before("diff", "norm") + hh, i * 18 + n2 + 8, i * 18 + n3 + 8, T, P, 1e-5)
                v.scalar_tensor_tensor(out=TMP0, in0=OC, scalar=cols[:, 6:7], in1=PS[:, 3072:4096],
                                       op0=ALU.mult, op1=ALU.mult).then_inc(xt, 1)
                v.wait_ge(xt, i * 2 + xts[0] + hh + 1)
                v.sem_inc(free[3], 1)
                v.wait_ge(hi, i * 2 + his[0] + hh + 1)
                v.tensor_tensor(OCS[:, bass.ds(i * (2 * T) + 4 * T + hh * T, T)], TMP0,
                                OCS[:, bass.ds(i * (2 * T) + hh * T, T)].bitcast(F32), ALU.subtract).then_inc(lo, 1)
                v.wait_ge(lo, i * 2 + his[0] + hh + 1)
            chain.leave(HEADS_C // 2)
        xts[0] += 4
        his[0] += 4

        with v.Fori(0, KC) as i:
            chain.enter(i, 3)
            m = M[:, bass.ds(i * T, T)]
            t = SC[:, 3 * TS:3 * TS + T]
            for j, p in enumerate((3, 0, 1)):
                v.wait_ge(sg_ready, i * 3 + j + 1)
                v.wait_ge(done[p], i * (1 if p == 3 else 2) + before("merge", p) + (1 if p == 3 else 2))
                sg = SC[:, j * TS:j * TS + T]
                chain(v.tensor_tensor(t if j else m, sg, pair(p), ALU.mult))
                v.sem_inc(free[p], 1)
                if j == 0:
                    v.sem_inc(m_ready, 1)
                else:
                    v.tensor_tensor(m, m, t, ALU.add).then_inc(m_ready, 1)
                    v.wait_ge(m_ready, i * 3 + j + 4)
            chain.leave(KC)

        def block_lo(src, last=None):
            with v.Fori(0, KC) as i:
                v.wait_ge(hi, i + his[0] + 1)
                v.tensor_tensor(H[:, bass.ds(i * T + KC * T, T)], src[:, bass.ds(i * T, T)],
                                H[:, bass.ds(i * T, T)].bitcast(F32), ALU.subtract).then_inc(lo, 1)
            his[0] += KC
            v.wait_ge(lo, his[0])

        block_lo(M)
        v.wait_ge(c_x, 16 * KC)

        def residual(phase, p0, gain=None, other=None, squares=True, extra=None, extra_steps=0):
            if squares:
                chain(v.memset(ACC, 0.0))
            with v.Fori(0, KC // 2) as i:
                if extra_steps:
                    chain.enter(i, extra_steps)
                for s in range(2):
                    x = X[:, bass.ds(i * (2 * T) + s * T, T)]
                    old = other[:, bass.ds(i * (2 * T) + s * T, T)] if other is not None else x
                    v.wait_ge(done[p0 + s], i + before(phase, p0 + s) + 1)
                    if gain is None:
                        ins = v.tensor_tensor(x, pair(p0 + s), old, ALU.add)
                    else:
                        ins = v.scalar_tensor_tensor(out=x, in0=pair(p0 + s), scalar=gain[:, bass.ds(i * 2 + s, 1)],
                                                     in1=old, op0=ALU.mult, op1=ALU.add)
                    ins.then_inc(x_new, 1)
                    v.wait_ge(x_new, i * 2 + before(phase, "xnew") + s + 1)
                    v.sem_inc(free[p0 + s], 1)
                    if squares:
                        v.wait_ge(sq_ready, i * 2 + sqs[0] + s + 1)
                        v.tensor_tensor(ACC, ACC, SQ, ALU.add).then_inc(sq_added, 1)
                        v.wait_ge(sq_added, i * 2 + acs[0] + s + 1)
                    if extra:
                        extra(i, s)
                if extra_steps:
                    chain.leave(KC // 2)
            if squares:
                sqs[0] += KC
                acs[0] += KC
                v.sem_inc(acc_ready, 1)

        residual("out1", 0, other=XIN)
        phase_scale("norm2", D, 1e-6)
        apply_split(H, KC * T, X, KC, T, lambda c: v1("ffn_g", c))

        chain(v.memset(SC[:, 0:2], 0.0))
        f0 = 0
        for n, chunks in enumerate(FF_PASSES):
            up = f"up{n}"
            with v.Fori(0, chunks) as i:
                chain.enter(i, 2)
                conv = SC[:, TS:TS + T]

                def tap(k):
                    return vec[:, bass.ds(i + (VEC[f"conv{k}"] + f0), 1)]

                v.wait_ge(gp_ready, i + f0 + 1)
                chain(v.tensor_scalar(conv, SC[:, 0:T], tap(0), None, ALU.mult))
                chain(v.scalar_tensor_tensor(out=conv, in0=SC[:, 1:1 + T], scalar=tap(1), in1=conv,
                                             op0=ALU.mult, op1=ALU.add))
                v.scalar_tensor_tensor(out=conv, in0=SC[:, 2:2 + T], scalar=tap(2), in1=conv,
                                       op0=ALU.mult, op1=ALU.add).then_inc(cv_ready, 1)
                v.wait_ge(cv_ready, i + f0 + 2)
                v.wait_ge(gl_ready, i + f0 + 1)
                v.wait_ge(done[1], i + before(up, 1) + 1)
                v.tensor_tensor(SC[:, 3 * TS:3 * TS + T], SC[:, 2 * TS:2 * TS + T], pair(1), ALU.mult).then_inc(xt, 1)
                v.wait_ge(xt, i + xts[0] + 1)
                v.sem_inc(free[1], 1)
                v.wait_ge(hi, i + his[0] + 1)
                v.tensor_tensor(FF[:, bass.ds(i * T + KC * T, T)], SC[:, 3 * TS:3 * TS + T],
                                FF[:, bass.ds(i * T, T)].bitcast(F32), ALU.subtract).then_inc(lo, 1)
                v.wait_ge(lo, i + his[0] + 1)
                chain.leave(chunks)
            xts[0] += chunks
            his[0] += chunks
            f0 += chunks
            if n < len(FF_PASSES) - 1:
                residual(f"down{n}", 2, squares=False)
            else:
                v.wait_ge(c_silu, 2)

                def ada(i, s):
                    v.wait_ge(ada_in[s], i * 16 + 16)
                    for j in range(8):
                        tile, row = ((j // 2, (CL, CC)[j % 2]) if j < 4 else (j - 2, CL))
                        chain(v.tensor_tensor_reduce(out=AJ[:, :], in0=AW[:, (s * 6 + tile) * D:(s * 6 + tile + 1) * D],
                                                     in1=row[:, :], scale=1.0, scalar=0.0, op0=ALU.mult, op1=ALU.add,
                                                     accum_out=adac[:, j:j + 1]))
                    both = adac[:, 0:4].rearrange("p (t c) -> p t c", c=2)
                    chain(v.tensor_copy(modb[:, bass.ds(i * 4 + 2 * s, 2)], both[:, :, 0]))
                    chain(v.tensor_copy(modb[:, bass.ds(i * 4 + 2 * s + 16, 2)], both[:, :, 1]))
                    chain(v.tensor_copy(modl[:, bass.ds(i * 8 + 4 * s, 4)], adac[:, 4:8]))
                    v.sem_inc(ada_used, 1)

                residual("down2", 2, extra=ada, extra_steps=22)
        for q in range(2):
            chain(v.tensor_tensor(modb[:, 16 * q:16 * q + 16], modb[:, 16 * q:16 * q + 16],
                                  vec[:, VEC["b_both"]:VEC["b_both"] + 16], ALU.add))
        chain(v.tensor_tensor(modl[:, :], modl[:, :], vec[:, VEC["b_lat"]:VEC["b_lat"] + 32], ALU.add))
        for fac, scale, g in ((fac0, modb[:, 8:16], "norm_g0"), (facc, modb[:, 24:32], "norm_g0"),
                              (fac1, modl[:, 16:24], "norm_g1")):
            chain(v.tensor_scalar(fac[:, :], scale, 1.0, None, ALU.add))
            chain(v.tensor_tensor(fac[:, :], fac[:, :], vec[:, VEC[g]:VEC[g] + 8], ALU.mult))

        phase_scale("fnorm", D, 1e-6)
        for c in range(KC):
            x = X[:, c * T:(c + 1) * T]
            v.scalar_tensor_tensor(out=x, in0=x, scalar=v1("final_g", c), in1=PS[:, 3072:4096],
                                   op0=ALU.mult, op1=ALU.mult).then_inc(x_new, 1)
        v.wait_ge(x_new, before("fnorm", "xnew") + KC)
        v.sem_inc(free[3], 1)
        add_squares(KC)
        phase_scale("norm3", D, 1e-6)
        apply_split(H, KC * T, X, KC, T, lambda c: fac0[:, c:c + 1], lambda c: modb[:, c:c + 1])
        add_squares(KC, CTX)
        v.wait_ge(ctx_in, 16)
        phase_scale("normc", D, 1e-6, CTX)
        apply_split(UC, KC * CTX, CXR, KC, CTX, lambda c: facc[:, c:c + 1], lambda c: modb[:, 16 + c:17 + c])
        v.wait_ge(cs_in, 16)
        v.wait_ge(done[0], before("kvpe", 0) + 2)
        v.tensor_tensor(TPE[:, CTX:TK], pair(0), CST[:, CTX:TK], ALU.mult).then_inc(tpe_ready, 1)
        v.wait_ge(tpe_ready, 1)
        v.sem_inc(free[0], 1)
        v.wait_ge(done[1], before("kvpe", 1) + 2)
        v.tensor_tensor(TPE[:, 0:CTX], pair(1, CTX), CST[:, 0:CTX], ALU.mult).then_inc(tpe_ready, 1)
        v.wait_ge(tpe_ready, 2)
        v.sem_inc(free[1], 1)
        add_squares(2)
        phase_scale("cqnorm", 256, 1e-6)
        apply_split(CQ, 2 * T, CQR, 2, T, lambda c: v1("g_qa", c))
        for phase, a, n in (("ckvnorm", 0, T), ("ckvcnorm", T, CTX)):
            phase_scale(phase, P, 1e-6, n)
            v.scalar_tensor_tensor(out=TMP0[:, 0:n], in0=CKR[:, a:a + n], scalar=v1("g_kva"),
                                   in1=PS[:, 3072:3072 + n], op0=ALU.mult, op1=ALU.mult).then_inc(xt, 1)
            xts[0] += 1
            his[0] += 1
            v.wait_ge(xt, xts[0])
            v.sem_inc(free[3], 1)
            v.wait_ge(hi, his[0])
            v.tensor_tensor(CKV[:, TK + a:TK + a + n], TMP0[:, 0:n], CKV[:, a:a + n].bitcast(F32),
                            ALU.subtract).then_inc(lo, 1)
            v.wait_ge(lo, his[0])

        v.wait_ge(csq_in, 16)
        with v.Fori(0, HEADS // 2) as i:
            chain.enter(i, 2 * 8 * 3)
            for hh in range(2):
                t0 = 8 * hh
                for n, (dst, p, m, at_) in enumerate(((QP, 1, T, 0), (VN, 0, T, 0), (VN, 1, CTX, T))):
                    k = i * 4 + before("heads", p) + 2 * hh + (1 if n == 0 else 2)
                    v.wait_ge(done[p], k)
                    if n == 0:
                        v.tensor_tensor(dst[:, :], pair(p), CSQ[:, :], ALU.mult).then_inc(hd_dve, 1)
                    else:
                        v.tensor_copy(dst[:, at_:at_ + m], pair(p, m)).then_inc(hd_dve, 1)
                    v.wait_ge(hd_dve, i * 6 + 3 * hh + n + 1)
                    v.sem_inc(free[p], 1)

                def peak(t):
                    base = 1536 * (t % 2)
                    v.wait_ge(sc_done, i * 16 + t0 + t + 1)
                    chain(v.tensor_reduce(cols[:, 22 + t % 2:23 + t % 2], PS[:, base:base + TK], AX, ALU.max))
                    v.tensor_scalar(cols[:, 16 + t % 2:17 + t % 2], cols[:, 22 + t % 2:23 + t % 2], -MLA_SCALE, None,
                                    ALU.mult).then_inc(mx_ready, 1)

                def normalise(t):
                    v.wait_ge(ex_ready, i * 16 + t0 + t + 1)
                    chain(v.reciprocal(cols[:, 24 + t % 2:25 + t % 2], cols[:, 18 + t % 2:19 + t % 2]))
                    e = E[:, (t % 2) * TK:(t % 2) * TK + TK]
                    chain(v.tensor_scalar(e, e, cols[:, 24 + t % 2:25 + t % 2], None, ALU.mult))
                    v.sem_inc(e_ready, 1)

                peak(0)
                normalise(0)
                for t in range(QT_N):
                    tg = t0 + t
                    if t + 1 < QT_N:
                        peak(t + 1)
                    v.wait_ge(tpb_done, i * 16 + tg + 1)
                    v.tensor_copy(PT[:, 512:1024], PS[:, 3584:4096]).then_inc(ptb, 1)
                    if t + 1 < QT_N:
                        normalise(t + 1)
                    v.wait_ge(pv_done, i * 16 + tg + 1)
                    g = G[:, bass.ds(i * (2 * T) + (hh * T + t * P), P)]
                    v.tensor_tensor(g, PS[:, 3584:3584 + P], g, ALU.mult).then_inc(pv_free, 1)
            chain.leave(HEADS // 2)
        v.wait_ge(pv_free, 65)
        block_lo(G)
        residual("out2", 0, gain=modl[:, 0:8])
        phase_scale("norm4", D, 1e-6)
        apply_split(H, KC * T, X, KC, T, lambda c: fac1[:, c:c + 1], lambda c: modl[:, 8 + c:9 + c])

        with v.Fori(0, FG) as i:
            chain.enter(i, 4)
            v.wait_ge(zr_ready, i + 1)
            chain(v.tensor_copy(ZEO[:, 0:1], ZR[:, 0:1]))
            chain(v.memset(ZEO[:, HALF:HALF + 1], 0.0))
            back = ZR[:, T - 1:HALF:-1]
            v.tensor_tensor(ZEO[:, 1:HALF], ZR[:, 1:HALF], back, ALU.add).then_inc(ze_ready, 1)
            v.tensor_tensor(ZEO[:, HALF + 1:2 * HALF], ZR[:, 1:HALF], back, ALU.subtract).then_inc(ze_ready, 1)
            v.wait_ge(done[2], i * 2 + before("four", 2) + 1)
            v.tensor_copy(M12[:, HALF:2 * HALF], PS[:, 2560:3072]).then_inc(m_evac, 1)
            v.wait_ge(m_evac, i * 2 + 2)
            v.sem_inc(free[2], 1)
            v.wait_ge(qs_ready, i + 1)
            y = Y[:, bass.ds(i * T, HALF)]
            chain(v.tensor_tensor(y, PS[:, 3072:3584], TMP0[:, 0:HALF], ALU.subtract))
            y = Y[:, bass.ds(i * T + HALF + 1, HALF - 1)]
            v.tensor_tensor(y, PS[:, 3583:3072:-1], TMP0[:, HALF - 1:0:-1], ALU.add).then_inc(y_ready, 1)
            v.wait_ge(y_ready, i * 2 + 2)
            v.sem_inc(free[3], 1)
            v.wait_ge(done[2], i * 2 + before("four", 2) + 2)
            chain(v.tensor_copy(Y[:, bass.ds(i * T + HALF, 1)], PS[:, 2048:2049]))
            v.sem_inc(free[2], 1)
            v.wait_ge(sgf_ready, i + 1)
            y = Y[:, bass.ds(i * T, T)]
            v.tensor_tensor(y, y, TMP1, ALU.mult).then_inc(y_ready, 1)
            v.wait_ge(y_ready, i * 2 + 3)
            chain.leave(FG)
        block_lo(Y)
        residual("out3", 0, gain=modl[:, 24:32])
        phase_scale("final", D, 1e-6)
        for c in range(KC):
            x = X[:, c * T:(c + 1) * T]
            v.scalar_tensor_tensor(out=x, in0=x, scalar=v1("final_g2", c), in1=PS[:, 3072:4096],
                                   op0=ALU.mult, op1=ALU.mult).then_inc(o_ready, 1)

    block_cm.__exit__(None, None, None)


def chunk_cols(w):
    k, n = w.shape
    return w.reshape(k // P, P, n // P, P).transpose(2, 1, 0, 3).reshape(n // P, P, k)


def pad_unit(u):
    return np.concatenate([u, np.zeros((P, UW - u.shape[1]), u.dtype)], axis=1)


def swap_rope(w):
    r1, r2, c1, c2 = np.split(w, 4, axis=1)
    return np.concatenate([w, r2, r1, c2, c1], axis=1)


def weight_units(a):
    units = []
    w_in = a["w_in"][0]
    cu, cv, cx = chunk_cols(w_in[:, 0:256]), chunk_cols(w_in[:, 256:512]), chunk_cols(w_in[:, 512:768])
    units += [cu[0], cu[1], cx[0], cx[1], cv[0], cv[1]]
    q, k, v = (chunk_cols(w_in[:, o:o + 512]) for o in (768, 1280, 1792))
    for h in range(HEADS_C):
        units += [q[h], k[h], v[h]]
    gate = chunk_cols(a["w_gate"][0])
    pa, pb, pc = (chunk_cols(a[n][0]) for n in ("proj_a", "proj_b", "proj_c"))
    for n in range(KC):
        units += [gate[n], gate[8 + n], gate[16 + n], np.concatenate([pa[n], pb[n], pc[n]], axis=1)]
    units += list(chunk_cols(a["w_out"][0]))
    up = chunk_cols(a["w_up"][0])
    down = chunk_cols(a["w_down"][0])
    f = 0
    for chunks in FF_PASSES:
        for j in range(f, f + chunks):
            units += [up[j], up[FFC + j]]
        units += [pad_unit(down[n][:, f * P:(f + chunks) * P]) for n in range(KC)]
        f += chunks
    m = a["mla_w_in_2"][0]
    units += [chunk_cols(m[:, 256:384])[0], chunk_cols(swap_rope(m[:, 384:448]))[0]]
    units += list(chunk_cols(m[:, 0:256]))
    units += list(chunk_cols(m[:, 448:]))
    wq, wkv = a["mla_w_qup_2"][0], a["mla_w_kvup_2"][0]
    for h in range(HEADS):
        qh = wq[:, h * 192:(h + 1) * 192]
        kv = chunk_cols(wkv[:, h * 256:(h + 1) * 256])
        units.append(pad_unit(np.concatenate(
            [chunk_cols(qh[:, 0:128])[0], chunk_cols(swap_rope(qh[:, 128:192]))[0], kv[0], kv[1]], axis=1)))
    units += list(chunk_cols(a["mla_w_out_2"][0]))
    fno = chunk_cols(a["fno_w_in_2"][0])
    for g in range(FG):
        units += [fno[g], fno[FG + g]]
    units += list(chunk_cols(a["fno_w_out_2"][0]))
    return np.ascontiguousarray(np.stack(units))


def feature_cols(x):
    return x.reshape(-1, P).T


def bucket_rows():
    n = np.arange(GROW)
    rel = (T - 1) - n
    pos = np.maximum(rel, 0)
    f = np.maximum(pos, 1).astype(np.float32)
    large = 16 + (np.log(f / np.float32(16)) / np.float32(math.log(8.0)) * np.float32(16)).astype(np.int32)
    bucket = np.where(pos < 16, pos, np.minimum(large, 31))
    rows = np.zeros((33, GROW), np.float32)
    rows[bucket, n] = 1.0
    rows[32] = np.where(rel < 0, np.float32(-1e30), 0.0)
    return rows


def rope_table():
    inv = (1.0 / (10000.0 ** (np.arange(0, 32, 2, dtype=np.float32) / np.float32(32)))).astype(np.float32)
    t = np.arange(T)
    row, col = (t // 64).astype(np.float32), (t % 64).astype(np.float32)
    ar, ac = inv[:, None] * row[None], inv[:, None] * col[None]
    cos = np.concatenate([np.cos(ar), np.cos(ar), np.cos(ac), np.cos(ac)])
    sin = np.concatenate([-np.sin(ar), np.sin(ar), -np.sin(ac), np.sin(ac)])
    lat = np.concatenate([cos, sin]).astype(np.float32)
    ctx = np.concatenate([np.ones((64, CTX)), np.zeros((64, CTX))]).astype(np.float32)
    return np.concatenate([ctx, lat], axis=1)


def dft_tables():
    t = np.arange(HALF)
    ang = 2 * np.pi * ((t[:, None] * t[None]) % T) / T
    tab = [f(ang).astype(np.float32).reshape(4, P, HALF).transpose(1, 0, 2).reshape(P, 4 * HALF)
           for f in (np.cos, np.sin)]
    d = np.arange(P)
    ang = 2 * np.pi * ((d[:, None] * d[None]) % P) / P
    norm = 1.0 / math.sqrt(T * P)
    csd = np.concatenate([np.cos(ang) * norm, np.sin(ang) * norm], axis=1).astype(np.float32)
    return tab[0], tab[1], csd


def arrays_of(a):
    c = np.ascontiguousarray
    vecs = {
        "attn_g": feature_cols(a["attn_norm_g"]), "b_gate": feature_cols(a["b_gate"]),
        "pool_scale": feature_cols(a["pool_scale"]), "subln": feature_cols(a["diff_subln_g"]),
        "ffn_g": feature_cols(a["ffn_norm_g"]), "conv0": feature_cols(a["conv_w"][0, 0]),
        "conv1": feature_cols(a["conv_w"][0, 1]), "conv2": feature_cols(a["conv_w"][0, 2]),
        "conv_b": feature_cols(a["conv_b"]), "final_g": feature_cols(a["final_norm_g"]),
        "norm_g0": feature_cols(a["norm_g_2"][0]), "norm_g1": feature_cols(a["norm_g_2"][1]),
        "b_both": feature_cols(a["b_ada_2"][0][:2048]),
        "b_lat": feature_cols(np.concatenate([a["b_ada_2"][0][2048:], a["b_ada_2"][1]])),
        "g_qa": feature_cols(a["mla_g_qa_2"]), "g_kva": feature_cols(a["mla_g_kva_2"]),
        "final_g2": feature_cols(a["final_g_2"]),
        "alt": np.where(np.arange(P) % 2, -1.0, 1.0).astype(np.float32)[:, None],
        "pool_inv": np.stack([np.repeat([1 / 2, 1 / 4], 64), np.repeat([1 / 8, 1 / 16], 64)], 1).astype(np.float32),
    }
    edge = np.zeros((P, 32), np.float32)
    t = np.arange(16)
    for g, win in enumerate((2, 4, 8, 16)):
        edge[64 * (g % 2):64 * (g % 2) + 64, 16 * (g // 2):16 * (g // 2) + 16] = 1.0 / np.minimum(t + 1, win)
    ada0 = chunk_rows(a["w_ada_2"][0])
    ada1 = chunk_rows(a["w_ada_2"][1])
    both, lat = ada0[:16], np.concatenate([ada0[16:], ada1])
    ada = np.stack([np.concatenate([both[2 * n:2 * n + 2], lat[4 * n:4 * n + 4]]) for n in range(8)])
    ada = ada.transpose(0, 2, 1, 3).reshape(8, P, 6 * D)
    ctab, stab, csd = dft_tables()
    half = np.eye(64, dtype=np.float32)
    return {
        "x": c(a["x"][0].T.reshape(KC, P, T)),
        "ctx": c(a["ctx_2"][0].T.reshape(KC, P, CTX).transpose(1, 0, 2).reshape(P, KC * CTX)),
        "units": weight_units(a),
        "vec": c(np.concatenate([vecs[n] for n, _ in VEC_PARTS], axis=1)),
        "onehot": bucket_rows(), "rel_bias": c(a["rel_bias"]),
        "ident": np.eye(P, dtype=np.float32),
        "dup": np.block([[half, half], [half, half]]),
        "ln_g": c(a["sgu_ln_g"][0]), "ln_b": c(a["sgu_ln_b"][0]),
        "wst": c(a["sgu_w"][0].transpose(2, 0, 1).reshape(P, 4 * P)),
        "tri": np.triu(np.ones((P, P), np.float32)),
        "sgu_b": c(a["sgu_b"][0]), "pool_w": c(a["pool_w"][0]), "edge": edge,
        "lam": c(a["diff_lam"][0].reshape(256)),
        "c": c(a["c_2"][0]), "c_ctx": c(a["c_ctx_2"]),
        "ada": c(ada),
        "cs": rope_table(), "ctab": ctab, "stab": stab, "csd": csd,
        "altrow": np.where(np.arange(HALF) % 2, -1.0, 1.0).astype(np.float32)[None],
    }


def chunk_rows(w):
    k, n = w.shape
    return w.T.reshape(n // P, P, k)


def kernel(**inputs):
    import concourse.bacc as bacc
    from concourse.bass_utils import run_bass_kernel_spmd as run

    nc = bacc.Bacc("TRN2", target_bir_lowering=False, num_devices=1)
    arrays = arrays_of({k: np.asarray(v) for k, v in inputs.items()})
    t_in = {k: nc.dram_tensor("in_" + k, v.shape, F32, kind="ExternalInput").ap() for k, v in arrays.items()}
    out = nc.dram_tensor("out", (KC, P, T), F32, kind="ExternalOutput").ap()
    build(nc, t_in, out)
    r = run(nc, [{"in_" + k: v for k, v in arrays.items()}], core_ids=[0])
    return r.results[0]["out"].reshape(D, T).T.reshape(1, T, D)
```

```python
import math

import numpy as np

import concourse.bass as bass
from concourse import mybir

F32 = mybir.dt.float32
F32R = mybir.dt.float32r
ALU = mybir.AluOpType
ACT = mybir.ActivationFunctionType
AX = mybir.AxisListType.X

P = 128
T = 1024
D = 1024
KC = D // P
UW = KC * P
CTX = 256
TK = CTX + T
HEADS_C = 4
HEADS = 8
QT_N = T // P
FFC = 22
FF_PASSES = [8, 8, 6]
FG = 8
HALF = T // 2
GROW = T + P
LAM_INIT = 0.8 - 0.6 * math.exp(0.0)
MLA_SCALE = 1.0 / math.sqrt(192.0)

VEC_PARTS = [("attn_g", 8), ("b_gate", 24), ("pool_scale", 2), ("subln", 1), ("ffn_g", 8), ("conv0", 22),
             ("conv1", 22), ("conv2", 22), ("conv_b", 22), ("final_g", 8), ("norm_g0", 8), ("norm_g1", 8),
             ("b_both", 16), ("b_lat", 32), ("g_qa", 2), ("g_kva", 1), ("final_g2", 8), ("alt", 1),
             ("pool_inv", 2)]
VEC = {}
_at = 0
for _name, _n in VEC_PARTS:
    VEC[_name] = _at
    _at += _n
NVEC = _at

NORM = {2: 1, 3: 1, "norm": 1}
PHASES = [
    ("bias", {0: 4, 1: 4}),
    ("norm1", {**NORM, "split": 8, "square": 8}),
    ("ux", {0: 2, 1: 2, "unit": 4}),
    ("va", {2: 2, 3: 2, "unit": 2}),
    ("gmlp", {2: 1, 3: 1, "split": 2}),
    ("pool", {2: 1, 3: 1, "split": 2}),
    ("diff", {0: 10 * 4, 1: 10 * 4, 2: 9 * 4, 3: 9 * 4, "unit": 12, "split": 4, "norm": 4}),
    ("merge", {0: 16, 1: 16, 2: 8, 3: 8, "unit": 32}),
    ("msplit", {"split": 8}),
    ("out1", {0: 4, 1: 4, "unit": 8, "xnew": 8, "square": 8}),
    ("norm2", {**NORM, "split": 8}),
    ("up0", {0: 8, 1: 8, "unit": 16, "split": 8}),
    ("down0", {2: 4, 3: 4, "unit": 8, "xnew": 8}),
    ("up1", {0: 8, 1: 8, "unit": 16, "split": 8}),
    ("down1", {2: 4, 3: 4, "unit": 8, "xnew": 8}),
    ("up2", {0: 6, 1: 6, "unit": 12, "split": 6}),
    ("down2", {2: 4, 3: 4, "unit": 8, "xnew": 8, "square": 8}),
    ("fnorm", {**NORM, "xnew": 8}),
    ("norm3", {**NORM, "split": 8, "square": 8}),
    ("normc", {**NORM, "split": 8, "square": 8}),
    ("kvpe", {0: 2, 1: 2, 2: 1, 3: 1, "unit": 2}),
    ("cq", {0: 1, 1: 1, "unit": 2}),
    ("cqnorm", {**NORM, "split": 2, "square": 2}),
    ("ckvnorm", {**NORM, "split": 1}),
    ("ckvcnorm", {**NORM, "split": 1}),
    ("mgate", {0: 4, 1: 4, "unit": 8}),
    ("heads", {"unit": 8}),
    ("osplit", {"split": 8}),
    ("out2", {0: 4, 1: 4, "unit": 8, "xnew": 8, "square": 8}),
    ("norm4", {**NORM, "split": 8}),
    ("four", {0: 8, 1: 8, 2: 16, 3: 16, "unit": 16}),
    ("ysplit", {"split": 8}),
    ("out3", {0: 4, 1: 4, "unit": 8, "xnew": 8, "square": 8}),
    ("final", {**NORM}),
]


def before(phase, what):
    total = 0
    for name, adds in PHASES:
        if name == phase:
            return total
        total += adds.get(what, 0)
    raise KeyError(phase)


NUNITS = sum(adds.get("unit", 0) for _, adds in PHASES)


class Chain:

    def __init__(self, eng, sem):
        self.eng, self.sem, self.n, self.off = eng, sem, 0, None

    def __call__(self, ins):
        ins.then_inc(self.sem, 1)
        self.n += 1
        self.eng.wait_ge(self.sem, self.n if self.off is None else self.off + self.n)

    def enter(self, i, per):
        self.off, self.per, self.start = i * per, per, self.n

    def leave(self, count):
        assert self.n - self.start == self.per, (self.n - self.start, self.per)
        self.n = self.start + self.per * count
        self.off = None


def build(nc, t_in, out):
    H_AT = 16512
    F_AT = H_AT + 65536
    X_AT = F_AT + 65536
    W_AT = X_AT + 32768
    T_AT = W_AT + 8192 + 16384
    TS = 1040
    C_AT = T_AT + 4 * TS * 4

    def at(name, cols, where, dt=F32, parts=P):
        return nc.alloc_sbuf_tensor_at(name, [parts, cols], dt, offset=where)

    H = at("H", 2 * KC * T, H_AT, F32R)
    w_raw = at("w_raw", 2 * UW, W_AT)
    w_hl = at("w_hl", 2 * 2 * UW, W_AT + 8192, F32R)
    SC = at("SC", 4 * TS, T_AT)
    ACC, SQ, TMP0, TMP1 = (SC[:, s * TS:s * TS + T] for s in range(4))
    TMP = [TMP0, TMP1]
    DIAG = SQ
    X = at("X", KC * T, X_AT)

    place = [C_AT]

    def small(name, cols, dt=F32):
        t = at(name, cols, place[0], dt)
        place[0] += (cols * 4 + 31) // 32 * 32
        return t

    ident = small("ident", P)
    ones = small("ones", P)
    dup = small("dup", P)
    vec = small("vec", NVEC)
    lngb = small("lngb", 512)
    cols = small("cols", 64)
    modb = small("modb", 32)
    modl = small("modl", 32)
    fac0 = small("fac0", 8)
    facc = small("facc", 8)
    fac1 = small("fac1", 8)
    adac = small("adac", 16)
    bn = small("bn", 6)
    lv = small("lv", 256)
    lvp = small("lvp", 64)
    stat = small("stat", 8)
    assert place[0] <= nc.sbuf_usable_end, place[0]

    def v1(name, j=0):
        return vec[:, VEC[name] + j:VEC[name] + j + 1]

    YA = at("YA", 2 * 2 * T, F_AT, F32R)
    YB = at("YB", 2 * 2 * T, F_AT + 16384, F32R)
    OCS = at("OCS", 2 * 4 * T, F_AT + 32768, F32R)
    onehot = at("onehot", GROW, F_AT)
    rb = at("rb", HEADS_C, F_AT + 4608)
    rbx = at("rbx", HEADS_C * P, F_AT + 4640)
    grow = at("grow", GROW, F_AT + 8192)
    U = at("U", 2 * T, F_AT + 32768)
    VA = at("VA", QT_N * 256, F_AT + 40960)
    PADX = T + 16
    XB = at("XB", 2 * PADX, F_AT + 49152)
    WST = at("WST", 4 * P, F_AT + 57472)
    SGB = at("SGB", 2 * P, F_AT + 59520)
    BD = at("BD", 2 * P, F_AT + 60544)
    EDGE = at("EDGE", 32, F_AT + 61568)
    TRI = at("TRI", P, F_AT + 61728)
    PA = SC[:, 0:2 * PADX]
    PB = at("PB", 2 * PADX, X_AT)
    SA = [at("SA0", T, X_AT), at("SA1", T, X_AT + 4096)]
    SB = [at("SB0", T, X_AT + 8192), ACC]
    AT = at("AT", T, X_AT + 12288)
    QT = at("QT", T, X_AT + 16384)
    KT = at("KT", T, X_AT + 20480)
    VC = at("VC", T, X_AT + 24576)
    BR = at("BR", T, X_AT + 28672)
    OC = TMP1
    M = at("M", KC * T, X_AT)
    XIN = at("XIN", KC * T, F_AT)
    FF = at("FF", 2 * KC * T, F_AT, F32R)
    CL = at("CL", D, H_AT)
    CC = at("CC", D, H_AT + 4096)
    AJ = at("AJ", D, H_AT + 8192)
    AW = at("AW", 12 * D, H_AT + 12288)
    UC = at("UC", 2 * KC * CTX, F_AT, F32R)
    CST = at("CST", TK, F_AT + 16384)
    CKR = at("CKR", TK, F_AT + 21504)
    TPE = at("TPE", TK, F_AT + 26624)
    CXR = at("CXR", KC * CTX, F_AT + 32768)
    CQR = at("CQR", 2 * T, F_AT + 49152)
    G = at("G", KC * T, F_AT)
    CQ = at("CQ", 2 * 2 * T, F_AT + 32768, F32R)
    CKV = at("CKV", 2 * TK, F_AT + 49152, F32R)
    KPR = at("KPR", TK, F_AT + 59392)
    QN = at("QN", 2 * T, H_AT, F32R)
    QP = at("QP", 2 * T, H_AT + 8192, F32R)
    KN = at("KN", 2 * TK, H_AT + 16384, F32R)
    KPE = at("KPE", 2 * TK, H_AT + 26624, F32R)
    VN = at("VN", 2 * TK, H_AT + 36864)
    E = at("E", 2 * TK, H_AT + 47104)
    PT = at("PT", TK, H_AT + 57344)
    CSQ = TMP1
    Y = at("Y", KC * T, F_AT)
    CTAB = at("CTAB", 4 * HALF, F_AT + 32768)
    STAB = at("STAB", 4 * HALF, F_AT + 40960)
    CSD = at("CSD", 2 * P, F_AT + 49152)
    M12 = at("M12", 2 * HALF, F_AT + 50176)
    ZEO = at("ZEO", 2 * HALF, F_AT + 54272)
    ZR = at("ZR", T, F_AT + 58368)
    MR = at("MR", P, F_AT + 62464)
    ALT = at("ALT", HALF, F_AT + 62976)

    PS = nc.alloc_psum_tensor("PS", [P, 4096], F32)
    scratch = nc.dram_tensor("bias_scratch", (HEADS_C, P * GROW), F32).ap()
    shifted = bass.AP(scratch.tensor, P - 1, [[P * GROW, HEADS_C], [GROW - 1, P], [1, T]])

    def pair(p, n=T, start=0):
        return PS[:, p * 1024 + start:p * 1024 + start + n]

    sem = nc.alloc_semaphore
    w_in = [sem("w_in0"), sem("w_in1")]
    w_hi = sem("w_hi")
    w_split = sem("w_split")
    w_seen, sc_seen = sem("w_seen"), sem("sc_seen")
    w_used = sem("w_used")
    done = [sem(f"done{p}") for p in range(4)]
    free = [sem(f"free{p}") for p in range(4)]
    hi = sem("hi")
    lo = sem("lo")
    xt = sem("xt")
    sq_added = sem("sq_added")
    acc_ready = sem("acc_ready")
    ms_ready = sem("ms_ready")
    sd_ready = sem("sd_ready")
    diag_ready = sem("diag_ready")
    x_new = sem("x_new")
    sq_ready = sem("sq_ready")
    s_dve, s_act, s_pe = sem("s_dve"), sem("s_act"), sem("s_pe")
    c_early, c_gm, c_x = sem("c_early"), sem("c_gm"), sem("c_x")
    x_in = [sem(f"x_in{c}") for c in range(KC)]
    memset_done = sem("memset_done")
    g_row = sem("g_row")
    g_out = sem("g_out")
    br_in = sem("br_in")
    rbx_ready = sem("rbx_ready")
    u_ready, xb_ready, va_ready = sem("u_ready"), sem("xb_ready"), sem("va_ready")
    va_ms, va_sd = sem("va_ms"), sem("va_sd")
    va_norm, wst_ready, p_ready = sem("va_norm"), sem("wst_ready"), sem("p_ready")
    qkv_ready = sem("qkv_ready")
    neg_ready, exp_ready, aa_ready, at_ready, oc_ready = (
        sem(n) for n in ("neg_ready", "exp_ready", "aa_ready", "at_ready", "oc_ready"))
    lam_sum, lam_exp = sem("lam_sum"), sem("lam_exp")
    sg_ready, m_ready = sem("sg_ready"), sem("m_ready")
    gp_ready, cv_ready, gl_ready = sem("gp_ready"), sem("cv_ready"), sem("gl_ready")
    ada_in = [sem("ada_in0"), sem("ada_in1")]
    ada_used = sem("ada_used")
    c_rows, c_silu = sem("c_rows"), sem("c_silu")
    ctx_in, cs_in, csq_in, ft_in = sem("ctx_in"), sem("cs_in"), sem("csq_in"), sem("ft_in")
    csq_free = sem("csq_free")
    ckr_ready, tpe_ready, kpe_ready, cqr_ready = (
        sem(n) for n in ("ckr_ready", "tpe_ready", "kpe_ready", "cqr_ready"))
    kpe_hi, kpe_lo = sem("kpe_hi"), sem("kpe_lo")
    hp_done = sem("hp_done")
    hq_hi, hq_lo = sem("hq_hi"), sem("hq_lo")
    qp_ready, vn_act, vn_dve = sem("qp_ready"), sem("vn_act"), sem("vn_dve")
    sc_done, mx_ready, ex_ready, e_ready = (
        sem(n) for n in ("sc_done", "mx_ready", "ex_ready", "e_ready"))
    tpa_done, tpb_done, pta, ptb = (sem(n) for n in ("tpa_done", "tpb_done", "pta", "ptb"))
    pv_done, pv_free = sem("pv_done"), sem("pv_free")
    zr_ready, ze_ready, m_evac, mr_ready, qs_ready, sgf_ready, y_ready = (
        sem(n) for n in ("zr_ready", "ze_ready", "m_evac", "mr_ready", "qs_ready", "sgf_ready", "y_ready"))
    gate_ready = sem("gate_ready")
    o_ready, o_out = sem("o_ready"), sem("o_out")

    block_cm = nc.Block()
    block = block_cm.__enter__()

    @block.sync
    def _(sp):
        sp.dma_start(onehot[0:33, :], t_in["onehot"]).then_inc(c_early, 16)
        sp.dma_start(rb[0:32, :], t_in["rel_bias"]).then_inc(c_early, 16)
        sp.dma_start(ident[:, :], t_in["ident"]).then_inc(c_early, 16)
        sp.dma_start(vec[:, :], t_in["vec"]).then_inc(c_early, 16)
        for c in range(KC):
            sp.dma_start(X[:, c * T:(c + 1) * T], t_in["x"][c]).then_inc(x_in[c], 16)
        sp.dma_start(lngb[:, 0:256], t_in["ln_g"].partition_broadcast(P)).then_inc(c_gm, 16)
        sp.dma_start(lngb[:, 256:512], t_in["ln_b"].partition_broadcast(P)).then_inc(c_gm, 16)
        sp.dma_start(WST[:, :], t_in["wst"]).then_inc(c_gm, 16)
        sp.dma_start(TRI[:, :], t_in["tri"]).then_inc(c_gm, 16)
        for g in range(4):
            half = slice(64 * (g % 2), 64 * (g % 2) + 64)
            sp.dma_start(SGB[half, (g // 2) * P:(g // 2 + 1) * P],
                         t_in["sgu_b"][g].partition_broadcast(64)).then_inc(c_gm, 16)
        sp.wait_ge(memset_done, 1)
        for g in range(4):
            half = slice(64 * (g % 2), 64 * (g % 2) + 64)
            sp.dma_start(BD[half, (g // 2) * P + 64 * (g % 2):(g // 2) * P + 64 * (g % 2) + 64],
                         t_in["pool_w"][g]).then_inc(c_gm, 16)
        sp.dma_start(EDGE[:, :], t_in["edge"]).then_inc(c_gm, 16)
        sp.dma_start(lv[:, :], t_in["lam"].partition_broadcast(P)).then_inc(c_gm, 16)
        sp.dma_start(dup[:, :], t_in["dup"]).then_inc(c_gm, 16)
        for u in range(2):
            sp.dma_start(w_raw[:, u * UW:(u + 1) * UW], t_in["units"][u]).then_inc(w_in[u], 16)
        with sp.Fori(1, NUNITS // 2) as i:
            for s in range(2):
                sp.wait_ge(w_split, 2 * i + (s - 1))
                sp.dma_start(w_raw[:, s * UW:(s + 1) * UW],
                             t_in["units"][bass.ds(2 * i + s, 1)].rearrange("o p n -> p (o n)")
                             ).then_inc(w_in[s], 16)

    @block.gpsimd
    def _(pool):
        def split_unit(s, number):
            pool.wait_ge(w_in[s], 16 * (number // 2 + 1) if isinstance(number, int) else number)
            hi_part = w_hl[:, s * 2 * UW:s * 2 * UW + UW]
            raw = w_raw[:, s * UW:(s + 1) * UW]
            return hi_part, w_hl[:, s * 2 * UW + UW:(s + 1) * 2 * UW], raw

        for s in range(2):
            hi_part, lo_part, raw = split_unit(s, s)
            pool.tensor_copy(hi_part, raw).then_inc(w_hi, 1)
            pool.wait_ge(w_hi, s + 1)
            pool.tensor_tensor(lo_part, raw, hi_part.bitcast(F32), ALU.subtract).then_inc(w_split, 1)
        with pool.Fori(1, NUNITS // 2) as i:
            for s in range(2):
                pool.wait_ge(w_used, 2 * i + (s - 1))
                hi_part, lo_part, raw = split_unit(s, 16 * i + 16)
                pool.sem_inc(w_seen, 1)
                pool.tensor_copy(hi_part, raw).then_inc(w_hi, 1)
                pool.wait_ge(w_hi, 2 * i + (s + 1))
                pool.tensor_tensor(lo_part, raw, hi_part.bitcast(F32), ALU.subtract).then_inc(w_split, 1)

    @block.tensor
    def _(pe):
        def w(s, part, k):
            return w_hl[:, (2 * s + part) * UW + k * P:(2 * s + part) * UW + (k + 1) * P]

        PASSES = ((0, 0), (0, 1), (1, 0))

        def feature_major(s, src, src_cols, src_chunk, ks, out_at, n=T, w0=0, opens=True, ready=None):
            for k in range(ks):
                if ready is not None:
                    pe.wait_ge(lo, ready + k + 1)
                for wp, xp in PASSES:
                    for a in range(0, n, 512):
                        m = min(512, n - a)
                        o = xp * src_cols + src_chunk * k + a
                        mm = pe.matmul(PS[:, out_at + a:out_at + a + m], w(s, wp, w0 + k), src[:, o:o + m],
                                       start=(k == 0 and wp == 0 and xp == 0), stop=(k == ks - 1 and wp == 1))
                        if opens:
                            mm.then_inc(w_used, 1)
                            opens = False
            return mm

        def token_major(s, src, src_cols, src_chunk, ks, out_at, tiles, w0=0, first=0):
            for i in range(tiles):
                for k in range(ks):
                    for n, (xp, wp) in enumerate(PASSES):
                        o = xp * src_cols + src_chunk * k + (first + i) * P
                        mm = pe.matmul(PS[:, out_at + i * P:out_at + (i + 1) * P], src[:, o:o + P],
                                       w(s, wp, w0 + k), start=(k == 0 and n == 0), stop=(k == ks - 1 and n == 2))
            return mm

        def take(p, number):
            pe.wait_ge(free[p], number + 1)

        def norm(idx, p2, p3, n=T):
            pe.wait_ge(acc_ready, idx + 1)
            take(2, p2)
            for j in range(n // P):
                mm = pe.matmul(PS[:, 2048 + j:2049 + j], ACC[:, j * P:(j + 1) * P], ones[:, 0:1],
                               start=True, stop=True)
            mm.then_inc(done[2], 1)
            pe.wait_ge(diag_ready, idx + 1)
            take(3, p3)
            for a in range(0, n, 512):
                m = min(512, n - a)
                mm = pe.matmul(PS[:, 3072 + a:3072 + a + m], ones[:, :], DIAG[:, a:a + m], start=True, stop=True)
            mm.then_inc(done[3], 1)

        def phase_norm(phase, n=T):
            norm(before(phase, "norm"), before(phase, 2), before(phase, 3), n)

        def b(phase, p):
            return before(phase, p)

        pe.wait_ge(rbx_ready, 1)
        for h in range(HEADS_C):
            take(0, h)
            take(1, h)
            for a in range(0, GROW, 512):
                m = min(512, GROW - a)
                mm = pe.matmul(PS[:, a:a + m], rbx[0:33, h * P:(h + 1) * P], onehot[0:33, a:a + m],
                               start=True, stop=True)
                if a == 512:
                    mm.then_inc(done[0], 1)
            mm.then_inc(done[1], 1)

        phase_norm("norm1")

        unit = 0
        for j in range(4):
            take(j % 2, b("ux", j % 2) + j // 2)
            pe.wait_ge(w_split, unit + 1)
            feature_major(unit % 2, H, KC * T, T, KC, (j % 2) * 1024, opens=unit > 0,
                          ready=None if j else 0).then_inc(done[j % 2], 1)
            unit += 1
        for j in range(2):
            take(2 + j, b("va", 2 + j))
            pe.wait_ge(w_split, unit + 1)
            feature_major(unit % 2, H, KC * T, T, KC, 2048 + j * 1024).then_inc(done[2 + j], 1)
            unit += 1
        for j in range(2):
            take(2 + j, b("va", 2 + j) + 1)
            for i in range(QT_N):
                mm = pe.transpose(PS[:, 2048 + j * 1024 + i * P:2048 + j * 1024 + (i + 1) * P],
                                  TMP[j][:, i * P:(i + 1) * P], ident[:, :])
            mm.then_inc(done[2 + j], 1)
        pe.wait_ge(wst_ready, 1)
        pe.wait_ge(va_norm, QT_N)
        for j in range(2):
            take(2 + j, b("gmlp", 2 + j))
            for i in range(QT_N):
                for g in range(2):
                    mm = pe.matmul(PS[64 * g:64 * g + 64, 2048 + j * 1024 + i * P:2048 + j * 1024 + (i + 1) * P],
                                   VA[:, i * 256 + (2 * j + g) * 64:i * 256 + (2 * j + g) * 64 + 64],
                                   WST[:, (2 * j + g) * P:(2 * j + g + 1) * P], start=True, stop=True)
            mm.then_inc(done[2 + j], 1)
        pe.wait_ge(c_gm, 16 * 15)
        for j in range(2):
            pe.wait_ge(p_ready, j + 1)
            take(2 + j, b("pool", 2 + j))
            for a in (0, 512):
                mm = pe.matmul(PS[:, 2048 + j * 1024 + a:2048 + j * 1024 + a + 512], BD[:, j * P:(j + 1) * P],
                               XB[:, j * PADX + 16 + a:j * PADX + 16 + a + 512], start=True, stop=True)
            mm.then_inc(done[2 + j], 1)

        with pe.Fori(0, HEADS_C // 2) as i:
            for hh in range(2):
                u0 = before("diff", "unit") + 3 * hh
                n0, n1, n2, n3 = (b("diff", p) + k * hh for p, k in ((0, 10), (1, 10), (2, 9), (3, 9)))

                def val(x, per):
                    return i * (2 * per) + x

                for n, p in enumerate((0, 1, 0)):
                    take(p, val((n0, n1, n0 + 1)[n], 10))
                    pe.wait_ge(w_split, val(u0 + n + 1, 3))
                    feature_major((u0 + n) % 2, H, KC * T, T, KC, p * 1024).then_inc(done[p], 1)

                def scores(t):
                    n = (t + 1) * P
                    for c in range(2):
                        take(2 + c, val((n2, n3)[c] + t, 9))
                        for a in range(0, n, 512):
                            m = min(512, n - a)
                            mm = pe.matmul(PS[:, (2 + c) * 1024 + a:(2 + c) * 1024 + a + m],
                                           QT[64 * c:64 * c + 64, t * P:(t + 1) * P],
                                           KT[64 * c:64 * c + 64, a:a + m], start=True, stop=True)
                        mm.then_inc(done[2 + c], 1)

                pe.wait_ge(qkv_ready, val(4 * hh + 2, 4))
                scores(0)
                pe.wait_ge(qkv_ready, val(4 * hh + 3, 4))
                take(1, val(n1 + 1, 10))
                for kb in range(QT_N):
                    mm = pe.transpose(PS[:, 1024 + kb * P:1024 + (kb + 1) * P], TMP0[:, kb * P:(kb + 1) * P],
                                      ident[:, :])
                mm.then_inc(done[1], 1)
                scores(1)
                for t in range(QT_N):
                    pe.wait_ge(aa_ready, val(8 * hh + t + 1, 8))
                    take(0, val(n0 + 2 + t, 10))
                    for kb in range(t + 1):
                        mm = pe.transpose(PS[:, kb * P:(kb + 1) * P], SA[t % 2][:, kb * P:(kb + 1) * P], ident[:, :])
                    mm.then_inc(done[0], 1)
                    if t + 2 < QT_N:
                        scores(t + 2)
                    if t == 0:
                        pe.wait_ge(qkv_ready, val(4 * hh + 4, 4))
                    pe.wait_ge(at_ready, val(8 * hh + t + 1, 8))
                    take(1, val(n1 + 2 + t, 10))
                    for kb in range(t + 1):
                        mm = pe.matmul(PS[:, 1024:1024 + P], VC[:, kb * P:(kb + 1) * P], AT[:, kb * P:(kb + 1) * P],
                                       start=(kb == 0), stop=(kb == t))
                    mm.then_inc(done[1], 1)
                norm(val(before("diff", "norm") + hh, 1), val(n2 + 8, 9), val(n3 + 8, 9))

        pe.wait_ge(lo, before("merge", "split"))
        with pe.Fori(0, KC) as i:
            u0 = before("merge", "unit")
            for j in range(3):
                take(j, i * (2 if j < 2 else 1) + b("merge", j))
                pe.wait_ge(w_split, i * 4 + u0 + j + 1)
                feature_major((u0 + j) % 2, H, KC * T, T, KC, j * 1024).then_inc(done[j], 1)
            pe.wait_ge(w_split, i * 4 + u0 + 4)
            s = (u0 + 3) % 2
            take(3, i + b("merge", 3))
            feature_major(s, YA, 2 * T, T, 2, 3072, w0=0).then_inc(done[3], 1)
            take(0, i * 2 + b("merge", 0) + 1)
            feature_major(s, YB, 2 * T, T, 2, 0, w0=2, opens=False).then_inc(done[0], 1)
            take(1, i * 2 + b("merge", 1) + 1)
            feature_major(s, OCS, 4 * T, T, 4, 1024, w0=4, opens=False).then_inc(done[1], 1)

        def project(phase, p0, src, ks, split_base):
            u0 = before(phase, "unit")
            with pe.Fori(0, KC // 2) as i:
                for s in range(2):
                    take(p0 + s, i + b(phase, p0 + s))
                    pe.wait_ge(w_split, i * 2 + u0 + s + 1)
                    feature_major((u0 + s) % 2, src, KC * T, T, ks, (p0 + s) * 1024,
                                  ready=None if s else split_base - ks).then_inc(done[p0 + s], 1)

        project("out1", 0, H, KC, before("out1", "split"))
        phase_norm("norm2")
        for n, chunks in enumerate(FF_PASSES):
            up, down = f"up{n}", f"down{n}"
            with pe.Fori(0, chunks) as i:
                u0 = before(up, "unit")
                for s in range(2):
                    take(s, i + b(up, s))
                    pe.wait_ge(w_split, i * 2 + u0 + s + 1)
                    feature_major((u0 + s) % 2, H, KC * T, T, KC, s * 1024,
                                  ready=None if s or n else before("norm2", "split")).then_inc(done[s], 1)
            project(down, 2, FF, chunks, before(down, "split"))
        phase_norm("fnorm")
        phase_norm("norm3")
        phase_norm("normc", CTX)

        pe.wait_ge(lo, before("kvpe", "split"))
        for j in range(2):
            u = before("kvpe", "unit") + j
            take(0, b("kvpe", 0) + j)
            pe.wait_ge(w_split, u + 1)
            feature_major(u % 2, H, KC * T, T, KC, 0).then_inc(done[0], 1)
            take(1, b("kvpe", 1) + j)
            feature_major(u % 2, UC, KC * CTX, CTX, KC, 1024, n=CTX, opens=False).then_inc(done[1], 1)
        for j in range(2):
            u = before("cq", "unit") + j
            take(j, b("cq", j))
            pe.wait_ge(w_split, u + 1)
            feature_major(u % 2, H, KC * T, T, KC, j * 1024).then_inc(done[j], 1)
        pe.wait_ge(tpe_ready, 2)
        take(2, b("kvpe", 2))
        for a in (0, 512):
            mm = pe.matmul(PS[:, 2048 + a:2560 + a], dup[:, :], TPE[:, CTX + a:CTX + a + 512], start=True, stop=True)
        mm.then_inc(done[2], 1)
        take(3, b("kvpe", 3))
        pe.matmul(PS[:, 3072:3072 + CTX], dup[:, :], TPE[:, 0:CTX], start=True, stop=True).then_inc(done[3], 1)
        phase_norm("cqnorm")
        phase_norm("ckvnorm")
        phase_norm("ckvcnorm", CTX)
        project("mgate", 0, H, KC, before("norm3", "split") + 8)

        hu = before("heads", "unit")

        def head_queries(h, hh):
            s = (hu + hh) % 2
            pe.wait_ge(w_split, h + hu + 1)
            feature_major(s, CQ, 2 * T, T, 2, 0, w0=0).then_inc(hp_done, 1)
            for n, (wp, xp) in enumerate(PASSES):
                mm = pe.matmul(PS[:, 1024:1024 + CTX], w(s, wp, 4), CKV[:, xp * TK + T:xp * TK + TK],
                               start=(n == 0), stop=(n == 2))
            mm.then_inc(hp_done, 1)

        def head_keys(h, hh):
            s = (hu + hh) % 2
            feature_major(s, CKV, TK, TK, 1, 1536, n=T, w0=4, opens=False).then_inc(hp_done, 1)
            pe.wait_ge(hq_lo, h * 4 + 1)
            feature_major(s, CQ, 2 * T, T, 2, 0, w0=2, opens=False).then_inc(hp_done, 1)

        def head_values(h, hh):
            s = (hu + hh) % 2
            pe.wait_ge(hq_lo, h * 4 + 3)
            token_major(s, CKV, TK, TK, 1, 1536, 10, w0=5).then_inc(hp_done, 1)

        def mla_scores(t):
            base = 1536 * (t % 2)
            for a in range(0, TK, 512):
                m = min(512, TK - a)
                for n, (qp_, kp_) in enumerate(PASSES):
                    pe.matmul(PS[:, base + a:base + a + m], QN[:, qp_ * T + t * P:qp_ * T + (t + 1) * P],
                              KN[:, kp_ * TK + a:kp_ * TK + a + m], start=(n == 0), stop=False)
                for n, (qp_, kp_) in enumerate(PASSES):
                    mm = pe.matmul(PS[:, base + a:base + a + m], QP[:, qp_ * T + t * P:qp_ * T + (t + 1) * P],
                                   KPE[:, kp_ * TK + a:kp_ * TK + a + m], start=False, stop=(n == 2))
            mm.then_inc(sc_done, 1)

        def first_scores(h):
            pe.wait_ge(hq_lo, h * 4 + 4)
            mla_scores(0)
            pe.wait_ge(vn_act, h * 2 + 2)
            pe.wait_ge(vn_dve, h + 1)
            mla_scores(1)

        def transposes(t, blocks, bank):
            for kb in range(*blocks):
                mm = pe.transpose(PS[:, bank + (kb - blocks[0]) * P:bank + (kb - blocks[0] + 1) * P],
                                  E[:, (t % 2) * TK + kb * P:(t % 2) * TK + (kb + 1) * P], ident[:, :])
            return mm

        def mla_head(h, hh, last=False):
            for t in range(QT_N):
                tg = h * 8 + t
                pe.wait_ge(e_ready, tg + 1)
                pe.wait_ge(pta, tg * 2 + 1)
                transposes(t, (0, 4), 3072).then_inc(tpa_done, 1)
                pe.wait_ge(pv_free, tg + 1)
                transposes(t, (4, 8), 3584).then_inc(tpb_done, 1)
                if t + 2 < QT_N:
                    mla_scores(t + 2)
                elif not last:
                    (head_queries if t == QT_N - 2 else head_keys)(h + 1, 1 - hh)
                pe.wait_ge(pta, tg * 2 + 2)
                transposes(t, (8, 10), 3072).then_inc(tpa_done, 1)
                pe.wait_ge(ptb, tg + 2)
                for kb in range(10):
                    if kb == 8:
                        pe.wait_ge(pta, tg * 2 + 3)
                    mm = pe.matmul(PS[:, 3584:3584 + P], VN[:, hh * TK + kb * P:hh * TK + (kb + 1) * P],
                                   PT[:, kb * P:(kb + 1) * P], start=(kb == 0), stop=(kb == 9))
                mm.then_inc(pv_done, 1)
            if not last:
                head_values(h + 1, 1 - hh)
                first_scores(h + 1)

        for p in range(4):
            take(p, b("heads", p))
        pe.wait_ge(lo, before("mgate", "split"))
        pe.wait_ge(kpe_lo, 1)
        head_queries(0, 0)
        head_keys(0, 0)
        head_values(0, 0)
        first_scores(0)
        with pe.Fori(0, HEADS // 2 - 1) as i:
            for hh in range(2):
                mla_head(i * 2 + hh, hh)
        mla_head(HEADS - 2, 0)
        mla_head(HEADS - 1, 1, last=True)
        pe.wait_ge(pv_free, 65)
        pe.wait_ge(pta, 129)
        pe.wait_ge(ptb, 65)
        project("out2", 0, H, KC, before("out2", "split"))
        phase_norm("norm4")

        pe.wait_ge(ft_in, 16 * 4)
        with pe.Fori(0, FG) as i:
            u0 = before("four", "unit")
            for s in range(2):
                take(s, i + b("four", s))
                pe.wait_ge(w_split, i * 2 + u0 + s + 1)
                feature_major((u0 + s) % 2, H, KC * T, T, KC, s * 1024,
                              ready=None if s else before("norm4", "split")).then_inc(done[s], 1)
            pe.wait_ge(ze_ready, i * 2 + 2)
            take(2, i * 2 + b("four", 2))
            for q in range(2):
                for k in range(4):
                    mm = pe.matmul(PS[:, 2048 + q * 512 + k * P:2048 + q * 512 + (k + 1) * P],
                                   ZEO[:, q * HALF + k * P:q * HALF + (k + 1) * P], CSD[:, q * P:(q + 1) * P],
                                   start=True, stop=True)
            mm.then_inc(done[2], 1)
            take(3, i * 2 + b("four", 3))
            pe.matmul(PS[0:1, 3072:3072 + P], ZR[:, HALF:HALF + 1], CSD[:, 0:P], start=True, stop=True
                      ).then_inc(done[3], 1)
            pe.wait_ge(m_evac, i * 2 + 2)
            pe.wait_ge(mr_ready, i + 1)
            take(3, i * 2 + b("four", 3) + 1)
            for k in range(4):
                pe.matmul(PS[:, 3072:3584], M12[:, k * P:(k + 1) * P], CTAB[:, k * HALF:(k + 1) * HALF],
                          start=(k == 0), stop=False)
            pe.matmul(PS[:, 3072:3584], MR[0:1, :], ALT[0:1, :], start=False, stop=True)
            for k in range(4):
                mm = pe.matmul(PS[:, 3584:4096], M12[:, HALF + k * P:HALF + (k + 1) * P],
                               STAB[:, k * HALF:(k + 1) * HALF], start=(k == 0), stop=(k == 3))
            mm.then_inc(done[3], 1)
            take(2, i * 2 + b("four", 2) + 1)
            for k in range(4):
                pe.matmul(PS[:, 2048:2049], M12[:, k * P:(k + 1) * P], v1("alt"), start=(k == 0), stop=False)
            pe.matmul(PS[:, 2048:2049], MR[0:1, :], ones[0:1, 0:1], start=False, stop=True).then_inc(done[2], 1)
        project("out3", 0, H, KC, before("out3", "split"))
        phase_norm("final")

    @block.scalar
    def _(act):
        chain = Chain(act, s_act)

        def norm(idx, eps_cols):
            act.wait_ge(ms_ready, idx + 1)
            act.activation(stat[:, 0:eps_cols], stat[:, 0:eps_cols], ACT.Sqrt).then_inc(sd_ready, 1)

        def phase_norm(phase, n=T):
            norm(before(phase, "norm"), n // P)

        for h in range(HEADS_C):
            act.wait_ge(g_row, h + 1)
            act.dma_start(scratch[h].rearrange("(p n) -> p n", p=P), grow[:, :]).then_inc(g_out, 16)
        for c in range(KC):
            act.wait_ge(x_in[c], 16)
            if c >= 1:
                act.wait_ge(sq_added, c)
            act.activation(SQ, X[:, c * T:(c + 1) * T], ACT.Square).then_inc(sq_ready, 1)
        phase_norm("norm1")
        xts = [0]

        def hi_blocks(dst, cols_, size, count, base):
            for c in range(count):
                xts[0] += 1
                act.wait_ge(xt, xts[0])
                act.activation(dst[:, c * size:(c + 1) * size], TMP[c % 2][:, 0:size], ACT.Copy).then_inc(hi, 1)

        hi_blocks(H, KC * T, T, KC, 0)
        act.wait_ge(lam_sum, 1)
        act.activation(cols[:, 2:4], cols[:, 0:2], ACT.Exp).then_inc(lam_exp, 1)
        for j in range(4):
            p = j % 2
            act.wait_ge(done[p], before("ux", p) + j // 2 + 1)
            if j < 2:
                chain(act.activation(U[:, j * T:(j + 1) * T], pair(p), ACT.Gelu))
            else:
                chain(act.activation(XB[:, (j - 2) * PADX + 16:(j - 2) * PADX + 16 + T], pair(p), ACT.Copy))
            act.sem_inc(free[p], 1)
            act.sem_inc(u_ready if j < 2 else xb_ready, 1)
        for j in range(2):
            act.wait_ge(done[2 + j], before("va", 2 + j) + 1)
            chain(act.activation(TMP[j], pair(2 + j), ACT.Gelu))
            act.sem_inc(free[2 + j], 1)
        for j in range(2):
            act.wait_ge(done[2 + j], before("va", 2 + j) + 2)
            dst = VA[:, :].rearrange("p (i c) -> p i c", i=QT_N)[:, :, j * P:(j + 1) * P]
            chain(act.activation(dst, pair(2 + j).rearrange("p (i c) -> p i c", i=QT_N), ACT.Copy))
            act.sem_inc(free[2 + j], 1)
            act.sem_inc(va_ready, 1)
        act.wait_ge(va_ms, 1)
        act.activation(stat[:, 0:QT_N], stat[:, 0:QT_N], ACT.Sqrt).then_inc(va_sd, 1)
        act.wait_ge(g_out, 16 * HEADS_C)
        for j in range(2):
            xts[0] += 1
            act.wait_ge(xt, xts[0])
            act.activation(YA[:, j * T:(j + 1) * T], TMP[j], ACT.Copy).then_inc(hi, 1)
        for j in range(2):
            act.wait_ge(done[2 + j], before("pool", 2 + j) + 1)
            act.activation(YB[:, j * T:(j + 1) * T], pair(2 + j), ACT.Copy, scale=v1("pool_scale", j)).then_inc(hi, 1)

        act.wait_ge(lo, 12)
        with act.Fori(0, HEADS_C // 2) as i:
            for hh in range(2):
                n0, n1 = before("diff", 0) + 10 * hh, before("diff", 1) + 10 * hh
                if hh == 1:
                    act.wait_ge(neg_ready, i * 16 + 8 * hh)
                else:
                    act.wait_ge(lo, i * 2 + 12)
                act.dma_start(BR[:, :], shifted[bass.ds(i * 2 + hh, 1)].rearrange("o p n -> p (o n)")
                              ).then_inc(br_in, 16)
                for n, (dst, p, number) in enumerate(((QT[:, :], 0, n0 + 1), (KT[:, :], 1, n1 + 1),
                                                      (TMP0, 0, n0 + 2), (VC[:, :], 1, n1 + 2))):
                    act.wait_ge(done[p], i * 20 + number)
                    if n == 2:
                        act.wait_ge(lo, i * 2 + (before("diff", "split") + hh))
                    act.activation(dst, pair(p), ACT.Copy, scale=1.0 if n else 0.125).then_inc(qkv_ready, 1)
                    act.wait_ge(qkv_ready, i * 8 + 4 * hh + n + 1)
                    act.sem_inc(free[p], 1)

                def exps(t):
                    n = (t + 1) * P
                    act.wait_ge(neg_ready, i * 16 + 8 * hh + t + 1)
                    for c, S in enumerate((SA[t % 2], SB[t % 2])):
                        o = 2 * (t % 2) + c
                        act.activation(S[:, 0:n], S[:, 0:n], ACT.Exp, bias=cols[:, 8 + o:9 + o],
                                       accum_out=cols[:, 50 + o:51 + o]).then_inc(exp_ready, 1)

                exps(0)
                exps(1)
                for t in range(QT_N):
                    n = (t + 1) * P
                    act.wait_ge(done[0], i * 20 + n0 + 3 + t)
                    act.activation(AT[:, 0:n], PS[:, 0:n], ACT.Copy).then_inc(at_ready, 1)
                    act.wait_ge(at_ready, i * 16 + 8 * hh + t + 1)
                    act.sem_inc(free[0], 1)
                    if t + 2 < QT_N:
                        exps(t + 2)
                act.wait_ge(oc_ready, i * 16 + 8 * hh + 8)
                act.activation(ACC, OC, ACT.Square).then_inc(acc_ready, 1)
                norm(i * 2 + before("diff", "norm") + hh, QT_N)
                act.wait_ge(xt, i * 2 + xts[0] + hh + 1)
                act.activation(OCS[:, bass.ds(i * (2 * T) + hh * T, T)], TMP0, ACT.Copy).then_inc(hi, 1)
        xts[0] += 4

        with act.Fori(0, KC) as i:
            for j in range(3):
                act.wait_ge(done[j], i * (2 if j < 2 else 1) + before("merge", j) + 1)
                act.wait_ge(m_ready, i * 3 + j + 1)
                act.activation(SC[:, j * TS:j * TS + T], pair(j), ACT.Sigmoid,
                               bias=vec[:, bass.ds(i + (VEC["b_gate"] + 8 * j), 1)]).then_inc(sg_ready, 1)
                act.wait_ge(sg_ready, i * 3 + j + 1)
                act.sem_inc(free[j], 1)
        act.wait_ge(done[1], before("out1", 1))
        for c in range(KC):
            act.dma_start(XIN[:, c * T:(c + 1) * T], t_in["x"][c]).then_inc(c_x, 16)

        def block_hi(src, base_split):
            with act.Fori(0, KC) as i:
                act.activation(H[:, bass.ds(i * T, T)], src[:, bass.ds(i * T, T)], ACT.Copy).then_inc(hi, 1)

        act.wait_ge(m_ready, 3 * KC + 3)
        block_hi(M, 0)

        def residual(phase, extra=None):
            def turn(i, more):
                for s in range(2):
                    act.wait_ge(x_new, i * 2 + before(phase, "xnew") + s + 1)
                    act.activation(SQ, X[:, bass.ds(i * (2 * T) + s * T, T)], ACT.Square).then_inc(sq_ready, 1)
                    if more:
                        more(i, s)

            with act.Fori(0, KC // 2 - 1) as i:
                turn(i, extra)
            turn(KC // 2 - 1, None)

        residual("out1")
        phase_norm("norm2")
        hi_blocks(H, KC * T, T, KC, 0)

        f0 = 0
        for n, chunks in enumerate(FF_PASSES):
            up = f"up{n}"
            with act.Fori(0, chunks) as i:
                act.wait_ge(done[0], i + before(up, 0) + 1)
                act.wait_ge(cv_ready, i + f0 + 1)
                act.activation(SC[:, 2:2 + T], pair(0), ACT.Copy).then_inc(gp_ready, 1)
                act.wait_ge(gp_ready, i + f0 + 1)
                act.sem_inc(free[0], 1)
                act.wait_ge(cv_ready, i + f0 + 2)
                act.activation(SC[:, 2 * TS:2 * TS + T], SC[:, TS:TS + T], ACT.Gelu,
                               bias=vec[:, bass.ds(i + (VEC["conv_b"] + f0), 1)]).then_inc(gl_ready, 1)
                act.wait_ge(xt, i + xts[0] + 1)
                act.activation(FF[:, bass.ds(i * T, T)], SC[:, 3 * TS:3 * TS + T], ACT.Copy).then_inc(hi, 1)
            xts[0] += chunks
            f0 += chunks
            if n == len(FF_PASSES) - 1:
                act.wait_ge(done[1], before("down2", 1))
                act.dma_start(CL[:, :], t_in["c"].partition_broadcast(P)).then_inc(c_rows, 16)
                act.dma_start(CC[:, :], t_in["c_ctx"].partition_broadcast(P)).then_inc(c_rows, 16)
                for g in range(2):
                    act.dma_start(AW[:, g * 6 * D:(g + 1) * 6 * D], t_in["ada"][g]).then_inc(ada_in[g], 16)
                act.wait_ge(c_rows, 32)
                act.activation(CL[:, :], CL[:, :], ACT.Silu).then_inc(c_silu, 1)
                act.activation(CC[:, :], CC[:, :], ACT.Silu).then_inc(c_silu, 1)

                def next_ada(i, s):
                    act.wait_ge(ada_used, i * 2 + s + 1)
                    act.dma_start(AW[:, s * 6 * D:(s + 1) * 6 * D],
                                  t_in["ada"][bass.ds(i * 2 + s + 2, 1)].rearrange("o p n -> p (o n)")
                                  ).then_inc(ada_in[s], 16)

                residual("down2", extra=next_ada)
        phase_norm("fnorm")
        for c in range(KC):
            act.wait_ge(x_new, before("fnorm", "xnew") + c + 1)
            if c >= 1:
                act.wait_ge(sq_added, before("norm3", "square") + c)
            act.activation(SQ, X[:, c * T:(c + 1) * T], ACT.Square).then_inc(sq_ready, 1)
        phase_norm("norm3")
        hi_blocks(H, KC * T, T, KC, 0)
        act.dma_start(CXR[:, :], t_in["ctx"]).then_inc(ctx_in, 16)
        act.dma_start(CST[:, :], t_in["cs"]).then_inc(cs_in, 16)
        act.wait_ge(ctx_in, 16)
        for c in range(KC):
            if c >= 1:
                act.wait_ge(sq_added, before("normc", "square") + c)
            act.activation(SQ[:, 0:CTX], CXR[:, c * CTX:(c + 1) * CTX], ACT.Square).then_inc(sq_ready, 1)
        phase_norm("normc", CTX)
        hi_blocks(UC, KC * CTX, CTX, KC, 0)
        act.wait_ge(done[0], before("kvpe", 0) + 1)
        chain(act.activation(CKR[:, 0:T], pair(0), ACT.Copy))
        act.sem_inc(free[0], 1)
        act.wait_ge(done[1], before("kvpe", 1) + 1)
        chain(act.activation(CKR[:, T:TK], pair(1, CTX), ACT.Copy))
        act.sem_inc(free[1], 1)
        act.sem_inc(ckr_ready, 1)
        for j in range(2):
            act.wait_ge(done[j], before("cq", j) + 1)
            chain(act.activation(CQR[:, j * T:(j + 1) * T], pair(j), ACT.Copy))
            act.sem_inc(free[j], 1)
        act.wait_ge(done[2], before("kvpe", 2) + 1)
        chain(act.activation(KPR[:, 0:T], pair(2), ACT.Copy))
        act.sem_inc(free[2], 1)
        act.wait_ge(done[3], before("kvpe", 3) + 1)
        chain(act.activation(KPR[:, T:TK], pair(3, CTX), ACT.Copy))
        act.sem_inc(free[3], 1)
        act.sem_inc(kpe_ready, 2)
        for c in range(2):
            if c:
                act.wait_ge(sq_added, before("cqnorm", "square") + 1)
            act.activation(SQ, CQR[:, c * T:(c + 1) * T], ACT.Square).then_inc(sq_ready, 1)
        phase_norm("cqnorm")
        hi_blocks(CQ, 2 * T, T, 2, 0)
        for phase, a, n in (("ckvnorm", 0, T), ("ckvcnorm", T, CTX)):
            act.wait_ge(lo, before(phase, "split"))
            act.activation(ACC[:, 0:n], CKR[:, a:a + n], ACT.Square).then_inc(acc_ready, 1)
            phase_norm(phase, n)
            xts[0] += 1
            act.wait_ge(xt, xts[0])
            act.activation(CKV[:, a:a + n], TMP0[:, 0:n], ACT.Copy).then_inc(hi, 1)
        act.wait_ge(lo, before("mgate", "split"))
        with act.Fori(0, KC // 2) as i:
            for s in range(2):
                act.wait_ge(done[s], i + before("mgate", s) + 1)
                act.activation(G[:, bass.ds(i * (2 * T) + s * T, T)], pair(s), ACT.Silu).then_inc(gate_ready, 1)
                act.wait_ge(gate_ready, i * 2 + s + 1)
                act.sem_inc(free[s], 1)
        act.dma_start(CSQ, t_in["cs"][:, CTX:TK]).then_inc(csq_in, 16)
        act.activation(KPE[:, 0:TK], KPR[:, :], ACT.Copy).then_inc(kpe_hi, 1)

        def hi_part(dst, src_at, n, count, at_=0):
            act.wait_ge(hp_done, count)
            act.activation(dst[:, at_:at_ + n], PS[:, src_at:src_at + n], ACT.Copy).then_inc(hq_hi, 1)

        def head_end(h, hh):
            act.wait_ge(qp_ready, h + 1)
            act.activation(QP[:, 0:T], TMP0, ACT.Copy).then_inc(hq_hi, 1)
            act.wait_ge(hp_done, h * 5 + 5)
            act.activation(VN[:, hh * TK:hh * TK + 512], PS[:, 1536:2048], ACT.Copy).then_inc(vn_act, 1)
            act.activation(VN[:, hh * TK + 1024:hh * TK + TK], PS[:, 2560:2560 + CTX], ACT.Copy).then_inc(vn_act, 1)
            mla_exp(h, 0)
            mla_exp(h, 1)

        def mla_exp(h, t):
            act.wait_ge(mx_ready, h * 8 + t + 1)
            base = 1536 * (t % 2)
            act.activation(E[:, (t % 2) * TK:(t % 2) * TK + TK], PS[:, base:base + TK], ACT.Exp,
                           bias=cols[:, 16 + t % 2:17 + t % 2], scale=MLA_SCALE,
                           accum_out=cols[:, 18 + t % 2:19 + t % 2]).then_inc(ex_ready, 1)

        def mla_head(h, hh, last=False):
            for t in range(QT_N):
                tg = h * 8 + t
                act.wait_ge(tpa_done, tg * 2 + 1)
                act.activation(PT[:, 0:512], PS[:, 3072:3584], ACT.Copy).then_inc(pta, 1)
                if t == QT_N - 2 and not last:
                    hi_part(QN, 0, T, h * 5 + 6)
                    hi_part(KN, 1024, CTX, h * 5 + 7, T)
                if t == QT_N - 1 and not last:
                    hi_part(KN, 1536, T, h * 5 + 8)
                act.wait_ge(tpa_done, tg * 2 + 2)
                act.activation(PT[:, 1024:TK], PS[:, 3072:3328], ACT.Copy).then_inc(pta, 1)
                if t + 2 < QT_N:
                    mla_exp(h, t + 2)
            if not last:
                head_end(h + 1, 1 - hh)

        hi_part(QN, 0, T, 1)
        hi_part(KN, 1024, CTX, 2, T)
        hi_part(KN, 1536, T, 3)
        head_end(0, 0)
        with act.Fori(0, HEADS // 2 - 1) as i:
            for hh in range(2):
                mla_head(i * 2 + hh, hh)
        mla_head(HEADS - 2, 0)
        mla_head(HEADS - 1, 1, last=True)
        act.wait_ge(pv_free, 65)
        block_hi(G, 0)

        act.dma_start(CTAB[:, :], t_in["ctab"]).then_inc(ft_in, 16)
        act.dma_start(STAB[:, :], t_in["stab"]).then_inc(ft_in, 16)
        act.dma_start(CSD[:, :], t_in["csd"]).then_inc(ft_in, 16)
        act.dma_start(ALT[0:1, :], t_in["altrow"]).then_inc(ft_in, 16)
        residual("out2")
        phase_norm("norm4")
        hi_blocks(H, KC * T, T, KC, 0)
        with act.Fori(0, FG) as i:
            act.wait_ge(done[0], i + before("four", 0) + 1)
            act.activation(ZR[:, :], pair(0), ACT.Copy).then_inc(zr_ready, 1)
            act.wait_ge(zr_ready, i + 1)
            act.sem_inc(free[0], 1)
            act.wait_ge(done[1], i + before("four", 1) + 1)
            act.wait_ge(y_ready, i * 2 + 1)
            act.activation(TMP1, pair(1), ACT.Silu).then_inc(sgf_ready, 1)
            act.wait_ge(sgf_ready, i + 1)
            act.sem_inc(free[1], 1)
            act.wait_ge(done[2], i * 2 + before("four", 2) + 1)
            act.activation(M12[:, 0:HALF], PS[:, 2048:2560], ACT.Copy).then_inc(m_evac, 1)
            act.wait_ge(done[3], i * 2 + before("four", 3) + 1)
            act.activation(MR[0:1, :], PS[0:1, 3072:3072 + P], ACT.Copy).then_inc(mr_ready, 1)
            act.wait_ge(mr_ready, i + 1)
            act.sem_inc(free[3], 1)
            act.wait_ge(done[3], i * 2 + before("four", 3) + 2)
            act.activation(TMP0[:, 0:HALF], PS[:, 3584:4096], ACT.Copy).then_inc(qs_ready, 1)
        act.wait_ge(y_ready, 2 * FG + 1)
        block_hi(Y, 0)
        residual("out3")
        phase_norm("final")
        for c in range(KC):
            act.wait_ge(o_ready, c + 1)
            act.dma_start(out[c], X[:, c * T:(c + 1) * T]).then_inc(o_out, 16)
        act.wait_ge(o_out, 16 * KC)

    @block.vector
    def _(v):
        chain = Chain(v, s_dve)
        for p in range(4):
            v.sem_inc(free[p], 1)
        for s in (pv_free, pta, ptb):
            v.sem_inc(s, 1)
        v.sem_inc(m_ready, 3)
        v.sem_inc(cv_ready, 1)
        v.sem_inc(y_ready, 1)
        xts = [0]
        his = [0]
        sqs = [0]

        chain(v.memset(ones[:, :], 1.0))
        v.memset(BD[:, :], 0.0).then_inc(memset_done, 1)
        chain(v.memset(XB[:, :], 0.0))
        v.wait_ge(c_early, 64)
        chain(v.memset(rbx[32:33, :], 1.0))
        chain(v.tensor_copy(rbx[0:32, :].rearrange("p (h n) -> p h n", h=HEADS_C),
                            rb[0:32, :].unsqueeze(2).to_broadcast([32, HEADS_C, P])))
        v.sem_inc(rbx_ready, 1)
        for h in range(HEADS_C):
            v.wait_ge(done[0], h + 1)
            v.wait_ge(done[1], h + 1)
            if h:
                v.wait_ge(g_out, 16 * h)
            chain(v.tensor_copy(grow[:, :], PS[:, 0:GROW]))
            v.sem_inc(free[0], 1)
            v.sem_inc(free[1], 1)
            v.sem_inc(g_row, 1)

        def add_squares(count, n=T, first=True):
            for c in range(count):
                sqs[0] += 1
                v.wait_ge(sq_ready, sqs[0])
                if c == 0:
                    ins = v.tensor_copy(ACC[:, 0:n], SQ[:, 0:n])
                else:
                    ins = v.tensor_tensor(ACC[:, 0:n], ACC[:, 0:n], SQ[:, 0:n], ALU.add)
                ins.then_inc(sq_added, 1)
                acs[0] += 1
                v.wait_ge(sq_added, acs[0])
            v.sem_inc(acc_ready, 1)

        acs = [0]

        def norm_scale(idx, p2, p3, n, width, eps):
            k = n // P
            v.wait_ge(done[2], p2 + 1)
            v.tensor_scalar(stat[:, 0:k], PS[:, 2048:2048 + k], 1.0 / width, eps, ALU.mult, ALU.add
                            ).then_inc(ms_ready, 1)
            v.wait_ge(ms_ready, idx + 1)
            v.sem_inc(free[2], 1)
            v.wait_ge(sd_ready, idx + 1)
            chain(v.reciprocal(stat[:, 0:k], stat[:, 0:k]))
            v.tensor_tensor(DIAG[:, 0:n].rearrange("p (j c) -> p j c", j=k),
                            ident[:, :].unsqueeze(1).to_broadcast([P, k, P]),
                            stat[:, 0:k].unsqueeze(2).to_broadcast([P, k, P]), ALU.mult).then_inc(diag_ready, 1)
            v.wait_ge(done[3], p3 + 1)

        def phase_scale(phase, width, eps, n=T):
            norm_scale(before(phase, "norm"), before(phase, 2), before(phase, 3), n, width, eps)

        def apply_split(dst, dst_cols, src, count, n, gain, shift=None, last_free=3):
            def make(c):
                t = TMP[c % 2][:, 0:n]
                ins = v.scalar_tensor_tensor(out=t, in0=src[:, c * n:(c + 1) * n], scalar=gain(c),
                                             in1=PS[:, 3072:3072 + n], op0=ALU.mult, op1=ALU.mult)
                if shift is not None:
                    chain(ins)
                    ins = v.tensor_scalar(t, t, shift(c), None, ALU.add)
                ins.then_inc(xt, 1)

            def low(c):
                his[0] += 1
                v.wait_ge(xt, xts[0] + c + 1)
                v.wait_ge(hi, his[0])
                h = dst[:, c * n:(c + 1) * n]
                v.tensor_tensor(dst[:, dst_cols + c * n:dst_cols + (c + 1) * n], TMP[c % 2][:, 0:n],
                                h.bitcast(F32), ALU.subtract).then_inc(lo, 1)
                v.wait_ge(lo, his[0])

            make(0)
            for c in range(count):
                if c + 1 < count:
                    make(c + 1)
                low(c)
            v.sem_inc(free[3], 1)
            xts[0] += count

        add_squares(KC)
        for c in range(KC):
            v.wait_ge(x_in[c], 16)
        phase_scale("norm1", D, 1e-6)
        apply_split(H, KC * T, X, KC, T, lambda c: v1("attn_g", c))

        v.wait_ge(c_gm, 16 * 15)
        for q in range(2):
            chain(v.tensor_tensor(lvp[:, :], lv[:, 128 * q:128 * q + 64], lv[:, 128 * q + 64:128 * q + 128], ALU.mult))
            chain(v.tensor_reduce(cols[:, q:q + 1], lvp[:, :], AX, ALU.add))
        v.sem_inc(lam_sum, 1)
        v.wait_ge(lam_exp, 1)
        chain(v.tensor_tensor(cols[:, 4:5], cols[:, 2:3], cols[:, 3:4], ALU.subtract))
        chain(v.tensor_scalar(cols[:, 5:6], cols[:, 4:5], LAM_INIT, None, ALU.add))
        chain(v.tensor_scalar(cols[:, 6:7], v1("subln"), 1.0 - LAM_INIT, None, ALU.mult))
        v.tensor_tensor(WST[:, :].rearrange("p (g t) -> p g t", g=4), WST[:, :].rearrange("p (g t) -> p g t", g=4),
                        TRI[:, :].unsqueeze(1).to_broadcast([P, 4, P]), ALU.mult).then_inc(wst_ready, 1)

        v.wait_ge(va_ready, 2)
        for i in range(QT_N):
            chain(v.bn_stats(bn[:, 0:6], VA[:, i * 256:(i + 1) * 256]))
            chain(v.bn_aggr(cols[:, 32 + 2 * i:34 + 2 * i], bn[:, 0:6]))
        chain(v.tensor_scalar(stat[:, 0:QT_N], cols[:, 32:48].rearrange("p (i c) -> p i c", c=2)[:, :, 1], 1e-5, None,
                              ALU.add))
        v.sem_inc(va_ms, 1)
        v.wait_ge(va_sd, 1)
        chain(v.reciprocal(stat[:, 0:QT_N], stat[:, 0:QT_N]))
        for i in range(QT_N):
            row = VA[:, i * 256:(i + 1) * 256]
            chain(v.tensor_scalar(row, row, cols[:, 32 + 2 * i:33 + 2 * i], stat[:, i:i + 1], ALU.subtract, ALU.mult))
            chain(v.tensor_tensor(row, row, lngb[:, 0:256], ALU.mult))
            v.tensor_tensor(row, row, lngb[:, 256:512], ALU.add).then_inc(va_norm, 1)
        v.wait_ge(u_ready, 2)
        for j in range(2):
            v.wait_ge(done[2 + j], before("gmlp", 2 + j) + 1)
            chain(v.tensor_tensor(TMP[j].rearrange("p (i t) -> p i t", i=QT_N),
                                  pair(2 + j).rearrange("p (i t) -> p i t", i=QT_N),
                                  SGB[:, j * P:(j + 1) * P].unsqueeze(1).to_broadcast([P, QT_N, P]), ALU.add))
            v.sem_inc(free[2 + j], 1)
            v.tensor_tensor(TMP[j], TMP[j], U[:, j * T:(j + 1) * T], ALU.mult).then_inc(xt, 1)
            xts[0] += 1
            v.wait_ge(xt, xts[0])
            his[0] += 1
            v.wait_ge(hi, his[0])
            v.tensor_tensor(YA[:, 2 * T + j * T:2 * T + (j + 1) * T], TMP[j],
                            YA[:, j * T:(j + 1) * T].bitcast(F32), ALU.subtract).then_inc(lo, 1)
            v.wait_ge(lo, his[0])

        v.wait_ge(xb_ready, 2)
        chain(v.memset(PA[:, 0:2 * PADX], 0.0))
        chain(v.memset(PB[:, :], 0.0))

        def double(dst, src, step, parts, j):
            a = j * PADX + 16
            chain(v.tensor_tensor(dst[parts, a:a + T], src[parts, a:a + T], src[parts, a - step:a - step + T], ALU.add))

        every = slice(0, P)
        for j in range(2):
            double(PA, XB, 1, every, j)
            double(PB, PA, 2, every, j)
        double(PA, PB, 4, every, 1)
        double(PB, PA, 8, slice(64, P), 1)
        sums = {0: PA, 1: PB, 2: PA, 3: PB}
        for g in range(4):
            j, parts = g // 2, slice(64 * (g % 2), 64 * (g % 2) + 64)
            a = j * PADX + 16
            s = sums[g]
            chain(v.tensor_tensor(s[parts, a:a + 16], s[parts, a:a + 16], EDGE[parts, j * 16:(j + 1) * 16], ALU.mult))
            x = XB[parts, a:a + T]
            chain(v.scalar_tensor_tensor(out=x[:, 16:T], in0=s[parts, a + 16:a + T],
                                         scalar=vec[parts, VEC["pool_inv"] + j:VEC["pool_inv"] + j + 1],
                                         in1=x[:, 16:T], op0=ALU.mult, op1=ALU.subtract))
            chain(v.tensor_tensor(x[:, 0:16], s[parts, a:a + 16], x[:, 0:16], ALU.subtract))
            if g % 2:
                v.sem_inc(p_ready, 1)
        for j in range(2):
            v.wait_ge(done[2 + j], before("pool", 2 + j) + 1)
            his[0] += 1
            v.wait_ge(hi, his[0])
            v.scalar_tensor_tensor(out=YB[:, 2 * T + j * T:2 * T + (j + 1) * T], in0=pair(2 + j),
                                   scalar=v1("pool_scale", j), in1=YB[:, j * T:(j + 1) * T].bitcast(F32),
                                   op0=ALU.mult, op1=ALU.subtract).then_inc(lo, 1)
            v.wait_ge(lo, his[0])
            v.sem_inc(free[2 + j], 1)

        with v.Fori(0, HEADS_C // 2) as i:
            chain.enter(i, 2 * (8 * 7 + 1))
            for hh in range(2):
                n0, n1, n2, n3 = (before("diff", p) + k * hh for p, k in ((0, 10), (1, 10), (2, 9), (3, 9)))
                v.wait_ge(br_in, i * 32 + 16 * hh + 16)

                def biased(t):
                    n = (t + 1) * P
                    o = 2 * (t % 2)
                    for c, S in enumerate((SA[t % 2], SB[t % 2])):
                        v.wait_ge(done[2 + c], i * 18 + (n2, n3)[c] + t + 1)
                        v.sem_inc(sc_seen, 1)
                        chain(v.tensor_tensor_reduce(out=S[:, 0:n], in0=PS[:, (2 + c) * 1024:(2 + c) * 1024 + n],
                                                     in1=BR[:, T - n:T], scale=1.0, scalar=-3.0e38, op0=ALU.add,
                                                     op1=ALU.max, accum_out=cols[:, 54 + c:55 + c]))
                        v.sem_inc(free[2 + c], 1)
                    v.tensor_scalar(cols[:, 8 + o:10 + o], cols[:, 54:56], -1.0, None, ALU.mult
                                    ).then_inc(neg_ready, 1)
                    v.wait_ge(neg_ready, i * 16 + 8 * hh + t + 1)

                def output(t):
                    v.wait_ge(done[1], i * 20 + n1 + 3 + t)
                    chain(v.tensor_copy(OC[:, t * P:(t + 1) * P], PS[:, 1024:1024 + P]))
                    v.sem_inc(free[1], 1)
                    v.sem_inc(oc_ready, 1)

                biased(0)
                biased(1)
                for t in range(QT_N):
                    n = (t + 1) * P
                    o = 2 * (t % 2)
                    S0, S1 = SA[t % 2], SB[t % 2]
                    v.wait_ge(exp_ready, i * 32 + 16 * hh + 2 * t + 2)
                    chain(v.reciprocal(cols[:, 14:16], cols[:, 50 + o:52 + o]))
                    chain(v.tensor_tensor(cols[:, 20:21], cols[:, 15:16], cols[:, 5:6], ALU.mult))
                    chain(v.tensor_scalar(S1[:, 0:n], S1[:, 0:n], cols[:, 20:21], None, ALU.mult))
                    chain(v.scalar_tensor_tensor(out=S0[:, 0:n], in0=S0[:, 0:n], scalar=cols[:, 14:15],
                                                 in1=S1[:, 0:n], op0=ALU.mult, op1=ALU.subtract))
                    v.sem_inc(aa_ready, 1)
                    if t:
                        output(t - 1)
                    if t + 2 < QT_N:
                        v.wait_ge(done[0], i * 20 + n0 + 3 + t)
                        biased(t + 2)
                output(QT_N - 1)
                norm_scale(i * 2 + before("diff", "norm") + hh, i * 18 + n2 + 8, i * 18 + n3 + 8, T, P, 1e-5)
                v.scalar_tensor_tensor(out=TMP0, in0=OC, scalar=cols[:, 6:7], in1=PS[:, 3072:4096],
                                       op0=ALU.mult, op1=ALU.mult).then_inc(xt, 1)
                v.wait_ge(xt, i * 2 + xts[0] + hh + 1)
                v.sem_inc(free[3], 1)
                v.wait_ge(hi, i * 2 + his[0] + hh + 1)
                v.tensor_tensor(OCS[:, bass.ds(i * (2 * T) + 4 * T + hh * T, T)], TMP0,
                                OCS[:, bass.ds(i * (2 * T) + hh * T, T)].bitcast(F32), ALU.subtract).then_inc(lo, 1)
                v.wait_ge(lo, i * 2 + his[0] + hh + 1)
            chain.leave(HEADS_C // 2)
        xts[0] += 4
        his[0] += 4

        with v.Fori(0, KC) as i:
            chain.enter(i, 3)
            m = M[:, bass.ds(i * T, T)]
            t = SC[:, 3 * TS:3 * TS + T]
            for j, p in enumerate((3, 0, 1)):
                v.wait_ge(sg_ready, i * 3 + j + 1)
                v.wait_ge(done[p], i * (1 if p == 3 else 2) + before("merge", p) + (1 if p == 3 else 2))
                sg = SC[:, j * TS:j * TS + T]
                chain(v.tensor_tensor(t if j else m, sg, pair(p), ALU.mult))
                v.sem_inc(free[p], 1)
                if j == 0:
                    v.sem_inc(m_ready, 1)
                else:
                    v.tensor_tensor(m, m, t, ALU.add).then_inc(m_ready, 1)
                    v.wait_ge(m_ready, i * 3 + j + 4)
            chain.leave(KC)

        def block_lo(src, last=None):
            with v.Fori(0, KC) as i:
                v.wait_ge(hi, i + his[0] + 1)
                v.tensor_tensor(H[:, bass.ds(i * T + KC * T, T)], src[:, bass.ds(i * T, T)],
                                H[:, bass.ds(i * T, T)].bitcast(F32), ALU.subtract).then_inc(lo, 1)
            his[0] += KC
            v.wait_ge(lo, his[0])

        block_lo(M)
        v.wait_ge(c_x, 16 * KC)

        def residual(phase, p0, gain=None, other=None, squares=True, extra=None, extra_steps=0):
            if squares:
                chain(v.memset(ACC, 0.0))
            with v.Fori(0, KC // 2) as i:
                if extra_steps:
                    chain.enter(i, extra_steps)
                for s in range(2):
                    x = X[:, bass.ds(i * (2 * T) + s * T, T)]
                    old = other[:, bass.ds(i * (2 * T) + s * T, T)] if other is not None else x
                    v.wait_ge(done[p0 + s], i + before(phase, p0 + s) + 1)
                    if gain is None:
                        ins = v.tensor_tensor(x, pair(p0 + s), old, ALU.add)
                    else:
                        ins = v.scalar_tensor_tensor(out=x, in0=pair(p0 + s), scalar=gain[:, bass.ds(i * 2 + s, 1)],
                                                     in1=old, op0=ALU.mult, op1=ALU.add)
                    ins.then_inc(x_new, 1)
                    v.wait_ge(x_new, i * 2 + before(phase, "xnew") + s + 1)
                    v.sem_inc(free[p0 + s], 1)
                    if squares:
                        v.wait_ge(sq_ready, i * 2 + sqs[0] + s + 1)
                        v.tensor_tensor(ACC, ACC, SQ, ALU.add).then_inc(sq_added, 1)
                        v.wait_ge(sq_added, i * 2 + acs[0] + s + 1)
                    if extra:
                        extra(i, s)
                if extra_steps:
                    chain.leave(KC // 2)
            if squares:
                sqs[0] += KC
                acs[0] += KC
                v.sem_inc(acc_ready, 1)

        residual("out1", 0, other=XIN)
        phase_scale("norm2", D, 1e-6)
        apply_split(H, KC * T, X, KC, T, lambda c: v1("ffn_g", c))

        chain(v.memset(SC[:, 0:2], 0.0))
        f0 = 0
        for n, chunks in enumerate(FF_PASSES):
            up = f"up{n}"
            with v.Fori(0, chunks) as i:
                chain.enter(i, 2)
                conv = SC[:, TS:TS + T]

                def tap(k):
                    return vec[:, bass.ds(i + (VEC[f"conv{k}"] + f0), 1)]

                v.wait_ge(gp_ready, i + f0 + 1)
                chain(v.tensor_scalar(conv, SC[:, 0:T], tap(0), None, ALU.mult))
                chain(v.scalar_tensor_tensor(out=conv, in0=SC[:, 1:1 + T], scalar=tap(1), in1=conv,
                                             op0=ALU.mult, op1=ALU.add))
                v.scalar_tensor_tensor(out=conv, in0=SC[:, 2:2 + T], scalar=tap(2), in1=conv,
                                       op0=ALU.mult, op1=ALU.add).then_inc(cv_ready, 1)
                v.wait_ge(cv_ready, i + f0 + 2)
                v.wait_ge(gl_ready, i + f0 + 1)
                v.wait_ge(done[1], i + before(up, 1) + 1)
                v.tensor_tensor(SC[:, 3 * TS:3 * TS + T], SC[:, 2 * TS:2 * TS + T], pair(1), ALU.mult).then_inc(xt, 1)
                v.wait_ge(xt, i + xts[0] + 1)
                v.sem_inc(free[1], 1)
                v.wait_ge(hi, i + his[0] + 1)
                v.tensor_tensor(FF[:, bass.ds(i * T + KC * T, T)], SC[:, 3 * TS:3 * TS + T],
                                FF[:, bass.ds(i * T, T)].bitcast(F32), ALU.subtract).then_inc(lo, 1)
                v.wait_ge(lo, i + his[0] + 1)
                chain.leave(chunks)
            xts[0] += chunks
            his[0] += chunks
            f0 += chunks
            if n < len(FF_PASSES) - 1:
                residual(f"down{n}", 2, squares=False)
            else:
                v.wait_ge(c_silu, 2)

                def ada(i, s):
                    v.wait_ge(ada_in[s], i * 16 + 16)
                    for j in range(8):
                        tile, row = ((j // 2, (CL, CC)[j % 2]) if j < 4 else (j - 2, CL))
                        chain(v.tensor_tensor_reduce(out=AJ[:, :], in0=AW[:, (s * 6 + tile) * D:(s * 6 + tile + 1) * D],
                                                     in1=row[:, :], scale=1.0, scalar=0.0, op0=ALU.mult, op1=ALU.add,
                                                     accum_out=adac[:, j:j + 1]))
                    both = adac[:, 0:4].rearrange("p (t c) -> p t c", c=2)
                    chain(v.tensor_copy(modb[:, bass.ds(i * 4 + 2 * s, 2)], both[:, :, 0]))
                    chain(v.tensor_copy(modb[:, bass.ds(i * 4 + 2 * s + 16, 2)], both[:, :, 1]))
                    chain(v.tensor_copy(modl[:, bass.ds(i * 8 + 4 * s, 4)], adac[:, 4:8]))
                    v.sem_inc(ada_used, 1)

                residual("down2", 2, extra=ada, extra_steps=22)
        for q in range(2):
            chain(v.tensor_tensor(modb[:, 16 * q:16 * q + 16], modb[:, 16 * q:16 * q + 16],
                                  vec[:, VEC["b_both"]:VEC["b_both"] + 16], ALU.add))
        chain(v.tensor_tensor(modl[:, :], modl[:, :], vec[:, VEC["b_lat"]:VEC["b_lat"] + 32], ALU.add))
        for fac, scale, g in ((fac0, modb[:, 8:16], "norm_g0"), (facc, modb[:, 24:32], "norm_g0"),
                              (fac1, modl[:, 16:24], "norm_g1")):
            chain(v.tensor_scalar(fac[:, :], scale, 1.0, None, ALU.add))
            chain(v.tensor_tensor(fac[:, :], fac[:, :], vec[:, VEC[g]:VEC[g] + 8], ALU.mult))

        phase_scale("fnorm", D, 1e-6)
        for c in range(KC):
            x = X[:, c * T:(c + 1) * T]
            v.scalar_tensor_tensor(out=x, in0=x, scalar=v1("final_g", c), in1=PS[:, 3072:4096],
                                   op0=ALU.mult, op1=ALU.mult).then_inc(x_new, 1)
        v.wait_ge(x_new, before("fnorm", "xnew") + KC)
        v.sem_inc(free[3], 1)
        add_squares(KC)
        phase_scale("norm3", D, 1e-6)
        apply_split(H, KC * T, X, KC, T, lambda c: fac0[:, c:c + 1], lambda c: modb[:, c:c + 1])
        add_squares(KC, CTX)
        v.wait_ge(ctx_in, 16)
        phase_scale("normc", D, 1e-6, CTX)
        apply_split(UC, KC * CTX, CXR, KC, CTX, lambda c: facc[:, c:c + 1], lambda c: modb[:, 16 + c:17 + c])
        v.wait_ge(cs_in, 16)
        v.wait_ge(done[0], before("kvpe", 0) + 2)
        v.tensor_tensor(TPE[:, CTX:TK], pair(0), CST[:, CTX:TK], ALU.mult).then_inc(tpe_ready, 1)
        v.wait_ge(tpe_ready, 1)
        v.sem_inc(free[0], 1)
        v.wait_ge(done[1], before("kvpe", 1) + 2)
        v.tensor_tensor(TPE[:, 0:CTX], pair(1, CTX), CST[:, 0:CTX], ALU.mult).then_inc(tpe_ready, 1)
        v.wait_ge(tpe_ready, 2)
        v.sem_inc(free[1], 1)
        add_squares(2)
        phase_scale("cqnorm", 256, 1e-6)
        apply_split(CQ, 2 * T, CQR, 2, T, lambda c: v1("g_qa", c))
        for phase, a, n in (("ckvnorm", 0, T), ("ckvcnorm", T, CTX)):
            phase_scale(phase, P, 1e-6, n)
            v.scalar_tensor_tensor(out=TMP0[:, 0:n], in0=CKR[:, a:a + n], scalar=v1("g_kva"),
                                   in1=PS[:, 3072:3072 + n], op0=ALU.mult, op1=ALU.mult).then_inc(xt, 1)
            xts[0] += 1
            his[0] += 1
            v.wait_ge(xt, xts[0])
            v.sem_inc(free[3], 1)
            v.wait_ge(hi, his[0])
            v.tensor_tensor(CKV[:, TK + a:TK + a + n], TMP0[:, 0:n], CKV[:, a:a + n].bitcast(F32),
                            ALU.subtract).then_inc(lo, 1)
            v.wait_ge(lo, his[0])

        v.wait_ge(kpe_hi, 1)
        v.tensor_tensor(KPE[:, TK:2 * TK], KPR[:, :], KPE[:, 0:TK].bitcast(F32), ALU.subtract).then_inc(kpe_lo, 1)
        v.wait_ge(csq_in, 16)

        def lo_part(dst, half, src_at, n, count, at_=0):
            v.wait_ge(hq_hi, count)
            v.tensor_tensor(dst[:, half + at_:half + at_ + n], PS[:, src_at:src_at + n],
                            dst[:, at_:at_ + n].bitcast(F32), ALU.subtract).then_inc(hq_lo, 1)

        def rotate(h):
            v.wait_ge(hp_done, h * 5 + 4)
            v.tensor_tensor(TMP0, PS[:, 0:T], CSQ, ALU.mult).then_inc(qp_ready, 1)

        def head_end(h, hh):
            v.wait_ge(hq_hi, h * 4 + 4)
            v.wait_ge(qp_ready, h + 1)
            v.tensor_tensor(QP[:, T:2 * T], TMP0, QP[:, 0:T].bitcast(F32), ALU.subtract).then_inc(hq_lo, 1)
            v.wait_ge(hp_done, h * 5 + 5)
            v.tensor_copy(VN[:, hh * TK + 512:hh * TK + 1024], PS[:, 2048:2560]).then_inc(vn_dve, 1)
            peak(h, 0)
            normalise(h, 0)
            peak(h, 1)

        def peak(h, t):
            base = 1536 * (t % 2)
            v.wait_ge(sc_done, h * 8 + t + 1)
            chain(v.tensor_reduce(cols[:, 22 + t % 2:23 + t % 2], PS[:, base:base + TK], AX, ALU.max))
            v.tensor_scalar(cols[:, 16 + t % 2:17 + t % 2], cols[:, 22 + t % 2:23 + t % 2], -MLA_SCALE, None,
                            ALU.mult).then_inc(mx_ready, 1)

        def normalise(h, t):
            v.wait_ge(ex_ready, h * 8 + t + 1)
            chain(v.reciprocal(cols[:, 24 + t % 2:25 + t % 2], cols[:, 18 + t % 2:19 + t % 2]))
            e = E[:, (t % 2) * TK:(t % 2) * TK + TK]
            v.tensor_scalar(e, e, cols[:, 24 + t % 2:25 + t % 2], None, ALU.mult).then_inc(e_ready, 1)

        def mla_head(h, hh, last=False):
            for t in range(QT_N):
                tg = h * 8 + t
                v.wait_ge(tpb_done, tg + 1)
                v.tensor_copy(PT[:, 512:1024], PS[:, 3584:4096]).then_inc(ptb, 1)
                if t + 1 < QT_N:
                    normalise(h, t + 1)
                if t + 2 < QT_N:
                    peak(h, t + 2)
                if t == QT_N - 2 and not last:
                    lo_part(QN, T, 0, T, h * 4 + 5)
                    lo_part(KN, TK, 1024, CTX, h * 4 + 6, T)
                if t == QT_N - 1 and not last:
                    lo_part(KN, TK, 1536, T, h * 4 + 7)
                    rotate(h + 1)
                v.wait_ge(pv_done, tg + 1)
                g = G[:, bass.ds(h * T + t * P, P)]
                v.tensor_tensor(g, PS[:, 3584:3584 + P], g, ALU.mult).then_inc(pv_free, 1)
            if not last:
                head_end(h + 1, 1 - hh)

        lo_part(QN, T, 0, T, 1)
        lo_part(KN, TK, 1024, CTX, 2, T)
        lo_part(KN, TK, 1536, T, 3)
        rotate(0)
        head_end(0, 0)
        with v.Fori(0, HEADS // 2 - 1) as i:
            chain.enter(i, 2 * 8 * 2)
            for hh in range(2):
                mla_head(i * 2 + hh, hh)
            chain.leave(HEADS // 2 - 1)
        mla_head(HEADS - 2, 0)
        mla_head(HEADS - 1, 1, last=True)
        v.wait_ge(pv_free, 65)
        block_lo(G)
        residual("out2", 0, gain=modl[:, 0:8])
        phase_scale("norm4", D, 1e-6)
        apply_split(H, KC * T, X, KC, T, lambda c: fac1[:, c:c + 1], lambda c: modl[:, 8 + c:9 + c])

        with v.Fori(0, FG) as i:
            chain.enter(i, 4)
            v.wait_ge(zr_ready, i + 1)
            chain(v.tensor_copy(ZEO[:, 0:1], ZR[:, 0:1]))
            chain(v.memset(ZEO[:, HALF:HALF + 1], 0.0))
            back = ZR[:, T - 1:HALF:-1]
            v.tensor_tensor(ZEO[:, 1:HALF], ZR[:, 1:HALF], back, ALU.add).then_inc(ze_ready, 1)
            v.tensor_tensor(ZEO[:, HALF + 1:2 * HALF], ZR[:, 1:HALF], back, ALU.subtract).then_inc(ze_ready, 1)
            v.wait_ge(done[2], i * 2 + before("four", 2) + 1)
            v.tensor_copy(M12[:, HALF:2 * HALF], PS[:, 2560:3072]).then_inc(m_evac, 1)
            v.wait_ge(m_evac, i * 2 + 2)
            v.sem_inc(free[2], 1)
            v.wait_ge(qs_ready, i + 1)
            y = Y[:, bass.ds(i * T, HALF)]
            chain(v.tensor_tensor(y, PS[:, 3072:3584], TMP0[:, 0:HALF], ALU.subtract))
            y = Y[:, bass.ds(i * T + HALF + 1, HALF - 1)]
            v.tensor_tensor(y, PS[:, 3583:3072:-1], TMP0[:, HALF - 1:0:-1], ALU.add).then_inc(y_ready, 1)
            v.wait_ge(y_ready, i * 2 + 2)
            v.sem_inc(free[3], 1)
            v.wait_ge(done[2], i * 2 + before("four", 2) + 2)
            chain(v.tensor_copy(Y[:, bass.ds(i * T + HALF, 1)], PS[:, 2048:2049]))
            v.sem_inc(free[2], 1)
            v.wait_ge(sgf_ready, i + 1)
            y = Y[:, bass.ds(i * T, T)]
            v.tensor_tensor(y, y, TMP1, ALU.mult).then_inc(y_ready, 1)
            v.wait_ge(y_ready, i * 2 + 3)
            chain.leave(FG)
        block_lo(Y)
        residual("out3", 0, gain=modl[:, 24:32])
        phase_scale("final", D, 1e-6)
        for c in range(KC):
            x = X[:, c * T:(c + 1) * T]
            v.scalar_tensor_tensor(out=x, in0=x, scalar=v1("final_g2", c), in1=PS[:, 3072:4096],
                                   op0=ALU.mult, op1=ALU.mult).then_inc(o_ready, 1)

    block_cm.__exit__(None, None, None)


def chunk_cols(w):
    k, n = w.shape
    return w.reshape(k // P, P, n // P, P).transpose(2, 1, 0, 3).reshape(n // P, P, k)


def pad_unit(u):
    return np.concatenate([u, np.zeros((P, UW - u.shape[1]), u.dtype)], axis=1)


def swap_rope(w):
    r1, r2, c1, c2 = np.split(w, 4, axis=1)
    return np.concatenate([w, r2, r1, c2, c1], axis=1)


def weight_units(a):
    units = []
    w_in = a["w_in"][0]
    cu, cv, cx = chunk_cols(w_in[:, 0:256]), chunk_cols(w_in[:, 256:512]), chunk_cols(w_in[:, 512:768])
    units += [cu[0], cu[1], cx[0], cx[1], cv[0], cv[1]]
    q, k, v = (chunk_cols(w_in[:, o:o + 512]) for o in (768, 1280, 1792))
    for h in range(HEADS_C):
        units += [q[h], k[h], v[h]]
    gate = chunk_cols(a["w_gate"][0])
    pa, pb, pc = (chunk_cols(a[n][0]) for n in ("proj_a", "proj_b", "proj_c"))
    for n in range(KC):
        units += [gate[n], gate[8 + n], gate[16 + n], np.concatenate([pa[n], pb[n], pc[n]], axis=1)]
    units += list(chunk_cols(a["w_out"][0]))
    up = chunk_cols(a["w_up"][0])
    down = chunk_cols(a["w_down"][0])
    f = 0
    for chunks in FF_PASSES:
        for j in range(f, f + chunks):
            units += [up[j], up[FFC + j]]
        units += [pad_unit(down[n][:, f * P:(f + chunks) * P]) for n in range(KC)]
        f += chunks
    m = a["mla_w_in_2"][0]
    units += [chunk_cols(m[:, 256:384])[0], chunk_cols(swap_rope(m[:, 384:448]))[0]]
    units += list(chunk_cols(m[:, 0:256]))
    units += list(chunk_cols(m[:, 448:]))
    wq, wkv = a["mla_w_qup_2"][0], a["mla_w_kvup_2"][0]
    for h in range(HEADS):
        qh = wq[:, h * 192:(h + 1) * 192]
        kv = chunk_cols(wkv[:, h * 256:(h + 1) * 256])
        units.append(pad_unit(np.concatenate(
            [chunk_cols(qh[:, 0:128])[0], chunk_cols(swap_rope(qh[:, 128:192]))[0], kv[0], kv[1]], axis=1)))
    units += list(chunk_cols(a["mla_w_out_2"][0]))
    fno = chunk_cols(a["fno_w_in_2"][0])
    for g in range(FG):
        units += [fno[g], fno[FG + g]]
    units += list(chunk_cols(a["fno_w_out_2"][0]))
    return np.ascontiguousarray(np.stack(units))


def feature_cols(x):
    return x.reshape(-1, P).T


def bucket_rows():
    n = np.arange(GROW)
    rel = (T - 1) - n
    pos = np.maximum(rel, 0)
    f = np.maximum(pos, 1).astype(np.float32)
    large = 16 + (np.log(f / np.float32(16)) / np.float32(math.log(8.0)) * np.float32(16)).astype(np.int32)
    bucket = np.where(pos < 16, pos, np.minimum(large, 31))
    rows = np.zeros((33, GROW), np.float32)
    rows[bucket, n] = 1.0
    rows[32] = np.where(rel < 0, np.float32(-1e30), 0.0)
    return rows


def rope_table():
    inv = (1.0 / (10000.0 ** (np.arange(0, 32, 2, dtype=np.float32) / np.float32(32)))).astype(np.float32)
    t = np.arange(T)
    row, col = (t // 64).astype(np.float32), (t % 64).astype(np.float32)
    ar, ac = inv[:, None] * row[None], inv[:, None] * col[None]
    cos = np.concatenate([np.cos(ar), np.cos(ar), np.cos(ac), np.cos(ac)])
    sin = np.concatenate([-np.sin(ar), np.sin(ar), -np.sin(ac), np.sin(ac)])
    lat = np.concatenate([cos, sin]).astype(np.float32)
    ctx = np.concatenate([np.ones((64, CTX)), np.zeros((64, CTX))]).astype(np.float32)
    return np.concatenate([ctx, lat], axis=1)


def dft_tables():
    t = np.arange(HALF)
    ang = 2 * np.pi * ((t[:, None] * t[None]) % T) / T
    tab = [f(ang).astype(np.float32).reshape(4, P, HALF).transpose(1, 0, 2).reshape(P, 4 * HALF)
           for f in (np.cos, np.sin)]
    d = np.arange(P)
    ang = 2 * np.pi * ((d[:, None] * d[None]) % P) / P
    norm = 1.0 / math.sqrt(T * P)
    csd = np.concatenate([np.cos(ang) * norm, np.sin(ang) * norm], axis=1).astype(np.float32)
    return tab[0], tab[1], csd


def arrays_of(a):
    c = np.ascontiguousarray
    vecs = {
        "attn_g": feature_cols(a["attn_norm_g"]), "b_gate": feature_cols(a["b_gate"]),
        "pool_scale": feature_cols(a["pool_scale"]), "subln": feature_cols(a["diff_subln_g"]),
        "ffn_g": feature_cols(a["ffn_norm_g"]), "conv0": feature_cols(a["conv_w"][0, 0]),
        "conv1": feature_cols(a["conv_w"][0, 1]), "conv2": feature_cols(a["conv_w"][0, 2]),
        "conv_b": feature_cols(a["conv_b"]), "final_g": feature_cols(a["final_norm_g"]),
        "norm_g0": feature_cols(a["norm_g_2"][0]), "norm_g1": feature_cols(a["norm_g_2"][1]),
        "b_both": feature_cols(a["b_ada_2"][0][:2048]),
        "b_lat": feature_cols(np.concatenate([a["b_ada_2"][0][2048:], a["b_ada_2"][1]])),
        "g_qa": feature_cols(a["mla_g_qa_2"]), "g_kva": feature_cols(a["mla_g_kva_2"]),
        "final_g2": feature_cols(a["final_g_2"]),
        "alt": np.where(np.arange(P) % 2, -1.0, 1.0).astype(np.float32)[:, None],
        "pool_inv": np.stack([np.repeat([1 / 2, 1 / 4], 64), np.repeat([1 / 8, 1 / 16], 64)], 1).astype(np.float32),
    }
    edge = np.zeros((P, 32), np.float32)
    t = np.arange(16)
    for g, win in enumerate((2, 4, 8, 16)):
        edge[64 * (g % 2):64 * (g % 2) + 64, 16 * (g // 2):16 * (g // 2) + 16] = 1.0 / np.minimum(t + 1, win)
    ada0 = chunk_rows(a["w_ada_2"][0])
    ada1 = chunk_rows(a["w_ada_2"][1])
    both, lat = ada0[:16], np.concatenate([ada0[16:], ada1])
    ada = np.stack([np.concatenate([both[2 * n:2 * n + 2], lat[4 * n:4 * n + 4]]) for n in range(8)])
    ada = ada.transpose(0, 2, 1, 3).reshape(8, P, 6 * D)
    ctab, stab, csd = dft_tables()
    half = np.eye(64, dtype=np.float32)
    return {
        "x": c(a["x"][0].T.reshape(KC, P, T)),
        "ctx": c(a["ctx_2"][0].T.reshape(KC, P, CTX).transpose(1, 0, 2).reshape(P, KC * CTX)),
        "units": weight_units(a),
        "vec": c(np.concatenate([vecs[n] for n, _ in VEC_PARTS], axis=1)),
        "onehot": bucket_rows(), "rel_bias": c(a["rel_bias"]),
        "ident": np.eye(P, dtype=np.float32),
        "dup": np.block([[half, half], [half, half]]),
        "ln_g": c(a["sgu_ln_g"][0]), "ln_b": c(a["sgu_ln_b"][0]),
        "wst": c(a["sgu_w"][0].transpose(2, 0, 1).reshape(P, 4 * P)),
        "tri": np.triu(np.ones((P, P), np.float32)),
        "sgu_b": c(a["sgu_b"][0]), "pool_w": c(a["pool_w"][0]), "edge": edge,
        "lam": c(a["diff_lam"][0].reshape(256)),
        "c": c(a["c_2"][0]), "c_ctx": c(a["c_ctx_2"]),
        "ada": c(ada),
        "cs": rope_table(), "ctab": ctab, "stab": stab, "csd": csd,
        "altrow": np.where(np.arange(HALF) % 2, -1.0, 1.0).astype(np.float32)[None],
    }


def chunk_rows(w):
    k, n = w.shape
    return w.T.reshape(n // P, P, k)


def kernel(**inputs):
    import concourse.bacc as bacc
    from concourse.bass_utils import run_bass_kernel_spmd as run

    nc = bacc.Bacc("TRN2", target_bir_lowering=False, num_devices=1)
    arrays = arrays_of({k: np.asarray(v) for k, v in inputs.items()})
    t_in = {k: nc.dram_tensor("in_" + k, v.shape, F32, kind="ExternalInput").ap() for k, v in arrays.items()}
    out = nc.dram_tensor("out", (KC, P, T), F32, kind="ExternalOutput").ap()
    build(nc, t_in, out)
    r = run(nc, [{"in_" + k: v for k, v in arrays.items()}], core_ids=[0])
    return r.results[0]["out"].reshape(D, T).T.reshape(1, T, D)
```

```python
import math

import numpy as np

import concourse.bass as bass
from concourse import mybir

F32 = mybir.dt.float32
F32R = mybir.dt.float32r
ALU = mybir.AluOpType
ACT = mybir.ActivationFunctionType
AX = mybir.AxisListType.X

P = 128
T = 1024
D = 1024
KC = D // P
UW = KC * P
CTX = 256
TK = CTX + T
HEADS_C = 4
HEADS = 8
QT_N = T // P
FFC = 22
FF_PASSES = [8, 8, 6]
FG = 8
HALF = T // 2
GROW = T + P
LAM_INIT = 0.8 - 0.6 * math.exp(0.0)
MLA_SCALE = 1.0 / math.sqrt(192.0)

VEC_PARTS = [("attn_g", 8), ("b_gate", 24), ("pool_scale", 2), ("subln", 1), ("ffn_g", 8), ("conv0", 22),
             ("conv1", 22), ("conv2", 22), ("conv_b", 22), ("final_g", 8), ("norm_g0", 8), ("norm_g1", 8),
             ("b_both", 16), ("b_lat", 32), ("g_qa", 2), ("g_kva", 1), ("final_g2", 8), ("alt", 1),
             ("pool_inv", 2)]
VEC = {}
_at = 0
for _name, _n in VEC_PARTS:
    VEC[_name] = _at
    _at += _n
NVEC = _at

NORM = {2: 1, 3: 1, "norm": 1}
PHASES = [
    ("bias", {0: 2, 1: 2, 2: 2, 3: 2}),
    ("norm1", {**NORM, "split": 8, "square": 8}),
    ("xb", {0: 1, 1: 1, "unit": 2}),
    ("va", {2: 1, 3: 1, "unit": 2}),
    ("u", {0: 1, 1: 1, "unit": 2}),
    ("vt", {2: 1, 3: 1}),
    ("pool", {2: 1, 3: 1, "split": 2}),
    ("gmlp", {2: 1, 3: 1, "split": 2}),
    ("diff", {0: 10 * 4, 1: 10 * 4, 2: 9 * 4, 3: 9 * 4, "unit": 12, "split": 4, "norm": 4}),
    ("merge", {0: 16, 1: 16, 2: 8, 3: 8, "unit": 32}),
    ("msplit", {"split": 8}),
    ("out1", {0: 4, 1: 5, "unit": 8, "xnew": 9, "square": 9}),
    ("norm2", {**NORM, "split": 8}),
    ("up0", {0: 8, 1: 8, "unit": 16, "split": 8}),
    ("down0", {2: 4, 3: 4, "unit": 8, "xnew": 8}),
    ("up1", {0: 8, 1: 8, "unit": 16, "split": 8}),
    ("down1", {2: 4, 3: 4, "unit": 8, "xnew": 8}),
    ("up2", {0: 6, 1: 6, "unit": 12, "split": 6}),
    ("down2", {2: 4, 3: 5, "unit": 8, "xnew": 9, "square": 18}),
    ("norm3", {2: 2, 3: 1, "norm": 1, "split": 16}),
    ("cq", {0: 1, 1: 1, "unit": 2}),
    ("cqnorm", {**NORM, "split": 2, "square": 2}),
    ("kvpe", {0: 2, 1: 2, 2: 1, 3: 1, "unit": 2}),
    ("ckvnorm", {2: 2, 3: 1, "norm": 1, "split": 2}),
    ("xscale", {3: 1}),
    ("mgate", {0: 4, 1: 4, "unit": 8}),
    ("heads", {"unit": 8}),
    ("osplit", {"split": 8}),
    ("out2", {0: 4, 1: 5, "unit": 8, "xnew": 9, "square": 9}),
    ("norm4", {**NORM, "split": 8}),
    ("four", {0: 8, 1: 8, 2: 16, 3: 16, "unit": 16}),
    ("ysplit", {"split": 8}),
    ("out3", {0: 4, 1: 5, "unit": 8, "xnew": 9, "square": 9}),
    ("final", {**NORM}),
]


def before(phase, what):
    total = 0
    for name, adds in PHASES:
        if name == phase:
            return total
        total += adds.get(what, 0)
    raise KeyError(phase)


ADA_TURNS = 4
NUNITS = sum(adds.get("unit", 0) for _, adds in PHASES)


class Chain:

    def __init__(self, eng, sem):
        self.eng, self.sem, self.n, self.off = eng, sem, 0, None

    def __call__(self, ins):
        ins.then_inc(self.sem, 1)
        self.n += 1
        self.eng.wait_ge(self.sem, self.n if self.off is None else self.off + self.n)

    def enter(self, i, per):
        self.off, self.per, self.start = i * per, per, self.n

    def leave(self, count):
        assert self.n - self.start == self.per, (self.n - self.start, self.per)
        self.n = self.start + self.per * count
        self.off = None


def build(nc, t_in, out):
    H_AT = 16512
    F_AT = H_AT + 65536
    X_AT = F_AT + 65536
    W_AT = X_AT + 32768
    T_AT = W_AT + 8192 + 16384
    TS = 1040
    C_AT = T_AT + 4 * TS * 4

    def at(name, cols, where, dt=F32, parts=P):
        return nc.alloc_sbuf_tensor_at(name, [parts, cols], dt, offset=where)

    H = at("H", 2 * KC * T, H_AT, F32R)
    w_raw = at("w_raw", 2 * UW, W_AT)
    w_hl = at("w_hl", 2 * 2 * UW, W_AT + 8192, F32R)
    SC = at("SC", 4 * TS, T_AT)
    ACC, SQ, TMP0, TMP1 = (SC[:, s * TS:s * TS + T] for s in range(4))
    TMP = [TMP0, TMP1]
    DIAG = SQ
    X = at("X", KC * T, X_AT)

    place = [C_AT]

    def small(name, cols, dt=F32):
        t = at(name, cols, place[0], dt)
        place[0] += (cols * 4 + 31) // 32 * 32
        return t

    ident = small("ident", P)
    ones = small("ones", P)
    dup = small("dup", P)
    vec = small("vec", NVEC)
    lngb = small("lngb", 512)
    cols = small("cols", 64)
    modb = small("modb", 32)
    modl = small("modl", 32)
    fac0 = small("fac0", 8)
    facc = small("facc", 8)
    fac1 = small("fac1", 8)
    adac = small("adac", 16)
    bn = small("bn", 6)
    lv = small("lv", 256)
    lvp = small("lvp", 64)
    stat = small("stat", 18)
    fstat = small("fstat", 18)
    assert place[0] <= nc.sbuf_usable_end, place[0]

    def v1(name, j=0):
        return vec[:, VEC[name] + j:VEC[name] + j + 1]

    YA = at("YA", 2 * 2 * T, F_AT, F32R)
    YB = at("YB", 2 * 2 * T, F_AT + 16384, F32R)
    OCS = at("OCS", 2 * 4 * T, F_AT + 32768, F32R)
    onehot = at("onehot", GROW, F_AT)
    rb = at("rb", HEADS_C, F_AT + 4608)
    rbx = at("rbx", HEADS_C * P, F_AT + 4640)
    grow = at("grow", HEADS_C * GROW, F_AT + 6688)
    U = at("U", 2 * T, F_AT + 32768)
    VA = at("VA", QT_N * 256, F_AT + 40960)
    PADX = T + 16
    XB = at("XB", 2 * PADX, F_AT + 49152)
    WST = at("WST", 4 * P, F_AT + 57472)
    SGB = at("SGB", 2 * P, F_AT + 59520)
    BD = at("BD", 2 * P, F_AT + 60544)
    EDGE = at("EDGE", 32, F_AT + 61568)
    TRI = at("TRI", P, F_AT + 61728)
    PA = SC[:, 0:2 * PADX]
    PB = at("PB", 2 * PADX, X_AT)
    SA = [at("SA0", T, X_AT), at("SA1", T, X_AT + 4096)]
    SB = [at("SB0", T, X_AT + 8192), ACC]
    AT = at("AT", T, X_AT + 12288)
    QT = at("QT", T, X_AT + 16384)
    KT = at("KT", T, X_AT + 20480)
    VC = at("VC", T, X_AT + 24576)
    BR = at("BR", T, X_AT + 28672)
    OC = TMP1
    M = at("M", KC * T, X_AT)
    XIN = at("XIN", KC * T, F_AT)
    FF = at("FF", 2 * KC * T, F_AT, F32R)
    CL = at("CL", D, X_AT + 16384)
    CC = at("CC", D, X_AT + 20480)
    AW = at("AW", 2 * D, X_AT + 24576)
    UC = at("UC", 2 * KC * CTX, F_AT, F32R)
    CST = at("CST", TK, F_AT + 16384)
    CKR = at("CKR", TK, F_AT + 21504)
    TPE = at("TPE", TK, F_AT + 26624)
    CXR = at("CXR", KC * CTX, F_AT + 57344)
    CXS = at("CXS", KC * CTX, F_AT + 24576)
    DIAGC = at("DIAGC", CTX, F_AT + 31744)
    ACC2 = TMP1
    ACCX = at("ACCX", CTX, H_AT + 61440)
    ACCK = at("ACCK", CTX, F_AT + 64512)
    CQR = at("CQR", 2 * T, F_AT + 49152)
    G = at("G", KC * T, F_AT)
    CQ = at("CQ", 2 * 2 * T, F_AT + 32768, F32R)
    CKV = at("CKV", 2 * TK, F_AT + 49152, F32R)
    KPR = at("KPR", TK, F_AT + 59392)
    QN = at("QN", 2 * T, H_AT, F32R)
    QP = at("QP", 2 * T, H_AT + 8192, F32R)
    KN = at("KN", 2 * TK, H_AT + 16384, F32R)
    KPE = at("KPE", 2 * TK, H_AT + 26624, F32R)
    VN = at("VN", 2 * TK, H_AT + 36864)
    E = at("E", 2 * TK, H_AT + 47104)
    PT = at("PT", TK, H_AT + 57344)
    CSQ = TMP1
    Y = at("Y", KC * T, F_AT)
    CTAB = at("CTAB", 4 * HALF, F_AT + 32768)
    STAB = at("STAB", 4 * HALF, F_AT + 40960)
    CSD = at("CSD", 2 * P, F_AT + 49152)
    M12 = at("M12", 2 * HALF, F_AT + 50176)
    ZEO = at("ZEO", 2 * HALF, F_AT + 54272)
    ZR = at("ZR", T, F_AT + 58368)
    MR = at("MR", P, F_AT + 62464)
    ALT = at("ALT", HALF, F_AT + 62976)

    PS = nc.alloc_psum_tensor("PS", [P, 4096], F32)
    scratch = nc.dram_tensor("bias_scratch", (HEADS_C, P * GROW), F32).ap()
    shifted = bass.AP(scratch.tensor, P - 1, [[P * GROW, HEADS_C], [GROW - 1, P], [1, T]])

    def pair(p, n=T, start=0):
        return PS[:, p * 1024 + start:p * 1024 + start + n]

    sem = nc.alloc_semaphore
    w_in = [sem("w_in0"), sem("w_in1")]
    w_hi = sem("w_hi")
    w_split = sem("w_split")
    w_seen, sc_seen = sem("w_seen"), sem("sc_seen")
    w_used = sem("w_used")
    done = [sem(f"done{p}") for p in range(4)]
    free = [sem(f"free{p}") for p in range(4)]
    hi = sem("hi")
    lo = sem("lo")
    xt = sem("xt")
    sq_added = sem("sq_added")
    acc_ready = sem("acc_ready")
    ms_ready = sem("ms_ready")
    sd_ready = sem("sd_ready")
    diag_ready = sem("diag_ready")
    x_new = sem("x_new")
    sq_ready = sem("sq_ready")
    s_dve, s_act = sem("s_dve"), sem("s_act")
    c_early, c_gm, c_x = sem("c_early"), sem("c_gm"), sem("c_x")
    x_in = [sem(f"x_in{c}") for c in range(KC)]
    memset_done = sem("memset_done")
    g_out = sem("g_out")
    br_in = sem("br_in")
    rbx_ready = sem("rbx_ready")
    u_ready, xb_ready, va_ready = sem("u_ready"), sem("xb_ready"), sem("va_ready")
    va_ms, va_sd = sem("va_ms"), sem("va_sd")
    va_norm, wst_ready, p_ready = sem("va_norm"), sem("wst_ready"), sem("p_ready")
    qkv_ready = sem("qkv_ready")
    neg_ready, exp_ready, aa_ready, at_ready, oc_ready = (
        sem(n) for n in ("neg_ready", "exp_ready", "aa_ready", "at_ready", "oc_ready"))
    lam_sum, lam_exp = sem("lam_sum"), sem("lam_exp")
    sg_ready, m_ready = sem("sg_ready"), sem("m_ready")
    gp_ready, cv_ready, gl_ready = sem("gp_ready"), sem("cv_ready"), sem("gl_ready")
    ada_in = [sem("ada_in0"), sem("ada_in1")]
    ada_used = sem("ada_used")
    ada_seen, cxs_ready = sem("ada_seen"), sem("cxs_ready")
    xdiag_ready = sem("xdiag_ready")
    c_rows, c_silu = sem("c_rows"), sem("c_silu")
    ctx_in, cs_in, csq_in, ft_in = sem("ctx_in"), sem("cs_in"), sem("csq_in"), sem("ft_in")
    tpe_ready = sem("tpe_ready")
    kpe_hi, kpe_lo = sem("kpe_hi"), sem("kpe_lo")
    hp_done = sem("hp_done")
    hq_hi, hq_lo = sem("hq_hi"), sem("hq_lo")
    qp_ready, vn_act, vn_dve = sem("qp_ready"), sem("vn_act"), sem("vn_dve")
    sc_done, mx_ready, ex_ready, e_ready = (
        sem(n) for n in ("sc_done", "mx_ready", "ex_ready", "e_ready"))
    tpa_done, tpb_done, pta, ptb = (sem(n) for n in ("tpa_done", "tpb_done", "pta", "ptb"))
    pv_done, pv_free = sem("pv_done"), sem("pv_free")
    zr_ready, ze_ready, m_evac, mr_ready, qs_ready, sgf_ready, y_ready = (
        sem(n) for n in ("zr_ready", "ze_ready", "m_evac", "mr_ready", "qs_ready", "sgf_ready", "y_ready"))
    gate_ready = sem("gate_ready")
    o_ready, o_out = sem("o_ready"), sem("o_out")

    block_cm = nc.Block()
    block = block_cm.__enter__()

    @block.sync
    def _(sp):
        sp.dma_start(onehot[0:33, :], t_in["onehot"]).then_inc(c_early, 16)
        sp.dma_start(rb[0:32, :], t_in["rel_bias"]).then_inc(c_early, 16)
        sp.dma_start(ident[:, :], t_in["ident"]).then_inc(c_early, 16)
        sp.dma_start(vec[:, :], t_in["vec"]).then_inc(c_early, 16)
        for c in range(KC):
            sp.dma_start(X[:, c * T:(c + 1) * T], t_in["x"][c]).then_inc(x_in[c], 16)
        for u in range(2):
            sp.dma_start(w_raw[:, u * UW:(u + 1) * UW], t_in["units"][u]).then_inc(w_in[u], 16)
        sp.dma_start(lngb[:, 0:256], t_in["ln_g"].partition_broadcast(P)).then_inc(c_gm, 16)
        sp.dma_start(lngb[:, 256:512], t_in["ln_b"].partition_broadcast(P)).then_inc(c_gm, 16)
        sp.dma_start(WST[:, :], t_in["wst"]).then_inc(c_gm, 16)
        sp.dma_start(TRI[:, :], t_in["tri"]).then_inc(c_gm, 16)
        for g in range(4):
            half = slice(64 * (g % 2), 64 * (g % 2) + 64)
            sp.dma_start(SGB[half, (g // 2) * P:(g // 2 + 1) * P],
                         t_in["sgu_b"][g].partition_broadcast(64)).then_inc(c_gm, 16)
        sp.wait_ge(memset_done, 1)
        for g in range(4):
            half = slice(64 * (g % 2), 64 * (g % 2) + 64)
            sp.dma_start(BD[half, (g // 2) * P + 64 * (g % 2):(g // 2) * P + 64 * (g % 2) + 64],
                         t_in["pool_w"][g]).then_inc(c_gm, 16)
        sp.dma_start(EDGE[:, :], t_in["edge"]).then_inc(c_gm, 16)
        sp.dma_start(lv[:, :], t_in["lam"].partition_broadcast(P)).then_inc(c_gm, 16)
        sp.dma_start(dup[:, :], t_in["dup"]).then_inc(c_gm, 16)

        def load_unit(s, number, i=0, per=0):
            sp.wait_ge(w_split, i * per + number - 1)
            sp.dma_start(w_raw[:, s * UW:(s + 1) * UW],
                         t_in["units"][bass.ds(i * per + number, 1)].rearrange("o p n -> p (o n)")
                         ).then_inc(w_in[s], 16)

        ada_units = before("merge", "unit") + 3
        with sp.Fori(0, (ada_units - 3) // 2) as i:
            for s in range(2):
                load_unit(s, 2 + s, i, 2)
        load_unit(0, ada_units - 1)
        sp.wait_ge(lo, before("merge", "split"))
        sp.wait_ge(qkv_ready, 4 * HEADS_C)
        with sp.Fori(0, ADA_TURNS) as i:
            for n in range(4):
                load_unit((n + 1) % 2, ada_units + n, i, 4)
                for k in range(3 * n, 3 * n + 3):
                    sp.wait_ge(ada_used, i * 12 + k + 1)
                    sp.dma_start(AW[:, (k % 2) * D:(k % 2 + 1) * D],
                                 t_in["ada"][bass.ds(i * 12 + k, 1)].rearrange("o p n -> p (o n)")
                                 ).then_inc(ada_in[k % 2], 16)
        load_unit(1, ada_units + 4 * ADA_TURNS)
        with sp.Fori(0, (NUNITS - ada_units - 4 * ADA_TURNS - 1) // 2) as i:
            for s in range(2):
                load_unit(s, ada_units + 4 * ADA_TURNS + 1 + s, i, 2)

    @block.gpsimd
    def _(pool):
        def split_unit(s, number):
            pool.wait_ge(w_in[s], 16 * (number // 2 + 1) if isinstance(number, int) else number)
            hi_part = w_hl[:, s * 2 * UW:s * 2 * UW + UW]
            raw = w_raw[:, s * UW:(s + 1) * UW]
            return hi_part, w_hl[:, s * 2 * UW + UW:(s + 1) * 2 * UW], raw

        for s in range(2):
            hi_part, lo_part, raw = split_unit(s, s)
            pool.tensor_copy(hi_part, raw).then_inc(w_hi, 1)
            pool.wait_ge(w_hi, s + 1)
            pool.tensor_tensor(lo_part, raw, hi_part.bitcast(F32), ALU.subtract).then_inc(w_split, 1)
        with pool.Fori(1, NUNITS // 2) as i:
            for s in range(2):
                pool.wait_ge(w_used, 2 * i + (s - 1))
                hi_part, lo_part, raw = split_unit(s, 16 * i + 16)
                pool.sem_inc(w_seen, 1)
                pool.tensor_copy(hi_part, raw).then_inc(w_hi, 1)
                pool.wait_ge(w_hi, 2 * i + (s + 1))
                pool.tensor_tensor(lo_part, raw, hi_part.bitcast(F32), ALU.subtract).then_inc(w_split, 1)

    @block.tensor
    def _(pe):
        def w(s, part, k):
            return w_hl[:, (2 * s + part) * UW + k * P:(2 * s + part) * UW + (k + 1) * P]

        PASSES = ((0, 0), (0, 1), (1, 0))

        def feature_major(s, src, src_cols, src_chunk, ks, out_at, n=T, w0=0, opens=True, ready=None,
                          k0=0, k1=None, a0=0):
            for k in range(k0, k1 or ks):
                if ready is not None:
                    pe.wait_ge(lo, ready + k + 1)
                for wp, xp in PASSES:
                    for a in range(a0, n, 512):
                        m = min(512, n - a)
                        o = xp * src_cols + src_chunk * k + a
                        mm = pe.matmul(PS[:, out_at + a:out_at + a + m], w(s, wp, w0 + k), src[:, o:o + m],
                                       start=(k == 0 and wp == 0 and xp == 0), stop=(k == ks - 1 and wp == 1))
                        if opens:
                            mm.then_inc(w_used, 1)
                            opens = False
            return mm

        def token_major(s, src, src_cols, src_chunk, ks, out_at, tiles, w0=0, first=0):
            for i in range(tiles):
                for k in range(ks):
                    for n, (xp, wp) in enumerate(PASSES):
                        o = xp * src_cols + src_chunk * k + (first + i) * P
                        mm = pe.matmul(PS[:, out_at + i * P:out_at + (i + 1) * P], src[:, o:o + P],
                                       w(s, wp, w0 + k), start=(k == 0 and n == 0), stop=(k == ks - 1 and n == 2))
            return mm

        def take(p, number):
            pe.wait_ge(free[p], number + 1)

        def norm_sum(idx, p2, parts=((ACC, T),), early=None):
            take(2, p2)
            blocks = [(src[:, j * P:(j + 1) * P], n == T and j >= T // P // 2) for src, n in parts for j in range(n // P)]
            for late in (False, True):
                if late or early is None:
                    pe.wait_ge(acc_ready, idx + 1)
                else:
                    pe.wait_ge(sq_added, early)
                for o, (block_, is_late) in enumerate(blocks):
                    if is_late == late:
                        mm = pe.matmul(PS[:, 2048 + o:2049 + o], block_, ones[:, 0:1], start=True, stop=True)
            mm.then_inc(done[2], 1)

        def norm_spread(idx, p3):
            take(3, p3)
            for a in range(0, T, 512):
                pe.wait_ge(diag_ready, idx * 2 + (a // 512 + 1))
                mm = pe.matmul(PS[:, 3072 + a:3584 + a], ones[:, :], DIAG[:, a:a + 512], start=True, stop=True)
            mm.then_inc(done[3], 1)

        def spread_context(p2):
            take(2, p2)
            pe.matmul(PS[:, 2048:2048 + CTX], ones[:, :], DIAGC[:, :], start=True, stop=True).then_inc(done[2], 1)

        def phase_norm(phase, early=None):
            norm_sum(before(phase, "norm"), before(phase, 2), early=early)
            norm_spread(before(phase, "norm"), before(phase, 3))

        def b(phase, p):
            return before(phase, p)

        pe.wait_ge(rbx_ready, 1)
        for h in range(HEADS_C):
            p = 2 * (h % 2)
            take(p, h // 2)
            take(p + 1, h // 2)
            for a in range(0, GROW, 512):
                m = min(512, GROW - a)
                mm = pe.matmul(PS[:, p * 1024 + a:p * 1024 + a + m], rbx[0:33, h * P:(h + 1) * P],
                               onehot[0:33, a:a + m], start=True, stop=True)
                if a == 512:
                    mm.then_inc(done[p], 1)
            mm.then_inc(done[p + 1], 1)

        phase_norm("norm1")

        def units(phase, p0, ready=None):
            for j in range(2):
                unit = before(phase, "unit") + j
                take(p0 + j, b(phase, p0 + j))
                pe.wait_ge(w_split, unit + 1)
                feature_major(unit % 2, H, KC * T, T, KC, (p0 + j) * 1024, opens=unit > 0,
                              ready=None if j else ready).then_inc(done[p0 + j], 1)
                yield j

        for _ in units("xb", 0, ready=0):
            pass
        for _ in units("va", 2):
            pass
        for turn in units("u", 0):
            if turn == 0:
                for j in range(2):
                    take(2 + j, b("vt", 2 + j))
                    for i in range(QT_N):
                        mm = pe.transpose(PS[:, 2048 + j * 1024 + i * P:2048 + j * 1024 + (i + 1) * P],
                                          TMP[j][:, i * P:(i + 1) * P], ident[:, :])
                    mm.then_inc(done[2 + j], 1)
        pe.wait_ge(c_gm, 16 * 15)
        for j in range(2):
            pe.wait_ge(p_ready, j + 1)
            take(2 + j, b("pool", 2 + j))
            for a in (0, 512):
                mm = pe.matmul(PS[:, 2048 + j * 1024 + a:2048 + j * 1024 + a + 512], BD[:, j * P:(j + 1) * P],
                               XB[:, j * PADX + 16 + a:j * PADX + 16 + a + 512], start=True, stop=True)
            mm.then_inc(done[2 + j], 1)
        def head_unit(h, hh, n, early=0, k0=0, k1=KC):
            p, number = ((0, 0), (1, 0), (0, 1))[n]
            if k0 == 0:
                take(p, h * 10 + (b("diff", p) + number - early))
                pe.wait_ge(w_split, h * 3 + (before("diff", "unit") + n + 1))
            mm = feature_major((before("diff", "unit") + 3 * hh + n) % 2, H, KC * T, T, KC, p * 1024,
                               opens=k0 == 0, k0=k0, k1=k1)
            if k1 == KC:
                mm.then_inc(done[p], 1)

        def scores(h, t):
            n = (t + 1) * P
            for c in range(2):
                take(2 + c, h * 9 + (b("diff", 2 + c) + t))
                for a in range(0, n, 512):
                    m = min(512, n - a)
                    mm = pe.matmul(PS[:, (2 + c) * 1024 + a:(2 + c) * 1024 + a + m],
                                   QT[64 * c:64 * c + 64, t * P:(t + 1) * P],
                                   KT[64 * c:64 * c + 64, a:a + m], start=True, stop=True)
                mm.then_inc(done[2 + c], 1)

        def diff_head(h, hh, last=False):
            head_unit(h, hh, 2, k1=4)
            pe.wait_ge(qkv_ready, h * 4 + 2)
            scores(h, 0)
            head_unit(h, hh, 2, k0=4)
            scores(h, 1)
            pe.wait_ge(qkv_ready, h * 4 + 3)
            take(1, h * 10 + (b("diff", 1) + 1))
            for kb in range(QT_N):
                mm = pe.transpose(PS[:, 1024 + kb * P:1024 + (kb + 1) * P], TMP0[:, kb * P:(kb + 1) * P],
                                  ident[:, :])
            mm.then_inc(done[1], 1)
            for t in range(QT_N):
                swapped = t == QT_N - 1 and not last
                pe.wait_ge(aa_ready, h * 8 + (t + 1))
                take(0, h * 10 + (b("diff", 0) + 2 + t + swapped))
                for kb in range(t + 1):
                    mm = pe.transpose(PS[:, kb * P:(kb + 1) * P], SA[t % 2][:, kb * P:(kb + 1) * P], ident[:, :])
                mm.then_inc(done[0], 1)
                if t + 2 < QT_N:
                    scores(h, t + 2)
                elif t == QT_N - 2 and not last:
                    head_unit(h + 1, hh + 1, 0, early=1)
                if t == 0:
                    pe.wait_ge(qkv_ready, h * 4 + 4)
                pe.wait_ge(at_ready, h * 8 + (t + 1))
                take(1, h * 10 + (b("diff", 1) + 2 + t))
                for kb in range(t + 1):
                    mm = pe.matmul(PS[:, 1024:1024 + P], VC[:, kb * P:(kb + 1) * P], AT[:, kb * P:(kb + 1) * P],
                                   start=(kb == 0), stop=(kb == t))
                mm.then_inc(done[1], 1)
            if not last:
                head_unit(h + 1, hh + 1, 1, k1=4)
            norm_sum(h + before("diff", "norm"), h * 9 + (b("diff", 2) + 8))
            if not last:
                head_unit(h + 1, hh + 1, 1, k0=4)
            norm_spread(h + before("diff", "norm"), h * 9 + (b("diff", 3) + 8))

        for n in range(2):
            head_unit(0, 0, n)
        pe.wait_ge(wst_ready, 1)
        pe.wait_ge(va_norm, QT_N)
        for j in range(2):
            take(2 + j, b("gmlp", 2 + j))
            for i in range(QT_N):
                for g in range(2):
                    mm = pe.matmul(PS[64 * g:64 * g + 64, 2048 + j * 1024 + i * P:2048 + j * 1024 + (i + 1) * P],
                                   VA[:, i * 256 + (2 * j + g) * 64:i * 256 + (2 * j + g) * 64 + 64],
                                   WST[:, (2 * j + g) * P:(2 * j + g + 1) * P], start=True, stop=True)
            mm.then_inc(done[2 + j], 1)
        with pe.Fori(0, HEADS_C // 2 - 1) as i:
            for hh in range(2):
                diff_head(i * 2 + hh, hh)
        diff_head(HEADS_C - 2, 0)
        diff_head(HEADS_C - 1, 1, last=True)

        with pe.Fori(0, KC) as i:
            u0 = before("merge", "unit")
            for j in range(3):
                take(j, i * (2 if j < 2 else 1) + b("merge", j))
                pe.wait_ge(w_split, i * 4 + u0 + j + 1)
                feature_major((u0 + j) % 2, H, KC * T, T, KC, j * 1024).then_inc(done[j], 1)
            pe.wait_ge(w_split, i * 4 + u0 + 4)
            s = (u0 + 3) % 2
            take(3, i + b("merge", 3))
            pe.wait_ge(lo, before("merge", "split"))
            feature_major(s, YA, 2 * T, T, 2, 3072, w0=0).then_inc(done[3], 1)
            take(0, i * 2 + b("merge", 0) + 1)
            feature_major(s, YB, 2 * T, T, 2, 0, w0=2, opens=False).then_inc(done[0], 1)
            take(1, i * 2 + b("merge", 1) + 1)
            feature_major(s, OCS, 4 * T, T, 4, 1024, w0=4, opens=False).then_inc(done[1], 1)

        def project(phase, p0, src, ks, split_base, halves=False):
            u0 = before(phase, "unit")

            def turn(i, s, split=False):
                take(p0 + s, i + b(phase, p0 + s))
                pe.wait_ge(w_split, i * 2 + u0 + s + 1)
                for a in (0, HALF) if split else (None,):
                    feature_major((u0 + s) % 2, src, KC * T, T, ks, (p0 + s) * 1024, opens=not a,
                                  n=T if a is None else a + HALF, a0=a or 0,
                                  ready=None if s else split_base - ks).then_inc(done[p0 + s], 1)

            turns = KC // 2 - halves
            with pe.Fori(0, turns) as i:
                for s in range(2):
                    turn(i, s)
            if halves:
                turn(turns, 0)
                turn(turns, 1, split=True)

        project("out1", 0, H, KC, before("out1", "split"), halves=True)
        phase_norm("norm2", early=before("norm2", "square") - 1)
        for n, chunks in enumerate(FF_PASSES):
            up, down = f"up{n}", f"down{n}"
            with pe.Fori(0, chunks) as i:
                u0 = before(up, "unit")
                for s in range(2):
                    take(s, i + b(up, s))
                    pe.wait_ge(w_split, i * 2 + u0 + s + 1)
                    feature_major((u0 + s) % 2, H, KC * T, T, KC, s * 1024,
                                  ready=None if s or n else before("norm2", "split")).then_inc(done[s], 1)
            project(down, 2, FF, chunks, before(down, "split"), halves=n == len(FF_PASSES) - 1)
        norm_sum(before("norm3", "norm"), before("norm3", 2), ((ACC, T), (ACCX, CTX), (ACC2, T)),
                 early=before("norm3", "square") - 2)
        norm_spread(before("norm3", "norm"), before("norm3", 3))
        spread_context(before("norm3", 2) + 1)

        for j in range(2):
            u = before("cq", "unit") + j
            take(j, b("cq", j))
            pe.wait_ge(w_split, u + 1)
            feature_major(u % 2, H, KC * T, T, KC, j * 1024,
                          ready=None if j else before("norm3", "split")).then_inc(done[j], 1)
        pe.wait_ge(lo, before("norm3", "split") + 16)
        for j in range(2):
            u = before("kvpe", "unit") + j
            take(0, b("kvpe", 0) + j)
            pe.wait_ge(w_split, u + 1)
            feature_major(u % 2, H, KC * T, T, KC, 0).then_inc(done[0], 1)
            take(1, b("kvpe", 1) + j)
            feature_major(u % 2, UC, KC * CTX, CTX, KC, 1024, n=CTX, opens=False).then_inc(done[1], 1)
            if j == 0:
                norm_sum(before("cqnorm", "norm"), before("cqnorm", 2))
            else:
                norm_spread(before("cqnorm", "norm"), before("cqnorm", 3))

        def mgate(i, s):
            take(s, i + b("mgate", s))
            pe.wait_ge(w_split, i * 2 + before("mgate", "unit") + s + 1)
            feature_major((before("mgate", "unit") + s) % 2, H, KC * T, T, KC, s * 1024).then_inc(done[s], 1)

        mgate(0, 0)
        pe.wait_ge(tpe_ready, 2)
        take(2, b("kvpe", 2))
        for a in (0, 512):
            mm = pe.matmul(PS[:, 2048 + a:2560 + a], dup[:, :], TPE[:, CTX + a:CTX + a + 512], start=True, stop=True)
        mm.then_inc(done[2], 1)
        take(3, b("kvpe", 3))
        pe.matmul(PS[:, 3072:3072 + CTX], dup[:, :], TPE[:, 0:CTX], start=True, stop=True).then_inc(done[3], 1)
        mgate(0, 1)
        norm_sum(before("ckvnorm", "norm"), before("ckvnorm", 2), ((ACC, T), (ACCK, CTX)))
        mgate(1, 0)
        norm_spread(before("ckvnorm", "norm"), before("ckvnorm", 3))
        spread_context(before("ckvnorm", 2) + 1)
        mgate(1, 1)
        pe.wait_ge(xdiag_ready, 1)
        take(3, b("xscale", 3))
        for a in (0, 512):
            mm = pe.matmul(PS[:, 3072 + a:3584 + a], ones[:, :], DIAG[:, a:a + 512], start=True, stop=True)
        mm.then_inc(done[3], 1)
        with pe.Fori(2, KC // 2) as i:
            for s in range(2):
                mgate(i, s)

        hu = before("heads", "unit")

        def head_queries(h, hh):
            s = (hu + hh) % 2
            pe.wait_ge(w_split, h + hu + 1)
            feature_major(s, CQ, 2 * T, T, 2, 0, w0=0).then_inc(hp_done, 1)
            for n, (wp, xp) in enumerate(PASSES):
                mm = pe.matmul(PS[:, 1024:1024 + CTX], w(s, wp, 4), CKV[:, xp * TK + T:xp * TK + TK],
                               start=(n == 0), stop=(n == 2))
            mm.then_inc(hp_done, 1)

        def head_keys(h, hh):
            s = (hu + hh) % 2
            feature_major(s, CKV, TK, TK, 1, 1536, n=T, w0=4, opens=False).then_inc(hp_done, 1)
            pe.wait_ge(hq_lo, h * 4 + 1)
            feature_major(s, CQ, 2 * T, T, 2, 0, w0=2, opens=False).then_inc(hp_done, 1)

        def head_values(h, hh):
            s = (hu + hh) % 2
            pe.wait_ge(hq_lo, h * 4 + 3)
            token_major(s, CKV, TK, TK, 1, 1536, 10, w0=5).then_inc(hp_done, 1)

        def mla_scores(t):
            base = 1536 * (t % 2)
            for a in range(0, TK, 512):
                m = min(512, TK - a)
                for n, (qp_, kp_) in enumerate(PASSES):
                    pe.matmul(PS[:, base + a:base + a + m], QN[:, qp_ * T + t * P:qp_ * T + (t + 1) * P],
                              KN[:, kp_ * TK + a:kp_ * TK + a + m], start=(n == 0), stop=False)
                for n, (qp_, kp_) in enumerate(PASSES):
                    mm = pe.matmul(PS[:, base + a:base + a + m], QP[:, qp_ * T + t * P:qp_ * T + (t + 1) * P],
                                   KPE[:, kp_ * TK + a:kp_ * TK + a + m], start=False, stop=(n == 2))
            mm.then_inc(sc_done, 1)

        def first_scores(h):
            pe.wait_ge(hq_lo, h * 4 + 4)
            mla_scores(0)
            pe.wait_ge(vn_act, h * 2 + 2)
            pe.wait_ge(vn_dve, h + 1)
            mla_scores(1)

        def transposes(t, blocks, bank):
            for kb in range(*blocks):
                mm = pe.transpose(PS[:, bank + (kb - blocks[0]) * P:bank + (kb - blocks[0] + 1) * P],
                                  E[:, (t % 2) * TK + kb * P:(t % 2) * TK + (kb + 1) * P], ident[:, :])
            return mm

        def mla_head(h, hh, last=False):
            for t in range(QT_N):
                tg = h * 8 + t
                pe.wait_ge(e_ready, tg + 1)
                pe.wait_ge(pta, tg * 2 + 1)
                transposes(t, (0, 4), 3072).then_inc(tpa_done, 1)
                pe.wait_ge(pv_free, tg + 1)
                transposes(t, (4, 8), 3584).then_inc(tpb_done, 1)
                if t + 2 < QT_N:
                    mla_scores(t + 2)
                elif not last:
                    (head_queries if t == QT_N - 2 else head_keys)(h + 1, 1 - hh)
                pe.wait_ge(pta, tg * 2 + 2)
                transposes(t, (8, 10), 3072).then_inc(tpa_done, 1)
                pe.wait_ge(ptb, tg + 2)
                for kb in range(10):
                    if kb == 8:
                        pe.wait_ge(pta, tg * 2 + 3)
                    mm = pe.matmul(PS[:, 3584:3584 + P], VN[:, hh * TK + kb * P:hh * TK + (kb + 1) * P],
                                   PT[:, kb * P:(kb + 1) * P], start=(kb == 0), stop=(kb == 9))
                mm.then_inc(pv_done, 1)
            if not last:
                head_values(h + 1, 1 - hh)
                first_scores(h + 1)

        for p in range(4):
            take(p, b("heads", p))
        pe.wait_ge(lo, before("mgate", "split"))
        head_queries(0, 0)
        head_keys(0, 0)
        head_values(0, 0)
        pe.wait_ge(kpe_lo, 1)
        first_scores(0)
        with pe.Fori(0, HEADS // 2 - 1) as i:
            for hh in range(2):
                mla_head(i * 2 + hh, hh)
        mla_head(HEADS - 2, 0)
        mla_head(HEADS - 1, 1, last=True)
        pe.wait_ge(pv_free, 65)
        pe.wait_ge(pta, 129)
        pe.wait_ge(ptb, 65)
        project("out2", 0, H, KC, before("out2", "split"), halves=True)
        phase_norm("norm4", early=before("norm4", "square") - 1)

        pe.wait_ge(ft_in, 16 * 4)
        with pe.Fori(0, FG) as i:
            u0 = before("four", "unit")
            for s in range(2):
                take(s, i + b("four", s))
                pe.wait_ge(w_split, i * 2 + u0 + s + 1)
                if s == 0:
                    feature_major(u0 % 2, H, KC * T, T, KC, 0, ready=before("norm4", "split")).then_inc(done[0], 1)
                else:
                    feature_major((u0 + 1) % 2, H, KC * T, T, KC, 1024, k1=6)
            pe.wait_ge(ze_ready, i * 2 + 2)
            take(2, i * 2 + b("four", 2))
            for q in range(2):
                for k in range(4):
                    mm = pe.matmul(PS[:, 2048 + q * 512 + k * P:2048 + q * 512 + (k + 1) * P],
                                   ZEO[:, q * HALF + k * P:q * HALF + (k + 1) * P], CSD[:, q * P:(q + 1) * P],
                                   start=True, stop=True)
            mm.then_inc(done[2], 1)
            take(3, i * 2 + b("four", 3))
            pe.matmul(PS[0:1, 3072:3072 + P], ZR[:, HALF:HALF + 1], CSD[:, 0:P], start=True, stop=True
                      ).then_inc(done[3], 1)
            feature_major((u0 + 1) % 2, H, KC * T, T, KC, 1024, opens=False, k0=6).then_inc(done[1], 1)
            pe.wait_ge(m_evac, i * 2 + 2)
            pe.wait_ge(mr_ready, i + 1)
            take(3, i * 2 + b("four", 3) + 1)
            for k in range(4):
                pe.matmul(PS[:, 3072:3584], M12[:, k * P:(k + 1) * P], CTAB[:, k * HALF:(k + 1) * HALF],
                          start=(k == 0), stop=False)
            pe.matmul(PS[:, 3072:3584], MR[0:1, :], ALT[0:1, :], start=False, stop=True)
            for k in range(4):
                mm = pe.matmul(PS[:, 3584:4096], M12[:, HALF + k * P:HALF + (k + 1) * P],
                               STAB[:, k * HALF:(k + 1) * HALF], start=(k == 0), stop=(k == 3))
            mm.then_inc(done[3], 1)
            take(2, i * 2 + b("four", 2) + 1)
            for k in range(4):
                pe.matmul(PS[:, 2048:2049], M12[:, k * P:(k + 1) * P], v1("alt"), start=(k == 0), stop=False)
            pe.matmul(PS[:, 2048:2049], MR[0:1, :], ones[0:1, 0:1], start=False, stop=True).then_inc(done[2], 1)
        project("out3", 0, H, KC, before("out3", "split"), halves=True)
        phase_norm("final", early=before("final", "square") - 1)

    @block.scalar
    def _(act):
        chain = Chain(act, s_act)

        def norm(idx, eps_cols):
            act.wait_ge(ms_ready, idx + 1)
            act.activation(stat[:, 0:eps_cols], stat[:, 0:eps_cols], ACT.Sqrt).then_inc(sd_ready, 1)

        def phase_norm(phase, n=T):
            norm(before(phase, "norm"), n // P)

        for c in range(KC):
            act.wait_ge(x_in[c], 16)
            if c >= 2:
                act.wait_ge(sq_added, c - 1)
            act.activation((SQ, TMP0)[c % 2], X[:, c * T:(c + 1) * T], ACT.Square).then_inc(sq_ready, 1)
            if c % 2:
                h = c // 2
                p = 2 * (h % 2)
                act.wait_ge(done[p], h // 2 + 1)
                act.wait_ge(done[p + 1], h // 2 + 1)
                row = grow[:, h * GROW:(h + 1) * GROW]
                chain(act.activation(row, PS[:, p * 1024:p * 1024 + GROW], ACT.Copy))
                act.sem_inc(free[p], 1)
                act.sem_inc(free[p + 1], 1)
                act.dma_start(scratch[h].rearrange("(p n) -> p n", p=P), row).then_inc(g_out, 16)
        phase_norm("norm1")
        xts = [0]

        def hi_blocks(dst, size, count, shift=None):
            for c in range(count):
                xts[0] += 1
                act.wait_ge(xt, xts[0])
                o, t = dst[:, c * size:(c + 1) * size], TMP[c % 2][:, 0:size]
                if shift is None:
                    ins = act.activation(o, t, ACT.Copy)
                else:
                    ins = act.activation(o, t, ACT.Identity, bias=shift(c))
                ins.then_inc(hi, 1)

        hi_blocks(H, T, KC)
        for j in range(2):
            act.wait_ge(done[j], before("xb", j) + 1)
            chain(act.activation(XB[:, j * PADX + 16:j * PADX + 16 + T], pair(j), ACT.Copy))
            act.sem_inc(free[j], 1)
            act.sem_inc(xb_ready, 1)
        act.wait_ge(lam_sum, 1)
        act.activation(cols[:, 2:4], cols[:, 0:2], ACT.Exp).then_inc(lam_exp, 1)
        for j in range(2):
            act.wait_ge(done[2 + j], before("va", 2 + j) + 1)
            act.wait_ge(lo, before("xb", "split"))
            chain(act.activation(TMP[j], pair(2 + j), ACT.Gelu))
            act.sem_inc(free[2 + j], 1)
        for j in range(2):
            act.wait_ge(done[j], before("u", j) + 1)
            chain(act.activation(U[:, j * T:(j + 1) * T], pair(j), ACT.Gelu))
            act.sem_inc(free[j], 1)
            act.sem_inc(u_ready, 1)
            if j == 0:
                for k in range(2):
                    act.wait_ge(done[2 + k], before("vt", 2 + k) + 1)
                    dst = VA[:, :].rearrange("p (i c) -> p i c", i=QT_N)[:, :, k * P:(k + 1) * P]
                    chain(act.activation(dst, pair(2 + k).rearrange("p (i c) -> p i c", i=QT_N), ACT.Copy))
                    act.sem_inc(free[2 + k], 1)
                    act.sem_inc(va_ready, 1)
        act.wait_ge(va_ms, 1)
        act.activation(stat[:, 0:QT_N], stat[:, 0:QT_N], ACT.Sqrt).then_inc(va_sd, 1)
        act.wait_ge(g_out, 16 * HEADS_C)
        for j in range(2):
            act.wait_ge(done[2 + j], before("pool", 2 + j) + 1)
            act.activation(YB[:, j * T:(j + 1) * T], pair(2 + j), ACT.Copy, scale=v1("pool_scale", j)).then_inc(hi, 1)
        for j in range(2):
            xts[0] += 1
            act.wait_ge(xt, xts[0])
            act.activation(YA[:, j * T:(j + 1) * T], TMP[j], ACT.Copy).then_inc(hi, 1)

        act.wait_ge(lo, before("diff", "split"))

        def load_bias(h):
            act.dma_start(BR[:, :], shifted[bass.ds(h, 1)].rearrange("o p n -> p (o n)")).then_inc(br_in, 16)

        def evacuate(h, n, early=0):
            dst, p, number = ((QT[:, :], 0, 1), (KT[:, :], 1, 1), (TMP0, 0, 2), (VC[:, :], 1, 2))[n]
            act.wait_ge(done[p], h * 10 + (before("diff", p) + number - early))
            act.activation(dst, pair(p), ACT.Copy, scale=1.0 if n else 0.125).then_inc(qkv_ready, 1)
            act.wait_ge(qkv_ready, h * 4 + (n + 1))
            act.sem_inc(free[p], 1)

        def exps(h, t):
            n = (t + 1) * P
            act.wait_ge(neg_ready, h * 8 + (t + 1))
            for c, S in enumerate((SA[t % 2], SB[t % 2])):
                o = 2 * (t % 2) + c
                act.activation(S[:, 0:n], S[:, 0:n], ACT.Exp, bias=cols[:, 8 + o:9 + o],
                               accum_out=cols[:, 50 + o:51 + o]).then_inc(exp_ready, 1)

        def diff_head(h, last=False):
            exps(h, 0)
            act.wait_ge(lo, h + before("diff", "split"))
            evacuate(h, 2)
            exps(h, 1)
            evacuate(h, 3)
            for t in range(QT_N):
                n = (t + 1) * P
                swapped = t == QT_N - 1 and not last
                if swapped:
                    evacuate(h + 1, 0, early=1)
                act.wait_ge(done[0], h * 10 + (before("diff", 0) + 3 + t + swapped))
                act.activation(AT[:, 0:n], PS[:, 0:n], ACT.Copy).then_inc(at_ready, 1)
                act.wait_ge(at_ready, h * 8 + (t + 1))
                act.sem_inc(free[0], 1)
                if t + 3 < QT_N:
                    exps(h, t + 2)
                elif t == QT_N - 2:
                    exps(h, t + 1)
                if t + 2 == QT_N and not last:
                    load_bias(h + 1)
            act.wait_ge(oc_ready, h * 8 + 8)
            act.activation(ACC, OC, ACT.Square).then_inc(acc_ready, 1)
            norm(h + before("diff", "norm"), QT_N)
            if not last:
                evacuate(h + 1, 1)
            act.wait_ge(xt, h + (xts[0] + 1))
            act.activation(OCS[:, bass.ds(h * T, T)], TMP0, ACT.Copy).then_inc(hi, 1)

        load_bias(0)
        for n in range(2):
            evacuate(0, n)
        with act.Fori(0, HEADS_C // 2 - 1) as i:
            for hh in range(2):
                diff_head(i * 2 + hh)
        diff_head(HEADS_C - 2)
        diff_head(HEADS_C - 1, last=True)
        xts[0] += 4

        act.wait_ge(lo, before("merge", "split"))
        act.dma_start(CL[:, :], t_in["c"].partition_broadcast(P)).then_inc(c_rows, 16)
        act.dma_start(CC[:, :], t_in["c_ctx"].partition_broadcast(P)).then_inc(c_rows, 16)
        act.wait_ge(c_rows, 32)
        act.activation(CL[:, :], CL[:, :], ACT.Silu).then_inc(c_silu, 1)
        act.activation(CC[:, :], CC[:, :], ACT.Silu).then_inc(c_silu, 1)

        with act.Fori(0, KC) as i:
            for j in range(3):
                act.wait_ge(done[j], i * (2 if j < 2 else 1) + before("merge", j) + 1)
                act.wait_ge(m_ready, i * 3 + j + 1)
                act.activation(SC[:, j * TS:j * TS + T], pair(j), ACT.Sigmoid,
                               bias=vec[:, bass.ds(i + (VEC["b_gate"] + 8 * j), 1)]).then_inc(sg_ready, 1)
                act.wait_ge(sg_ready, i * 3 + j + 1)
                act.sem_inc(free[j], 1)

        def hi_chunk(src, i):
            act.activation(H[:, bass.ds(i * T, T)], src[:, bass.ds(i * T, T)], ACT.Copy).then_inc(hi, 1)

        act.wait_ge(m_ready, 3 * KC)
        with act.Fori(0, KC - 1) as i:
            hi_chunk(M, i)
        act.wait_ge(done[1], before("out1", 1))
        for c in range(KC):
            act.dma_start(XIN[:, c * T:(c + 1) * T], t_in["x"][c]).then_inc(c_x, 16)
        act.wait_ge(m_ready, 3 * KC + 3)
        hi_chunk(M, KC - 1)

        def residual(phase, gain=None):
            def square(i, s, half=0, size=T):
                x = X[:, bass.ds(i * (2 * T) + (s * T + half * HALF), size)]
                act.wait_ge(x_new, i * 2 + before(phase, "xnew") + s + half + 1)
                act.activation(SQ[:, half * HALF:half * HALF + size], x, ACT.Square).then_inc(sq_ready, 1)
                if gain:
                    act.activation(TMP0[:, half * HALF:half * HALF + size], x, ACT.Square,
                                   scale=vec[:, bass.ds(i * 2 + (VEC[gain] + s), 1)]).then_inc(sq_ready, 1)

            last = KC // 2 - 1
            with act.Fori(0, last) as i:
                for s in range(2):
                    square(i, s)
            square(last, 0)
            for half in range(2):
                square(last, 1, half, HALF)

        residual("out1")
        phase_norm("norm2")
        hi_blocks(H, T, KC)

        f0 = 0
        for n, chunks in enumerate(FF_PASSES):
            up = f"up{n}"
            if n == len(FF_PASSES) - 1:
                assert chunks <= KC - 2
                for p in (2, 3):
                    act.wait_ge(done[p], before(up, p))
                act.dma_start(CXR[:, :], t_in["ctx"]).then_inc(ctx_in, 16)
            with act.Fori(0, chunks) as i:
                act.wait_ge(done[0], i + before(up, 0) + 1)
                act.wait_ge(cv_ready, i + f0 + 1)
                act.activation(SC[:, 2:2 + T], pair(0), ACT.Copy).then_inc(gp_ready, 1)
                act.wait_ge(gp_ready, i + f0 + 1)
                act.sem_inc(free[0], 1)
                act.wait_ge(cv_ready, i + f0 + 2)
                act.activation(SC[:, 2 * TS:2 * TS + T], SC[:, TS:TS + T], ACT.Gelu,
                               bias=vec[:, bass.ds(i + (VEC["conv_b"] + f0), 1)]).then_inc(gl_ready, 1)
                act.wait_ge(xt, i + xts[0] + 1)
                act.activation(FF[:, bass.ds(i * T, T)], SC[:, 3 * TS:3 * TS + T], ACT.Copy).then_inc(hi, 1)
            xts[0] += chunks
            f0 += chunks
        act.wait_ge(ctx_in, 16)
        act.activation(CXS[:, :], CXR[:, :], ACT.Square).then_inc(cxs_ready, 1)
        residual("down2", gain="final_g")
        act.wait_ge(done[3], before("norm3", 3))
        act.dma_start(CST[:, :], t_in["cs"]).then_inc(cs_in, 16)
        act.wait_ge(ms_ready, before("norm3", "norm") + 1)
        act.activation(fstat[:, :], stat[:, :], ACT.Sqrt).then_inc(sd_ready, 1)
        hi_blocks(H, T, KC, lambda c: modb[:, c:c + 1])
        hi_blocks(UC, CTX, KC, lambda c: modb[:, 16 + c:17 + c])
        for j in range(2):
            act.wait_ge(done[j], before("cq", j) + 1)
            chain(act.activation(CQR[:, j * T:(j + 1) * T], pair(j), ACT.Copy))
            act.sem_inc(free[j], 1)
            if j:
                act.wait_ge(sq_added, before("cqnorm", "square") + 1)
            act.activation(SQ, CQR[:, j * T:(j + 1) * T], ACT.Square).then_inc(sq_ready, 1)
        act.wait_ge(done[0], before("kvpe", 0) + 1)
        chain(act.activation(CKR[:, 0:T], pair(0), ACT.Copy))
        act.sem_inc(free[0], 1)
        act.wait_ge(done[1], before("kvpe", 1) + 1)
        chain(act.activation(CKR[:, T:TK], pair(1, CTX), ACT.Copy))
        act.sem_inc(free[1], 1)
        phase_norm("cqnorm")
        chain(act.activation(ACCK[:, :], CKR[:, T:TK], ACT.Square))
        chain(act.activation(ACC, CKR[:, 0:T], ACT.Square))
        act.sem_inc(acc_ready, 1)
        hi_blocks(CQ, T, 2)

        def mgate(i, s):
            act.wait_ge(done[s], i + before("mgate", s) + 1)
            act.activation(G[:, bass.ds(i * (2 * T) + s * T, T)], pair(s), ACT.Silu).then_inc(gate_ready, 1)
            act.wait_ge(gate_ready, i * 2 + s + 1)
            act.sem_inc(free[s], 1)

        mgate(0, 0)
        act.wait_ge(done[2], before("kvpe", 2) + 1)
        chain(act.activation(KPR[:, 0:T], pair(2), ACT.Copy))
        act.sem_inc(free[2], 1)
        act.wait_ge(done[3], before("kvpe", 3) + 1)
        chain(act.activation(KPR[:, T:TK], pair(3, CTX), ACT.Copy))
        act.sem_inc(free[3], 1)
        mgate(0, 1)
        norm(before("ckvnorm", "norm"), TK // P)
        mgate(1, 0)
        for a, n in ((0, T), (T, CTX)):
            xts[0] += 1
            act.wait_ge(xt, xts[0])
            act.activation(CKV[:, a:a + n], TMP[a // T][:, 0:n], ACT.Copy).then_inc(hi, 1)
        mgate(1, 1)
        act.wait_ge(lo, before("mgate", "split"))
        with act.Fori(2, KC // 2) as i:
            for s in range(2):
                mgate(i, s)
        act.dma_start(CSQ, t_in["cs"][:, CTX:TK]).then_inc(csq_in, 16)
        act.activation(KPE[:, 0:TK], KPR[:, :], ACT.Copy).then_inc(kpe_hi, 1)

        def hi_part(dst, src_at, n, count, at_=0):
            act.wait_ge(hp_done, count)
            act.activation(dst[:, at_:at_ + n], PS[:, src_at:src_at + n], ACT.Copy).then_inc(hq_hi, 1)

        def head_end(h, hh):
            act.wait_ge(qp_ready, h + 1)
            act.activation(QP[:, 0:T], TMP0, ACT.Copy).then_inc(hq_hi, 1)
            act.wait_ge(hp_done, h * 5 + 5)
            act.activation(VN[:, hh * TK:hh * TK + 512], PS[:, 1536:2048], ACT.Copy).then_inc(vn_act, 1)
            act.activation(VN[:, hh * TK + 1024:hh * TK + TK], PS[:, 2560:2560 + CTX], ACT.Copy).then_inc(vn_act, 1)
            mla_exp(h, 0)
            mla_exp(h, 1)

        def mla_exp(h, t):
            act.wait_ge(mx_ready, h * 8 + t + 1)
            base = 1536 * (t % 2)
            act.activation(E[:, (t % 2) * TK:(t % 2) * TK + TK], PS[:, base:base + TK], ACT.Exp,
                           bias=cols[:, 16 + t % 2:17 + t % 2], scale=MLA_SCALE,
                           accum_out=cols[:, 18 + t % 2:19 + t % 2]).then_inc(ex_ready, 1)

        def mla_head(h, hh, last=False):
            for t in range(QT_N):
                tg = h * 8 + t
                act.wait_ge(tpa_done, tg * 2 + 1)
                act.activation(PT[:, 0:512], PS[:, 3072:3584], ACT.Copy).then_inc(pta, 1)
                if t == QT_N - 2 and not last:
                    hi_part(QN, 0, T, h * 5 + 6)
                    hi_part(KN, 1024, CTX, h * 5 + 7, T)
                if t == QT_N - 1 and not last:
                    hi_part(KN, 1536, T, h * 5 + 8)
                act.wait_ge(tpa_done, tg * 2 + 2)
                act.activation(PT[:, 1024:TK], PS[:, 3072:3328], ACT.Copy).then_inc(pta, 1)
                if t + 2 < QT_N:
                    mla_exp(h, t + 2)
            if not last:
                head_end(h + 1, 1 - hh)

        hi_part(QN, 0, T, 1)
        hi_part(KN, 1024, CTX, 2, T)
        hi_part(KN, 1536, T, 3)
        head_end(0, 0)
        with act.Fori(0, HEADS // 2 - 1) as i:
            for hh in range(2):
                mla_head(i * 2 + hh, hh)
        mla_head(HEADS - 2, 0)
        mla_head(HEADS - 1, 1, last=True)
        act.wait_ge(pv_free, 65)
        with act.Fori(0, KC) as i:
            hi_chunk(G, i)

        act.dma_start(CTAB[:, :], t_in["ctab"]).then_inc(ft_in, 16)
        act.dma_start(STAB[:, :], t_in["stab"]).then_inc(ft_in, 16)
        act.dma_start(CSD[:, :], t_in["csd"]).then_inc(ft_in, 16)
        act.dma_start(ALT[0:1, :], t_in["altrow"]).then_inc(ft_in, 16)
        residual("out2")
        phase_norm("norm4")
        hi_blocks(H, T, KC, lambda c: modl[:, 8 + c:9 + c])

        def fourier(i, last=False):
            act.wait_ge(done[0], i + before("four", 0) + 1)
            act.activation(ZR[:, :], pair(0), ACT.Copy).then_inc(zr_ready, 1)
            act.wait_ge(zr_ready, i + 1)
            act.sem_inc(free[0], 1)
            act.wait_ge(done[2], i * 2 + before("four", 2) + 1)
            act.activation(M12[:, 0:HALF], PS[:, 2048:2560], ACT.Copy).then_inc(m_evac, 1)
            act.wait_ge(done[3], i * 2 + before("four", 3) + 1)
            act.activation(MR[0:1, :], PS[0:1, 3072:3072 + P], ACT.Copy).then_inc(mr_ready, 1)
            act.wait_ge(mr_ready, i + 1)
            act.sem_inc(free[3], 1)
            act.wait_ge(done[1], i + before("four", 1) + 1)
            act.wait_ge(y_ready, i * 2 + 1)
            act.activation(TMP1, pair(1), ACT.Silu).then_inc(sgf_ready, 1)
            act.wait_ge(sgf_ready, i + 1)
            act.sem_inc(free[1], 1)
            if last:
                with act.Fori(0, KC - 1) as c:
                    hi_chunk(Y, c)
            act.wait_ge(done[3], i * 2 + before("four", 3) + 2)
            act.activation(TMP0[:, 0:HALF], PS[:, 3584:4096], ACT.Copy).then_inc(qs_ready, 1)

        with act.Fori(0, FG - 1) as i:
            fourier(i)
        fourier(FG - 1, last=True)
        act.wait_ge(y_ready, 2 * FG + 1)
        hi_chunk(Y, KC - 1)
        residual("out3")
        phase_norm("final")
        for c in range(KC):
            act.wait_ge(o_ready, c + 1)
            act.dma_start(out[c], X[:, c * T:(c + 1) * T]).then_inc(o_out, 16)
        act.wait_ge(o_out, 16 * KC)

    @block.vector
    def _(v):
        chain = Chain(v, s_dve)
        for p in range(4):
            v.sem_inc(free[p], 1)
        for s in (pv_free, pta, ptb):
            v.sem_inc(s, 1)
        v.sem_inc(m_ready, 3)
        v.sem_inc(cv_ready, 1)
        v.sem_inc(y_ready, 1)
        xts = [0]
        his = [0]
        sqs = [0]

        chain(v.memset(ones[:, :], 1.0))
        v.memset(BD[:, :], 0.0).then_inc(memset_done, 1)
        chain(v.memset(XB[:, :], 0.0))
        v.wait_ge(c_early, 64)
        chain(v.memset(rbx[32:33, :], 1.0))
        chain(v.tensor_copy(rbx[0:32, :].rearrange("p (h n) -> p h n", h=HEADS_C),
                            rb[0:32, :].unsqueeze(2).to_broadcast([32, HEADS_C, P])))
        v.sem_inc(rbx_ready, 1)
        def add_squares(count, n=T, bufs=(SQ, SQ)):
            for c in range(count):
                sqs[0] += 1
                v.wait_ge(sq_ready, sqs[0])
                if c == 0:
                    ins = v.tensor_copy(ACC[:, 0:n], bufs[0][:, 0:n])
                else:
                    ins = v.tensor_tensor(ACC[:, 0:n], ACC[:, 0:n], bufs[c % 2][:, 0:n], ALU.add)
                ins.then_inc(sq_added, 1)
                acs[0] += 1
                v.wait_ge(sq_added, acs[0])
            v.sem_inc(acc_ready, 1)

        acs = [0]

        def scale_diagonal(phase, width, n, eps=1e-6):
            norm_scale(before(phase, "norm"), before(phase, 2), None, n, width, eps)

        def norm_scale(idx, p2, p3, n, width, eps):
            k = n // P
            v.wait_ge(done[2], p2 + 1)
            v.tensor_scalar(stat[:, 0:k], PS[:, 2048:2048 + k], 1.0 / width, eps, ALU.mult, ALU.add
                            ).then_inc(ms_ready, 1)
            v.wait_ge(ms_ready, idx + 1)
            v.sem_inc(free[2], 1)
            v.wait_ge(sd_ready, idx + 1)
            chain(v.reciprocal(stat[:, 0:k], stat[:, 0:k]))
            if n == TK:
                chain(diagonal(DIAGC[:, :], stat, T // P, k))
            for a in (0, 4):
                diagonal(DIAG[:, a * P:(a + 4) * P], stat, a, a + 4).then_inc(diag_ready, 1)
            if p3 is not None:
                v.wait_ge(done[3], p3 + 1)

        def diagonal(dst, src, a, b):
            return v.tensor_tensor(dst.rearrange("p (j c) -> p j c", j=b - a),
                                   ident[:, :].unsqueeze(1).to_broadcast([P, b - a, P]),
                                   src[:, a:b].unsqueeze(2).to_broadcast([P, b - a, P]), ALU.mult)

        def phase_scale(phase, width, eps, n=T):
            norm_scale(before(phase, "norm"), before(phase, 2), before(phase, 3), n, width, eps)

        def apply_split(dst, dst_cols, src, count, n, gain, shift=None, scales=3):
            def make(c):
                v.scalar_tensor_tensor(out=TMP[c % 2][:, 0:n], in0=src[:, c * n:(c + 1) * n], scalar=gain(c),
                                       in1=pair(scales, n), op0=ALU.mult, op1=ALU.mult).then_inc(xt, 1)

            def low(c):
                his[0] += 1
                v.wait_ge(xt, xts[0] + c + 1)
                v.wait_ge(hi, his[0])
                h = dst[:, c * n:(c + 1) * n].bitcast(F32)
                l, t = dst[:, dst_cols + c * n:dst_cols + (c + 1) * n], TMP[c % 2][:, 0:n]
                if shift is None:
                    ins = v.tensor_tensor(l, t, h, ALU.subtract)
                else:
                    ins = v.scalar_tensor_tensor(out=l, in0=t, scalar=shift(c), in1=h, op0=ALU.add, op1=ALU.subtract)
                ins.then_inc(lo, 1)
                v.wait_ge(lo, his[0])

            make(0)
            for c in range(count):
                if c + 1 < count:
                    make(c + 1)
                low(c)
            v.sem_inc(free[scales], 1)
            xts[0] += count

        add_squares(KC, bufs=(SQ, TMP0))
        for c in range(KC):
            v.wait_ge(x_in[c], 16)
        phase_scale("norm1", D, 1e-6)
        apply_split(H, KC * T, X, KC, T, lambda c: v1("attn_g", c))

        v.wait_ge(c_gm, 16 * 15)
        for q in range(2):
            chain(v.tensor_tensor(lvp[:, :], lv[:, 128 * q:128 * q + 64], lv[:, 128 * q + 64:128 * q + 128], ALU.mult))
            chain(v.tensor_reduce(cols[:, q:q + 1], lvp[:, :], AX, ALU.add))
        v.sem_inc(lam_sum, 1)
        v.wait_ge(lam_exp, 1)
        chain(v.tensor_tensor(cols[:, 4:5], cols[:, 2:3], cols[:, 3:4], ALU.subtract))
        chain(v.tensor_scalar(cols[:, 5:6], cols[:, 4:5], LAM_INIT, None, ALU.add))
        chain(v.tensor_scalar(cols[:, 6:7], v1("subln"), 1.0 - LAM_INIT, None, ALU.mult))
        v.tensor_tensor(WST[:, :].rearrange("p (g t) -> p g t", g=4), WST[:, :].rearrange("p (g t) -> p g t", g=4),
                        TRI[:, :].unsqueeze(1).to_broadcast([P, 4, P]), ALU.mult).then_inc(wst_ready, 1)

        v.wait_ge(xb_ready, 2)
        chain(v.memset(PA[:, 0:2 * PADX], 0.0))
        chain(v.memset(PB[:, :], 0.0))

        def double(dst, src, step, parts, j):
            a = j * PADX + 16
            chain(v.tensor_tensor(dst[parts, a:a + T], src[parts, a:a + T], src[parts, a - step:a - step + T], ALU.add))

        every = slice(0, P)
        for j in range(2):
            double(PA, XB, 1, every, j)
            double(PB, PA, 2, every, j)
        double(PA, PB, 4, every, 1)
        double(PB, PA, 8, slice(64, P), 1)
        sums = {0: PA, 1: PB, 2: PA, 3: PB}
        for g in range(4):
            j, parts = g // 2, slice(64 * (g % 2), 64 * (g % 2) + 64)
            a = j * PADX + 16
            s = sums[g]
            chain(v.tensor_tensor(s[parts, a:a + 16], s[parts, a:a + 16], EDGE[parts, j * 16:(j + 1) * 16], ALU.mult))
            x = XB[parts, a:a + T]
            chain(v.scalar_tensor_tensor(out=x[:, 16:T], in0=s[parts, a + 16:a + T],
                                         scalar=vec[parts, VEC["pool_inv"] + j:VEC["pool_inv"] + j + 1],
                                         in1=x[:, 16:T], op0=ALU.mult, op1=ALU.subtract))
            chain(v.tensor_tensor(x[:, 0:16], s[parts, a:a + 16], x[:, 0:16], ALU.subtract))
            if g % 2:
                v.sem_inc(p_ready, 1)
        v.wait_ge(va_ready, 2)
        for i in range(QT_N):
            chain(v.bn_stats(bn[:, 0:6], VA[:, i * 256:(i + 1) * 256]))
            chain(v.bn_aggr(cols[:, 32 + 2 * i:34 + 2 * i], bn[:, 0:6]))
        chain(v.tensor_scalar(stat[:, 0:QT_N], cols[:, 32:48].rearrange("p (i c) -> p i c", c=2)[:, :, 1], 1e-5, None,
                              ALU.add))
        v.sem_inc(va_ms, 1)
        for j in range(2):
            v.wait_ge(done[2 + j], before("pool", 2 + j) + 1)
            his[0] += 1
            v.wait_ge(hi, his[0])
            v.scalar_tensor_tensor(out=YB[:, 2 * T + j * T:2 * T + (j + 1) * T], in0=pair(2 + j),
                                   scalar=v1("pool_scale", j), in1=YB[:, j * T:(j + 1) * T].bitcast(F32),
                                   op0=ALU.mult, op1=ALU.subtract).then_inc(lo, 1)
            v.wait_ge(lo, his[0])
            v.sem_inc(free[2 + j], 1)
        v.wait_ge(va_sd, 1)
        chain(v.reciprocal(stat[:, 0:QT_N], stat[:, 0:QT_N]))
        for i in range(QT_N):
            row = VA[:, i * 256:(i + 1) * 256]
            chain(v.tensor_scalar(row, row, cols[:, 32 + 2 * i:33 + 2 * i], stat[:, i:i + 1], ALU.subtract, ALU.mult))
            chain(v.tensor_tensor(row, row, lngb[:, 0:256], ALU.mult))
            v.tensor_tensor(row, row, lngb[:, 256:512], ALU.add).then_inc(va_norm, 1)
        v.wait_ge(u_ready, 2)
        for j in range(2):
            v.wait_ge(done[2 + j], before("gmlp", 2 + j) + 1)
            chain(v.tensor_tensor(TMP[j].rearrange("p (i t) -> p i t", i=QT_N),
                                  pair(2 + j).rearrange("p (i t) -> p i t", i=QT_N),
                                  SGB[:, j * P:(j + 1) * P].unsqueeze(1).to_broadcast([P, QT_N, P]), ALU.add))
            v.sem_inc(free[2 + j], 1)
            v.tensor_tensor(TMP[j], TMP[j], U[:, j * T:(j + 1) * T], ALU.mult).then_inc(xt, 1)
            xts[0] += 1
            v.wait_ge(xt, xts[0])
            his[0] += 1
            v.wait_ge(hi, his[0])
            v.tensor_tensor(YA[:, 2 * T + j * T:2 * T + (j + 1) * T], TMP[j],
                            YA[:, j * T:(j + 1) * T].bitcast(F32), ALU.subtract).then_inc(lo, 1)
            v.wait_ge(lo, his[0])

        def biased(h, t):
            n = (t + 1) * P
            o = 2 * (t % 2)
            for c, S in enumerate((SA[t % 2], SB[t % 2])):
                v.wait_ge(done[2 + c], h * 9 + (before("diff", 2 + c) + t + 1))
                v.sem_inc(sc_seen, 1)
                chain(v.tensor_tensor_reduce(out=S[:, 0:n], in0=PS[:, (2 + c) * 1024:(2 + c) * 1024 + n],
                                             in1=BR[:, T - n:T], scale=1.0, scalar=-3.0e38, op0=ALU.add,
                                             op1=ALU.max, accum_out=cols[:, 54 + c:55 + c]))
                v.sem_inc(free[2 + c], 1)
            v.tensor_scalar(cols[:, 8 + o:10 + o], cols[:, 54:56], -1.0, None, ALU.mult).then_inc(neg_ready, 1)
            v.wait_ge(neg_ready, h * 8 + (t + 1))

        def combine(h, t):
            n = (t + 1) * P
            o = 2 * (t % 2)
            S0, S1 = SA[t % 2], SB[t % 2]
            v.wait_ge(exp_ready, h * 16 + (2 * t + 2))
            chain(v.reciprocal(cols[:, 14:16], cols[:, 50 + o:52 + o]))
            chain(v.tensor_tensor(cols[:, 20:21], cols[:, 15:16], cols[:, 5:6], ALU.mult))
            chain(v.tensor_scalar(S1[:, 0:n], S1[:, 0:n], cols[:, 20:21], None, ALU.mult))
            chain(v.scalar_tensor_tensor(out=S0[:, 0:n], in0=S0[:, 0:n], scalar=cols[:, 14:15],
                                         in1=S1[:, 0:n], op0=ALU.mult, op1=ALU.subtract))
            v.sem_inc(aa_ready, 1)

        def diff_head(h):
            v.wait_ge(br_in, h * 16 + 16)
            biased(h, 0)
            biased(h, 1)
            combine(h, 0)
            for t in range(QT_N):
                if t + 1 < QT_N:
                    combine(h, t + 1)
                if t + 2 < QT_N:
                    v.wait_ge(done[0], h * 10 + (before("diff", 0) + 3 + t))
                    biased(h, t + 2)
                v.wait_ge(done[1], h * 10 + (before("diff", 1) + 3 + t))
                chain(v.tensor_copy(OC[:, t * P:(t + 1) * P], PS[:, 1024:1024 + P]))
                v.sem_inc(free[1], 1)
                v.sem_inc(oc_ready, 1)
            norm_scale(h + before("diff", "norm"), h * 9 + (before("diff", 2) + 8), h * 9 + (before("diff", 3) + 8),
                       T, P, 1e-5)
            v.scalar_tensor_tensor(out=TMP0, in0=OC, scalar=cols[:, 6:7], in1=PS[:, 3072:4096],
                                   op0=ALU.mult, op1=ALU.mult).then_inc(xt, 1)
            v.wait_ge(xt, h + (xts[0] + 1))
            v.sem_inc(free[3], 1)
            v.wait_ge(hi, h + (his[0] + 1))
            v.tensor_tensor(OCS[:, bass.ds(h * T + 4 * T, T)], TMP0,
                            OCS[:, bass.ds(h * T, T)].bitcast(F32), ALU.subtract).then_inc(lo, 1)
            v.wait_ge(lo, h + (his[0] + 1))

        with v.Fori(0, HEADS_C // 2 - 1) as i:
            chain.enter(i, 2 * (8 * 7 + 1))
            for hh in range(2):
                diff_head(i * 2 + hh)
            chain.leave(HEADS_C // 2 - 1)
        diff_head(HEADS_C - 2)
        diff_head(HEADS_C - 1)
        xts[0] += 4
        his[0] += 4

        def ada(i, tiles):
            for k in tiles:
                group, tile = k // 6, k % 6
                v.wait_ge(ada_in[k % 2], i * 96 + 16 * (k // 2) + 16)
                v.sem_inc(ada_seen, 1)
                for n, row in enumerate((CL, CC) if tile < 2 else (CL,)):
                    col = 2 * tile + n if tile < 2 else tile + 2
                    w = AW[:, (k % 2) * D:(k % 2 + 1) * D]
                    chain(v.tensor_tensor_reduce(out=SC[:, 3 * TS:3 * TS + D], in0=w, in1=row[:, :], scale=1.0,
                                                 scalar=0.0, op0=ALU.mult, op1=ALU.add,
                                                 accum_out=adac[:, col:col + 1]))
                v.sem_inc(ada_used, 1)
                if tile == 5:
                    both = adac[:, 0:4].rearrange("p (t c) -> p t c", c=2)
                    chain(v.tensor_copy(modb[:, bass.ds(i * 4 + 2 * group, 2)], both[:, :, 0]))
                    chain(v.tensor_copy(modb[:, bass.ds(i * 4 + 2 * group + 16, 2)], both[:, :, 1]))
                    chain(v.tensor_copy(modl[:, bass.ds(i * 8 + 4 * group, 4)], adac[:, 4:8]))

        v.sem_inc(ada_used, 2)
        v.wait_ge(c_silu, 2)

        def merge(i, parts=range(3)):
            m = M[:, bass.ds(i * T, T)]
            t = SC[:, 3 * TS:3 * TS + T]
            for j in parts:
                p = (3, 0, 1)[j]
                v.wait_ge(sg_ready, i * 3 + j + 1)
                v.wait_ge(done[p], i * (1 if p == 3 else 2) + before("merge", p) + (1 if p == 3 else 2))
                sg = SC[:, j * TS:j * TS + T]
                chain(v.tensor_tensor(t if j else m, sg, pair(p), ALU.mult))
                v.sem_inc(free[p], 1)
                if j == 0:
                    v.sem_inc(m_ready, 1)
                else:
                    v.tensor_tensor(m, m, t, ALU.add).then_inc(m_ready, 1)
                    v.wait_ge(m_ready, i * 3 + j + 4)

        def lo_chunks(src, a, b):
            def one(i):
                v.wait_ge(hi, i + (his[0] - a + 1))
                v.tensor_tensor(H[:, bass.ds(i * T + KC * T, T)], src[:, bass.ds(i * T, T)],
                                H[:, bass.ds(i * T, T)].bitcast(F32), ALU.subtract).then_inc(lo, 1)

            if b - a == 1:
                one(a)
            else:
                with v.Fori(a, b) as i:
                    one(i)
            his[0] += b - a
            v.wait_ge(lo, his[0])

        with v.Fori(0, ADA_TURNS) as i:
            chain.enter(i, 3 + 16 + 6)
            ada(i, range(0, 8))
            merge(i)
            ada(i, range(8, 12))
            chain.leave(ADA_TURNS)
        with v.Fori(ADA_TURNS, KC - 1) as i:
            chain.enter(i - ADA_TURNS, 3)
            merge(i)
            chain.leave(KC - 1 - ADA_TURNS)
        lo_chunks(M, 0, 3)
        merge(KC - 1, (0,))
        lo_chunks(M, 3, 6)
        merge(KC - 1, (1,))
        lo_chunks(M, 6, 7)
        merge(KC - 1, (2,))
        lo_chunks(M, 7, 8)

        v.wait_ge(c_x, 16 * KC)

        def residual(phase, p0, gain=None, other=None, squares=((ACC, SQ),)):
            for total, _ in squares:
                chain(v.memset(total, 0.0))
            k = len(squares)

            def turn(i, s, half=0, size=T):
                o = s * T + half * HALF
                x = X[:, bass.ds(i * (2 * T) + o, size)]
                old = other[:, bass.ds(i * (2 * T) + o, size)] if other is not None else x
                new = pair(p0 + s, size, half * HALF)
                v.wait_ge(done[p0 + s], i + before(phase, p0 + s) + half + 1)
                if gain is None:
                    ins = v.tensor_tensor(x, new, old, ALU.add)
                else:
                    ins = v.scalar_tensor_tensor(out=x, in0=new, scalar=gain[:, bass.ds(i * 2 + s, 1)],
                                                 in1=old, op0=ALU.mult, op1=ALU.add)
                ins.then_inc(x_new, 1)
                v.wait_ge(x_new, i * 2 + before(phase, "xnew") + s + half + 1)
                v.sem_inc(free[p0 + s], 1)
                for n, (total, sq) in enumerate(squares):
                    part = slice(half * HALF, half * HALF + size)
                    count = (s + half) * k + n + 1
                    v.wait_ge(sq_ready, i * (2 * k) + sqs[0] + count)
                    v.tensor_tensor(total[:, part], total[:, part], sq[:, part], ALU.add).then_inc(sq_added, 1)
                    v.wait_ge(sq_added, i * (2 * k) + acs[0] + count)

            turns = KC // 2 - (k > 0)
            with v.Fori(0, turns) as i:
                for s in range(2):
                    turn(i, s)
            if squares:
                turn(turns, 0)
                for half in range(2):
                    turn(turns, 1, half, HALF)
                sqs[0] += (KC + 1) * k
                acs[0] += (KC + 1) * k
                v.sem_inc(acc_ready, 1)

        residual("out1", 0, other=XIN)
        phase_scale("norm2", D, 1e-6)
        apply_split(H, KC * T, X, KC, T, lambda c: v1("ffn_g", c))

        chain(v.memset(SC[:, 0:2], 0.0))
        f0 = 0
        for n, chunks in enumerate(FF_PASSES):
            up = f"up{n}"
            with v.Fori(0, chunks) as i:
                chain.enter(i, 2)
                conv = SC[:, TS:TS + T]

                def tap(k):
                    return vec[:, bass.ds(i + (VEC[f"conv{k}"] + f0), 1)]

                v.wait_ge(gp_ready, i + f0 + 1)
                chain(v.tensor_scalar(conv, SC[:, 0:T], tap(0), None, ALU.mult))
                chain(v.scalar_tensor_tensor(out=conv, in0=SC[:, 1:1 + T], scalar=tap(1), in1=conv,
                                             op0=ALU.mult, op1=ALU.add))
                v.scalar_tensor_tensor(out=conv, in0=SC[:, 2:2 + T], scalar=tap(2), in1=conv,
                                       op0=ALU.mult, op1=ALU.add).then_inc(cv_ready, 1)
                v.wait_ge(cv_ready, i + f0 + 2)
                v.wait_ge(gl_ready, i + f0 + 1)
                v.wait_ge(done[1], i + before(up, 1) + 1)
                v.tensor_tensor(SC[:, 3 * TS:3 * TS + T], SC[:, 2 * TS:2 * TS + T], pair(1), ALU.mult).then_inc(xt, 1)
                v.wait_ge(xt, i + xts[0] + 1)
                v.sem_inc(free[1], 1)
                v.wait_ge(hi, i + his[0] + 1)
                v.tensor_tensor(FF[:, bass.ds(i * T + KC * T, T)], SC[:, 3 * TS:3 * TS + T],
                                FF[:, bass.ds(i * T, T)].bitcast(F32), ALU.subtract).then_inc(lo, 1)
                v.wait_ge(lo, i + his[0] + 1)
                chain.leave(chunks)
            xts[0] += chunks
            his[0] += chunks
            f0 += chunks
            if n < len(FF_PASSES) - 1:
                residual(f"down{n}", 2, squares=())
            if n == 0:
                for q in range(2):
                    chain(v.tensor_tensor(modb[:, 16 * q:16 * q + 16], modb[:, 16 * q:16 * q + 16],
                                          vec[:, VEC["b_both"]:VEC["b_both"] + 16], ALU.add))
                chain(v.tensor_tensor(modl[:, :], modl[:, :], vec[:, VEC["b_lat"]:VEC["b_lat"] + 32], ALU.add))
                for fac, scale, g in ((fac0, modb[:, 8:16], "norm_g0"), (facc, modb[:, 24:32], "norm_g0"),
                                      (fac1, modl[:, 16:24], "norm_g1")):
                    chain(v.tensor_scalar(fac[:, :], scale, 1.0, None, ALU.add))
                    chain(v.tensor_tensor(fac[:, :], fac[:, :], vec[:, VEC[g]:VEC[g] + 8], ALU.mult))
                chain(v.tensor_tensor(fac0[:, :], fac0[:, :], vec[:, VEC["final_g"]:VEC["final_g"] + 8], ALU.mult))

        v.wait_ge(cxs_ready, 1)
        chain(v.tensor_reduce(ACCX[:, :], CXS[:, :].rearrange("p (c n) -> p n c", c=KC), AX, ALU.add))
        residual("down2", 2, squares=((ACC, SQ), (ACC2, TMP0)))

        v.wait_ge(done[2], before("norm3", 2) + 1)
        a, k = T // P, TK // P
        chain(v.tensor_scalar(stat[:, 0:k], PS[:, 2048:2048 + k], 1.0 / D, 1e-6, ALU.mult, ALU.add))
        chain(v.tensor_scalar(stat[:, k:k + a], PS[:, 2048 + k:2048 + k + a], 1.0 / D, None, ALU.mult))
        v.sem_inc(free[2], 1)
        v.scalar_tensor_tensor(out=stat[:, k:k + a], in0=stat[:, 0:a], scalar=1e-6, in1=stat[:, k:k + a],
                               op0=ALU.mult, op1=ALU.add).then_inc(ms_ready, 1)
        v.wait_ge(sd_ready, before("norm3", "norm") + 1)
        chain(v.reciprocal(fstat[:, :], fstat[:, :]))
        chain(diagonal(DIAGC[:, :], fstat, a, k))
        for o in (0, 4):
            diagonal(DIAG[:, o * P:(o + 4) * P], fstat, k + o, k + o + 4).then_inc(diag_ready, 1)
        v.wait_ge(done[3], before("norm3", 3) + 1)
        v.wait_ge(done[2], before("norm3", 2) + 2)
        apply_split(H, KC * T, X, KC, T, lambda c: fac0[:, c:c + 1], lambda c: modb[:, c:c + 1])
        apply_split(UC, KC * CTX, CXR, KC, CTX, lambda c: facc[:, c:c + 1], lambda c: modb[:, 16 + c:17 + c],
                    scales=2)
        add_squares(2)
        scale_diagonal("cqnorm", 256, T)
        v.wait_ge(cs_in, 16)
        v.wait_ge(done[0], before("kvpe", 0) + 2)
        v.tensor_tensor(TPE[:, CTX:TK], pair(0), CST[:, CTX:TK], ALU.mult).then_inc(tpe_ready, 1)
        v.wait_ge(tpe_ready, 1)
        v.sem_inc(free[0], 1)
        v.wait_ge(done[1], before("kvpe", 1) + 2)
        v.tensor_tensor(TPE[:, 0:CTX], pair(1, CTX), CST[:, 0:CTX], ALU.mult).then_inc(tpe_ready, 1)
        v.wait_ge(tpe_ready, 2)
        v.sem_inc(free[1], 1)
        v.wait_ge(done[3], before("cqnorm", 3) + 1)
        apply_split(CQ, 2 * T, CQR, 2, T, lambda c: v1("g_qa", c))
        scale_diagonal("ckvnorm", P, TK)
        v.wait_ge(done[3], before("ckvnorm", 3) + 1)
        v.wait_ge(done[2], before("ckvnorm", 2) + 2)
        for n, (a, m) in enumerate(((0, T), (T, CTX))):
            v.scalar_tensor_tensor(out=TMP[n][:, 0:m], in0=CKR[:, a:a + m], scalar=v1("g_kva"),
                                   in1=pair(3 - n, m), op0=ALU.mult, op1=ALU.mult).then_inc(xt, 1)
        for n, (a, m) in enumerate(((0, T), (T, CTX))):
            xts[0] += 1
            his[0] += 1
            v.wait_ge(xt, xts[0])
            v.sem_inc(free[3 - n], 1)
            v.wait_ge(hi, his[0])
            v.tensor_tensor(CKV[:, TK + a:TK + a + m], TMP[n][:, 0:m], CKV[:, a:a + m].bitcast(F32),
                            ALU.subtract).then_inc(lo, 1)
        diagonal(DIAG, fstat, 0, T // P).then_inc(xdiag_ready, 1)
        v.wait_ge(done[3], before("xscale", 3) + 1)
        for c in range(KC):
            x = X[:, c * T:(c + 1) * T]
            ins = v.scalar_tensor_tensor(out=x, in0=x, scalar=v1("final_g", c), in1=pair(3),
                                         op0=ALU.mult, op1=ALU.mult)
        chain(ins)
        v.sem_inc(free[3], 1)

        v.wait_ge(kpe_hi, 1)
        v.tensor_tensor(KPE[:, TK:2 * TK], KPR[:, :], KPE[:, 0:TK].bitcast(F32), ALU.subtract).then_inc(kpe_lo, 1)
        v.wait_ge(csq_in, 16)

        def lo_part(dst, half, src_at, n, count, at_=0):
            v.wait_ge(hq_hi, count)
            v.tensor_tensor(dst[:, half + at_:half + at_ + n], PS[:, src_at:src_at + n],
                            dst[:, at_:at_ + n].bitcast(F32), ALU.subtract).then_inc(hq_lo, 1)

        def rotate(h):
            v.wait_ge(hp_done, h * 5 + 4)
            v.tensor_tensor(TMP0, PS[:, 0:T], CSQ, ALU.mult).then_inc(qp_ready, 1)

        def head_end(h, hh):
            v.wait_ge(hq_hi, h * 4 + 4)
            v.wait_ge(qp_ready, h + 1)
            v.tensor_tensor(QP[:, T:2 * T], TMP0, QP[:, 0:T].bitcast(F32), ALU.subtract).then_inc(hq_lo, 1)
            v.wait_ge(hp_done, h * 5 + 5)
            v.tensor_copy(VN[:, hh * TK + 512:hh * TK + 1024], PS[:, 2048:2560]).then_inc(vn_dve, 1)
            peak(h, 0)
            normalise(h, 0)
            peak(h, 1)

        def peak(h, t):
            base = 1536 * (t % 2)
            v.wait_ge(sc_done, h * 8 + t + 1)
            chain(v.tensor_reduce(cols[:, 22 + t % 2:23 + t % 2], PS[:, base:base + TK], AX, ALU.max))
            v.tensor_scalar(cols[:, 16 + t % 2:17 + t % 2], cols[:, 22 + t % 2:23 + t % 2], -MLA_SCALE, None,
                            ALU.mult).then_inc(mx_ready, 1)

        def normalise(h, t):
            v.wait_ge(ex_ready, h * 8 + t + 1)
            chain(v.reciprocal(cols[:, 24 + t % 2:25 + t % 2], cols[:, 18 + t % 2:19 + t % 2]))
            e = E[:, (t % 2) * TK:(t % 2) * TK + TK]
            v.tensor_scalar(e, e, cols[:, 24 + t % 2:25 + t % 2], None, ALU.mult).then_inc(e_ready, 1)

        def mla_head(h, hh, last=False):
            for t in range(QT_N):
                tg = h * 8 + t
                v.wait_ge(tpb_done, tg + 1)
                v.tensor_copy(PT[:, 512:1024], PS[:, 3584:4096]).then_inc(ptb, 1)
                if t + 1 < QT_N:
                    normalise(h, t + 1)
                if t + 2 < QT_N:
                    peak(h, t + 2)
                if t == QT_N - 2 and not last:
                    lo_part(QN, T, 0, T, h * 4 + 5)
                    lo_part(KN, TK, 1024, CTX, h * 4 + 6, T)
                if t == QT_N - 1 and not last:
                    lo_part(KN, TK, 1536, T, h * 4 + 7)
                    rotate(h + 1)
                v.wait_ge(pv_done, tg + 1)
                g = G[:, bass.ds(h * T + t * P, P)]
                v.tensor_tensor(g, PS[:, 3584:3584 + P], g, ALU.mult).then_inc(pv_free, 1)
            if not last:
                head_end(h + 1, 1 - hh)

        lo_part(QN, T, 0, T, 1)
        lo_part(KN, TK, 1024, CTX, 2, T)
        lo_part(KN, TK, 1536, T, 3)
        rotate(0)
        head_end(0, 0)
        with v.Fori(0, HEADS // 2 - 1) as i:
            chain.enter(i, 2 * 8 * 2)
            for hh in range(2):
                mla_head(i * 2 + hh, hh)
            chain.leave(HEADS // 2 - 1)
        mla_head(HEADS - 2, 0)
        mla_head(HEADS - 1, 1, last=True)
        v.wait_ge(pv_free, 65)
        lo_chunks(G, 0, KC)
        residual("out2", 0, gain=modl[:, 0:8])
        phase_scale("norm4", D, 1e-6)
        apply_split(H, KC * T, X, KC, T, lambda c: fac1[:, c:c + 1], lambda c: modl[:, 8 + c:9 + c])

        def fourier(i, last=False):
            v.wait_ge(zr_ready, i + 1)
            chain(v.tensor_copy(ZEO[:, 0:1], ZR[:, 0:1]))
            chain(v.memset(ZEO[:, HALF:HALF + 1], 0.0))
            back = ZR[:, T - 1:HALF:-1]
            v.tensor_tensor(ZEO[:, 1:HALF], ZR[:, 1:HALF], back, ALU.add).then_inc(ze_ready, 1)
            v.tensor_tensor(ZEO[:, HALF + 1:2 * HALF], ZR[:, 1:HALF], back, ALU.subtract).then_inc(ze_ready, 1)
            v.wait_ge(done[2], i * 2 + before("four", 2) + 1)
            v.tensor_copy(M12[:, HALF:2 * HALF], PS[:, 2560:3072]).then_inc(m_evac, 1)
            v.wait_ge(m_evac, i * 2 + 2)
            v.sem_inc(free[2], 1)
            if last:
                lo_chunks(Y, 0, KC - 1)
            v.wait_ge(qs_ready, i + 1)
            y = Y[:, bass.ds(i * T, HALF)]
            chain(v.tensor_tensor(y, PS[:, 3072:3584], TMP0[:, 0:HALF], ALU.subtract))
            y = Y[:, bass.ds(i * T + HALF + 1, HALF - 1)]
            v.tensor_tensor(y, PS[:, 3583:3072:-1], TMP0[:, HALF - 1:0:-1], ALU.add).then_inc(y_ready, 1)
            v.wait_ge(y_ready, i * 2 + 2)
            v.sem_inc(free[3], 1)
            v.wait_ge(done[2], i * 2 + before("four", 2) + 2)
            chain(v.tensor_copy(Y[:, bass.ds(i * T + HALF, 1)], PS[:, 2048:2049]))
            v.sem_inc(free[2], 1)
            v.wait_ge(sgf_ready, i + 1)
            y = Y[:, bass.ds(i * T, T)]
            v.tensor_tensor(y, y, TMP1, ALU.mult).then_inc(y_ready, 1)
            v.wait_ge(y_ready, i * 2 + 3)

        with v.Fori(0, FG - 1) as i:
            chain.enter(i, 4)
            fourier(i)
            chain.leave(FG - 1)
        fourier(FG - 1, last=True)
        lo_chunks(Y, KC - 1, KC)
        residual("out3", 0, gain=modl[:, 24:32])
        phase_scale("final", D, 1e-6)
        for c in range(KC):
            x = X[:, c * T:(c + 1) * T]
            v.scalar_tensor_tensor(out=x, in0=x, scalar=v1("final_g2", c), in1=PS[:, 3072:4096],
                                   op0=ALU.mult, op1=ALU.mult).then_inc(o_ready, 1)

    block_cm.__exit__(None, None, None)


def chunk_cols(w):
    k, n = w.shape
    return w.reshape(k // P, P, n // P, P).transpose(2, 1, 0, 3).reshape(n // P, P, k)


def pad_unit(u):
    return np.concatenate([u, np.zeros((P, UW - u.shape[1]), u.dtype)], axis=1)


def swap_rope(w):
    r1, r2, c1, c2 = np.split(w, 4, axis=1)
    return np.concatenate([w, r2, r1, c2, c1], axis=1)


def weight_units(a):
    units = []
    w_in = a["w_in"][0]
    cu, cv, cx = chunk_cols(w_in[:, 0:256]), chunk_cols(w_in[:, 256:512]), chunk_cols(w_in[:, 512:768])
    units += [cx[0], cx[1], cv[0], cv[1], cu[0], cu[1]]
    q, k, v = (chunk_cols(w_in[:, o:o + 512]) for o in (768, 1280, 1792))
    for h in range(HEADS_C):
        units += [q[h], k[h], v[h]]
    gate = chunk_cols(a["w_gate"][0])
    pa, pb, pc = (chunk_cols(a[n][0]) for n in ("proj_a", "proj_b", "proj_c"))
    for n in range(KC):
        units += [gate[n], gate[8 + n], gate[16 + n], np.concatenate([pa[n], pb[n], pc[n]], axis=1)]
    units += list(chunk_cols(a["w_out"][0]))
    up = chunk_cols(a["w_up"][0])
    down = chunk_cols(a["w_down"][0])
    f = 0
    for chunks in FF_PASSES:
        for j in range(f, f + chunks):
            units += [up[j], up[FFC + j]]
        units += [pad_unit(down[n][:, f * P:(f + chunks) * P]) for n in range(KC)]
        f += chunks
    m = a["mla_w_in_2"][0]
    units += list(chunk_cols(m[:, 0:256]))
    units += [chunk_cols(m[:, 256:384])[0], chunk_cols(swap_rope(m[:, 384:448]))[0]]
    units += list(chunk_cols(m[:, 448:]))
    wq, wkv = a["mla_w_qup_2"][0], a["mla_w_kvup_2"][0]
    for h in range(HEADS):
        qh = wq[:, h * 192:(h + 1) * 192]
        kv = chunk_cols(wkv[:, h * 256:(h + 1) * 256])
        units.append(pad_unit(np.concatenate(
            [chunk_cols(qh[:, 0:128])[0], chunk_cols(swap_rope(qh[:, 128:192]))[0], kv[0], kv[1]], axis=1)))
    units += list(chunk_cols(a["mla_w_out_2"][0]))
    fno = chunk_cols(a["fno_w_in_2"][0])
    for g in range(FG):
        units += [fno[g], fno[FG + g]]
    units += list(chunk_cols(a["fno_w_out_2"][0]))
    return np.ascontiguousarray(np.stack(units))


def feature_cols(x):
    return x.reshape(-1, P).T


def bucket_rows():
    n = np.arange(GROW)
    rel = (T - 1) - n
    pos = np.maximum(rel, 0)
    f = np.maximum(pos, 1).astype(np.float32)
    large = 16 + (np.log(f / np.float32(16)) / np.float32(math.log(8.0)) * np.float32(16)).astype(np.int32)
    bucket = np.where(pos < 16, pos, np.minimum(large, 31))
    rows = np.zeros((33, GROW), np.float32)
    rows[bucket, n] = 1.0
    rows[32] = np.where(rel < 0, np.float32(-1e30), 0.0)
    return rows


def rope_table():
    inv = (1.0 / (10000.0 ** (np.arange(0, 32, 2, dtype=np.float32) / np.float32(32)))).astype(np.float32)
    t = np.arange(T)
    row, col = (t // 64).astype(np.float32), (t % 64).astype(np.float32)
    ar, ac = inv[:, None] * row[None], inv[:, None] * col[None]
    cos = np.concatenate([np.cos(ar), np.cos(ar), np.cos(ac), np.cos(ac)])
    sin = np.concatenate([-np.sin(ar), np.sin(ar), -np.sin(ac), np.sin(ac)])
    lat = np.concatenate([cos, sin]).astype(np.float32)
    ctx = np.concatenate([np.ones((64, CTX)), np.zeros((64, CTX))]).astype(np.float32)
    return np.concatenate([ctx, lat], axis=1)


def dft_tables():
    t = np.arange(HALF)
    ang = 2 * np.pi * ((t[:, None] * t[None]) % T) / T
    tab = [f(ang).astype(np.float32).reshape(4, P, HALF).transpose(1, 0, 2).reshape(P, 4 * HALF)
           for f in (np.cos, np.sin)]
    d = np.arange(P)
    ang = 2 * np.pi * ((d[:, None] * d[None]) % P) / P
    norm = 1.0 / math.sqrt(T * P)
    csd = np.concatenate([np.cos(ang) * norm, np.sin(ang) * norm], axis=1).astype(np.float32)
    return tab[0], tab[1], csd


def arrays_of(a):
    c = np.ascontiguousarray
    vecs = {
        "attn_g": feature_cols(a["attn_norm_g"]), "b_gate": feature_cols(a["b_gate"]),
        "pool_scale": feature_cols(a["pool_scale"]), "subln": feature_cols(a["diff_subln_g"]),
        "ffn_g": feature_cols(a["ffn_norm_g"]), "conv0": feature_cols(a["conv_w"][0, 0]),
        "conv1": feature_cols(a["conv_w"][0, 1]), "conv2": feature_cols(a["conv_w"][0, 2]),
        "conv_b": feature_cols(a["conv_b"]), "final_g": feature_cols(a["final_norm_g"]),
        "norm_g0": feature_cols(a["norm_g_2"][0]), "norm_g1": feature_cols(a["norm_g_2"][1]),
        "b_both": feature_cols(a["b_ada_2"][0][:2048]),
        "b_lat": feature_cols(np.concatenate([a["b_ada_2"][0][2048:], a["b_ada_2"][1]])),
        "g_qa": feature_cols(a["mla_g_qa_2"]), "g_kva": feature_cols(a["mla_g_kva_2"]),
        "final_g2": feature_cols(a["final_g_2"]),
        "alt": np.where(np.arange(P) % 2, -1.0, 1.0).astype(np.float32)[:, None],
        "pool_inv": np.stack([np.repeat([1 / 2, 1 / 4], 64), np.repeat([1 / 8, 1 / 16], 64)], 1).astype(np.float32),
    }
    edge = np.zeros((P, 32), np.float32)
    t = np.arange(16)
    for g, win in enumerate((2, 4, 8, 16)):
        edge[64 * (g % 2):64 * (g % 2) + 64, 16 * (g // 2):16 * (g // 2) + 16] = 1.0 / np.minimum(t + 1, win)
    ada0 = chunk_rows(a["w_ada_2"][0])
    ada1 = chunk_rows(a["w_ada_2"][1])
    both, lat = ada0[:16], np.concatenate([ada0[16:], ada1])
    ada = np.stack([np.concatenate([both[2 * n:2 * n + 2], lat[4 * n:4 * n + 4]]) for n in range(8)])
    ada = ada.reshape(48, P, D)
    ctab, stab, csd = dft_tables()
    half = np.eye(64, dtype=np.float32)
    return {
        "x": c(a["x"][0].T.reshape(KC, P, T)),
        "ctx": c(a["ctx_2"][0].T.reshape(KC, P, CTX).transpose(1, 0, 2).reshape(P, KC * CTX)),
        "units": weight_units(a),
        "vec": c(np.concatenate([vecs[n] for n, _ in VEC_PARTS], axis=1)),
        "onehot": bucket_rows(), "rel_bias": c(a["rel_bias"]),
        "ident": np.eye(P, dtype=np.float32),
        "dup": np.block([[half, half], [half, half]]),
        "ln_g": c(a["sgu_ln_g"][0]), "ln_b": c(a["sgu_ln_b"][0]),
        "wst": c(a["sgu_w"][0].transpose(2, 0, 1).reshape(P, 4 * P)),
        "tri": np.triu(np.ones((P, P), np.float32)),
        "sgu_b": c(a["sgu_b"][0]), "pool_w": c(a["pool_w"][0]), "edge": edge,
        "lam": c(a["diff_lam"][0].reshape(256)),
        "c": c(a["c_2"][0]), "c_ctx": c(a["c_ctx_2"]),
        "ada": c(ada),
        "cs": rope_table(), "ctab": ctab, "stab": stab, "csd": csd,
        "altrow": np.where(np.arange(HALF) % 2, -1.0, 1.0).astype(np.float32)[None],
    }


def chunk_rows(w):
    k, n = w.shape
    return w.T.reshape(n // P, P, k)


def kernel(**inputs):
    import concourse.bacc as bacc
    from concourse.bass_utils import run_bass_kernel_spmd as run

    nc = bacc.Bacc("TRN2", target_bir_lowering=False, num_devices=1)
    arrays = arrays_of({k: np.asarray(v) for k, v in inputs.items()})
    t_in = {k: nc.dram_tensor("in_" + k, v.shape, F32, kind="ExternalInput").ap() for k, v in arrays.items()}
    out = nc.dram_tensor("out", (KC, P, T), F32, kind="ExternalOutput").ap()
    build(nc, t_in, out)
    r = run(nc, [{"in_" + k: v for k, v in arrays.items()}], core_ids=[0])
    return r.results[0]["out"].reshape(D, T).T.reshape(1, T, D)
```
